# Optimizing a Trainium2 kernel written in Bass

```python
import math
import jax, jax.numpy as jnp
from jax import lax
import numpy as np

D_MODEL = 1024
BATCH = 1
SEQ = 512
DEPTH = 2
DEC_BATCH = 8
DEC_SEQ = 8
PAST_LEN = 2048
PAGE_SIZE = 128

N_MIXERS = 2
N_MLA_LAYERS = (DEPTH + 1) // 2
N_MLSTM_LAYERS = DEPTH // 2
MLA_HEADS = 16
MLA_NOPE = 64
MLA_ROPE = 32
MLA_V = 64
Q_RANK = 384
KV_RANK = 256
MLA_IN = Q_RANK + KV_RANK + MLA_ROPE
MLA_SCALE = (MLA_NOPE + MLA_ROPE) ** -0.5
ROPE_BASE = 10000.0
Q_BLOCK = 128
MLSTM_HEADS = 4
MLSTM_DK = 128
MLSTM_DV = 256
MLSTM_QK = MLSTM_HEADS * MLSTM_DK
MLSTM_HV = MLSTM_HEADS * MLSTM_DV
MLSTM_IN = 2 * MLSTM_QK + 2 * MLSTM_HV + 2 * MLSTM_HEADS
MLSTM_CHUNK = 64
GATE_CAP = 15.0
D_FF = 2816
PLE_DIM = 256
NORM_EPS = 1e-6

kernel_name = 'hybrid_mla_mlstm_macaron_step'

def rmsnorm(x, g):
    x32 = x.astype(jnp.float32)
    y = x32 * lax.rsqrt(jnp.mean(x32 * x32, axis=-1, keepdims=True) + NORM_EPS)
    return (y * g.astype(jnp.float32)).astype(x.dtype)

def swiglu(h, w_in, w_out):
    a, b = jnp.split(h @ w_in, 2, axis=-1)
    return (jax.nn.silu(a) * b) @ w_out

def rope(x, pos):
    half = x.shape[-1] // 2
    inv = ROPE_BASE ** (-jnp.arange(half, dtype=jnp.float32) / half)
    ang = pos.astype(jnp.float32)[:, None] * inv[None, :]
    cos = jnp.cos(ang)[:, None, :]
    sin = jnp.sin(ang)[:, None, :]
    x32 = x.astype(jnp.float32)
    x1, x2 = x32[..., :half], x32[..., half:]
    return jnp.concatenate([x1 * cos - x2 * sin, x1 * sin + x2 * cos], axis=-1).astype(x.dtype)

def mla_project(h, pos, w_in, g_q, g_kv, w_uq):
    z = h @ w_in
    cq = rmsnorm(z[..., :Q_RANK], g_q)
    ckv = rmsnorm(z[..., Q_RANK:Q_RANK + KV_RANK], g_kv)
    kr = rope(z[..., Q_RANK + KV_RANK:][:, :, None, :], pos)[:, :, 0, :]
    q = jnp.einsum('btr,rhd->bthd', cq, w_uq)
    q_nope = q[..., :MLA_NOPE]
    q_rope = rope(q[..., MLA_NOPE:], pos)
    return q_nope, q_rope, ckv, kr

def latent_attend(q_nope, q_rope, ckv, kr, q_pos, k_pos, w_uk):
    q_abs = jnp.einsum('...qhd,rhd->...qhr', q_nope, w_uk)
    s = jnp.einsum('...qhr,...kr->...hqk', q_abs, ckv) + jnp.einsum('...qhd,...kd->...hqk', q_rope, kr)
    s = s.astype(jnp.float32) * MLA_SCALE
    s = jnp.where(k_pos[None, :] <= q_pos[:, None], s, -jnp.inf)
    p = jax.nn.softmax(s, axis=-1).astype(ckv.dtype)
    return jnp.einsum('...hqk,...kr->...qhr', p, ckv)

def mla_attend_prompt(q_nope, q_rope, ckv, kr, w_uk):
    b, t = q_nope.shape[0], q_nope.shape[1]
    qb = math.gcd(Q_BLOCK, t)
    nb = t // qb
    pos = jnp.arange(t)

    def blocks(a):
        return jnp.moveaxis(a.reshape((b, nb, qb) + a.shape[2:]), 1, 0)

    def one(args):
        qn, qr, qp = args
        return latent_attend(qn, qr, ckv, kr, qp, pos, w_uk)

    o = lax.map(one, (blocks(q_nope), blocks(q_rope), pos.reshape(nb, qb)))
    return jnp.moveaxis(o, 0, 1).reshape(b, t, MLA_HEADS, KV_RANK)

def mla_attend_sample(q_nope, q_rope, ckv_new, kr_new, cache_ckv, cache_krope, layer, page_table, w_uk):
    past = page_table.shape[1] * cache_ckv.shape[2]
    t = q_nope.shape[1]
    q_pos = past + jnp.arange(t)
    k_pos = jnp.arange(past + t)

    def one(args):
        pt, qn, qr, cn, kn = args
        ck = cache_ckv[layer, pt].reshape(past, KV_RANK).astype(cn.dtype)
        kk = cache_krope[layer, pt].reshape(past, MLA_ROPE).astype(kn.dtype)
        ck = jnp.concatenate([ck, cn], axis=0)
        kk = jnp.concatenate([kk, kn], axis=0)
        return latent_attend(qn, qr, ck, kk, q_pos, k_pos, w_uk)

    return lax.map(one, (page_table, q_nope, q_rope, ckv_new, kr_new))

def mla_output(o_lat, w_uv, w_out):
    b, t = o_lat.shape[0], o_lat.shape[1]
    v = jnp.einsum('bthr,rhv->bthv', o_lat, w_uv).reshape(b, t, MLA_HEADS * MLA_V)
    return v @ w_out

def mlstm_chunkwise(q, k, v, ig, lf, C0, n0, m0):
    b, t = q.shape[0], q.shape[1]
    L = math.gcd(MLSTM_CHUNK, t)
    nc = t // L

    def chunks(a):
        a = jnp.swapaxes(a, 1, 2)
        a = a.reshape(a.shape[:2] + (nc, L) + a.shape[3:])
        return jnp.moveaxis(a, 2, 0)

    causal = jnp.tril(jnp.ones((L, L), dtype=bool))

    def step(carry, inp):
        C, n, m = carry
        qc, kc, vc, ic, fc = inp
        bcum = jnp.cumsum(fc, axis=-1)
        logD = ic[..., None, :] + bcum[..., :, None] - bcum[..., None, :]
        logD = jnp.where(causal, logD, -jnp.inf)
        m_t = jnp.maximum(bcum + m[..., None], jnp.max(logD, axis=-1))
        decay = jnp.exp(bcum + m[..., None] - m_t)
        S = jnp.einsum('bhtd,bhsd->bhts', qc, kc) * jnp.exp(logD - m_t[..., None])
        num = jnp.einsum('bhts,bhsv->bhtv', S, vc) + decay[..., None] * jnp.einsum('bhtd,bhdv->bhtv', qc, C)
        den = jnp.sum(S, axis=-1) + decay * jnp.einsum('bhtd,bhd->bht', qc, n)
        h = num / jnp.maximum(jnp.abs(den), jnp.exp(-m_t))[..., None]
        m_new = m_t[..., -1]
        w_s = jnp.exp(ic + bcum[..., -1:] - bcum - m_new[..., None])
        carry_decay = jnp.exp(bcum[..., -1] + m - m_new)
        C_new = carry_decay[..., None, None] * C + jnp.einsum('bhs,bhsd,bhsv->bhdv', w_s, kc, vc)
        n_new = carry_decay[..., None] * n + jnp.einsum('bhs,bhsd->bhd', w_s, kc)
        return (C_new, n_new, m_new), h

    (C, n, m), hs = lax.scan(step, (C0, n0, m0), (chunks(q), chunks(k), chunks(v), chunks(ig), chunks(lf)))
    hs = jnp.moveaxis(hs, 0, 2).reshape(b, MLSTM_HEADS, t, MLSTM_DV)
    return jnp.swapaxes(hs, 1, 2), (C, n, m)

def softcap(x):
    return GATE_CAP * jnp.tanh(x / GATE_CAP)

def mlstm_mixer(h, C0, n0, m0, w_in, b_i, b_f, g_head, w_out):
    b, t = h.shape[0], h.shape[1]
    z = h @ w_in
    cuts = [MLSTM_QK, 2 * MLSTM_QK, 2 * MLSTM_QK + MLSTM_HV, 2 * MLSTM_QK + 2 * MLSTM_HV,
            2 * MLSTM_QK + 2 * MLSTM_HV + MLSTM_HEADS]
    q, k, v, o, ig, fg = jnp.split(z.astype(jnp.float32), cuts, axis=-1)
    q = q.reshape(b, t, MLSTM_HEADS, MLSTM_DK) * (MLSTM_DK ** -0.5)
    k = k.reshape(b, t, MLSTM_HEADS, MLSTM_DK)
    v = v.reshape(b, t, MLSTM_HEADS, MLSTM_DV)
    ig = softcap(ig + b_i.astype(jnp.float32))
    lf = jax.nn.log_sigmoid(softcap(fg + b_f.astype(jnp.float32)))
    hh, state = mlstm_chunkwise(q, k, v, ig, lf, C0.astype(jnp.float32), n0.astype(jnp.float32),
                                m0.astype(jnp.float32))
    hh = hh * lax.rsqrt(jnp.mean(hh * hh, axis=-1, keepdims=True) + NORM_EPS)
    hh = hh.reshape(b, t, MLSTM_HV) * g_head.astype(jnp.float32)
    out = (jax.nn.sigmoid(o) * hh).astype(h.dtype)
    return out @ w_out, state

def setup_inputs(seed: int = 0) -> dict:
    key = jax.random.key(seed)
    keys = list(jax.random.split(key, 40))

    def nrm(shape, scale=1.0):
        return jax.random.normal(keys.pop(), shape, jnp.float32) * scale

    def gain(shape):
        return 1.0 + nrm(shape, 0.02)

    n_pages = PAST_LEN // PAGE_SIZE
    n_pool = (5 * DEC_BATCH * n_pages) // 4
    page_table = jax.random.permutation(keys.pop(), n_pool)[:DEC_BATCH * n_pages]
    page_table = page_table.reshape(DEC_BATCH, n_pages).astype(jnp.int32)
    nA, nB = N_MLA_LAYERS, N_MLSTM_LAYERS
    return {
        'x_prompt': nrm((BATCH, SEQ, D_MODEL)),
        'x_sample': nrm((DEC_BATCH, DEC_SEQ, D_MODEL)),
        'cache_ckv': nrm((nA, n_pool, PAGE_SIZE, KV_RANK)),
        'cache_krope': nrm((nA, n_pool, PAGE_SIZE, MLA_ROPE)),
        'state_C': nrm((nB, DEC_BATCH, MLSTM_HEADS, MLSTM_DK, MLSTM_DV), MLSTM_DK ** -0.5),
        'state_n': nrm((nB, DEC_BATCH, MLSTM_HEADS, MLSTM_DK)),
        'state_m': nrm((nB, DEC_BATCH, MLSTM_HEADS)),
        'page_table': page_table,
        'p_prompt': nrm((DEPTH, BATCH, SEQ, PLE_DIM)),
        'p_sample': nrm((DEPTH, DEC_BATCH, DEC_SEQ, PLE_DIM)),
        'g_ffa': gain((DEPTH, D_MODEL)),
        'w_ffa_in': nrm((DEPTH, D_MODEL, 2 * D_FF), D_MODEL ** -0.5),
        'w_ffa_out': nrm((DEPTH, D_FF, D_MODEL), D_FF ** -0.5),
        'g_mix': gain((DEPTH, D_MODEL)),
        'g_ffb': gain((DEPTH, D_MODEL)),
        'w_ffb_in': nrm((DEPTH, D_MODEL, 2 * D_FF), D_MODEL ** -0.5),
        'w_ffb_out': nrm((DEPTH, D_FF, D_MODEL), D_FF ** -0.5),
        'g_ple': gain((DEPTH, D_MODEL)),
        'w_ple_gate': nrm((DEPTH, D_MODEL, D_MODEL), D_MODEL ** -0.5),
        'w_ple_proj': nrm((DEPTH, PLE_DIM, D_MODEL), PLE_DIM ** -0.5),
        'w_mla_in': nrm((nA, D_MODEL, MLA_IN), D_MODEL ** -0.5),
        'g_q_lat': gain((nA, Q_RANK)),
        'g_kv_lat': gain((nA, KV_RANK)),
        'w_uq': nrm((nA, Q_RANK, MLA_HEADS, MLA_NOPE + MLA_ROPE), Q_RANK ** -0.5),
        'w_uk': nrm((nA, KV_RANK, MLA_HEADS, MLA_NOPE), KV_RANK ** -0.5),
        'w_uv': nrm((nA, KV_RANK, MLA_HEADS, MLA_V), KV_RANK ** -0.5),
        'w_mla_out': nrm((nA, MLA_HEADS * MLA_V, D_MODEL), (MLA_HEADS * MLA_V) ** -0.5),
        'w_mlstm_in': nrm((nB, D_MODEL, MLSTM_IN), D_MODEL ** -0.5),
        'b_igate': nrm((nB, MLSTM_HEADS), 0.1),
        'b_fgate': jnp.linspace(3.0, 6.0, MLSTM_HEADS, dtype=jnp.float32)[None, :] + nrm((nB, MLSTM_HEADS), 0.1),
        'g_mlstm_head': gain((nB, MLSTM_HV)),
        'w_mlstm_out': nrm((nB, MLSTM_HV, D_MODEL), MLSTM_HV ** -0.5),
        'g_final': gain((D_MODEL,)),
    }

def reference(x_prompt, x_sample, cache_ckv, cache_krope, state_C, state_n, state_m, page_table,
              p_prompt, p_sample, g_ffa, w_ffa_in, w_ffa_out, g_mix, g_ffb, w_ffb_in, w_ffb_out,
              g_ple, w_ple_gate, w_ple_proj, w_mla_in, g_q_lat, g_kv_lat, w_uq, w_uk, w_uv, w_mla_out,
              w_mlstm_in, b_igate, b_fgate, g_mlstm_head, w_mlstm_out, g_final):
    seq = x_prompt.shape[1]
    dec_seq = x_sample.shape[1]
    past = page_table.shape[1] * cache_ckv.shape[2]
    positions = (jnp.arange(seq), past + jnp.arange(dec_seq))
    xs = [x_prompt, x_sample]
    ps = (p_prompt, p_sample)
    ckv_out, kr_out = ([], []), ([], [])
    C_out, n_out, m_out = ([], []), ([], []), ([], [])
    for i in range(DEPTH):
        j = i // N_MIXERS
        for g in range(2):
            x = xs[g]
            pos = positions[g]
            x = x + 0.5 * swiglu(rmsnorm(x, g_ffa[i]), w_ffa_in[i], w_ffa_out[i])
            h = rmsnorm(x, g_mix[i])
            if i % N_MIXERS == 0:
                q_nope, q_rope, ckv, kr = mla_project(h, pos, w_mla_in[j], g_q_lat[j], g_kv_lat[j], w_uq[j])
                if g == 0:
                    o_lat = mla_attend_prompt(q_nope, q_rope, ckv, kr, w_uk[j])
                else:
                    o_lat = mla_attend_sample(q_nope, q_rope, ckv, kr, cache_ckv, cache_krope, j,
                                              page_table, w_uk[j])
                mix = mla_output(o_lat, w_uv[j], w_mla_out[j])
                ckv_out[g].append(ckv)
                kr_out[g].append(kr)
            else:
                if g == 0:
                    nb = x.shape[0]
                    C0 = jnp.zeros((nb, MLSTM_HEADS, MLSTM_DK, MLSTM_DV), jnp.float32)
                    n0 = jnp.zeros((nb, MLSTM_HEADS, MLSTM_DK), jnp.float32)
                    m0 = jnp.zeros((nb, MLSTM_HEADS), jnp.float32)
                else:
                    C0, n0, m0 = state_C[j], state_n[j], state_m[j]
                mix, (C, n, m) = mlstm_mixer(h, C0, n0, m0, w_mlstm_in[j], b_igate[j], b_fgate[j],
                                             g_mlstm_head[j], w_mlstm_out[j])
                C_out[g].append(C)
                n_out[g].append(n)
                m_out[g].append(m)
            x = x + mix
            x = x + 0.5 * swiglu(rmsnorm(x, g_ffb[i]), w_ffb_in[i], w_ffb_out[i])
            gate = jax.nn.sigmoid(rmsnorm(x, g_ple[i]) @ w_ple_gate[i])
            x = x + gate * (ps[g][i] @ w_ple_proj[i])
            xs[g] = x
    y_prompt = rmsnorm(xs[0], g_final)
    y_sample = rmsnorm(xs[1], g_final)
    return (y_prompt, y_sample,
            jnp.stack(ckv_out[0]), jnp.stack(kr_out[0]), jnp.stack(ckv_out[1]), jnp.stack(kr_out[1]),
            jnp.stack(C_out[0]), jnp.stack(n_out[0]), jnp.stack(m_out[0]),
            jnp.stack(C_out[1]), jnp.stack(n_out[1]), jnp.stack(m_out[1]))


_drawn_inputs = setup_inputs


def setup_inputs(seed=0):
    import zlib

    import numpy as np

    out = dict(_drawn_inputs(seed))
    spreads = {}
    factors = {'g_ffa': 3.191,
     'g_ffb': 4.44,
     'g_ple': 8.0,
     'g_q_lat': 8.0,
     'g_kv_lat': 3.039,
     'g_mlstm_head': 7.4,
     'g_final': 2.873}
    for name, (base, spread) in spreads.items():
        noise = np.random.default_rng([zlib.crc32(name.encode()), seed]).standard_normal(out[name].shape)
        drawn = base * np.exp(spread * noise) if base else spread * noise
        out[name] = __import__('jax').numpy.asarray(drawn.astype(out[name].dtype))
    for name, factor in factors.items():
        out[name] = (out[name] * factor).astype(out[name].dtype)
    return out
```

```python
from contextlib import ExitStack

import numpy as np

import concourse.bass as bass
from concourse import mybir

ACT = mybir.ActivationFunctionType
ALU = mybir.AluOpType
AX = mybir.AxisListType
F32 = mybir.dt.float32
F32R = mybir.dt.float32r
BF16 = mybir.dt.bfloat16

P = 128
D = 1024
NC_D = D // P
FF = 2816
NC_F = FF // P
TP, TS = 512, 64
T = TP + TS
H = T // 2
NB, TB = 8, 8
NTT = 5
EPS = 1e-6
NH, NOPE, ROPE, VD = 16, 64, 32, 64
QR, KR = 384, 256
PAGE, NPG = 128, 16
SCALE = (NOPE + ROPE) ** -0.5
LH, DK, DV = 4, 128, 256
CAP = 15.0
PD = 256
UNIT = 112
RAW, SPLIT = 4, 2
NEG = -1e30
FF_PARTS = [(0, 6), (6, 12), (12, 17), (17, 22)]

GAINS = ["ffa0", "mix0", "ffb0", "ple0", "ffa1", "mix1", "ffb1", "ple1", "final", "head"]
GCOL = {n: i * NC_D for i, n in enumerate(GAINS)}
GCOL["q"], GCOL["kv"] = 80, 83
NG = 85
C_ID, C_ONE, C_ROPE, C_BLK, C_SEL, C_TRI, C_STRI = 0, 128, 136, 712, 720, 1232, 1360
NCF = 1424
B_ID, B_CAUSAL, B_SAMPLE = 0, 128, 256
NCB = 768

STAGES = [("embed", 8, 8)]
for _l in (0, 1):
    STAGES += [(f"ffa{_l}_in", 44, 44), (f"ffa{_l}_out", 32, 8)]
    STAGES += [("mla_in", 6, 6), ("mla_heads", 16, 0), ("mla_out", 8, 8)] if _l == 0 else \
        [("mlstm_gates", 1, 1), ("mlstm_in", 24, 24), ("mlstm_out", 8, 8)]
    STAGES += [(f"ffb{_l}_in", 44, 44), (f"ffb{_l}_out", 32, 8), (f"gate{_l}", 8, 8), (f"pe{_l}", 0, 2), (f"proj{_l}", 8, 8)]
P0, T0 = {}, {}
_p = _t = 0
for _n, _a, _b in STAGES:
    P0[_n], T0[_n] = _p, _t
    _p, _t = _p + _a, _t + _b
NPANEL = _p


class Region:

    def __init__(self, nc, start, end):
        self.nc, self.start, self.at, self.end = nc, start, start, end

    def put(self, name, shape, dt=F32):
        size = int(np.prod(shape[1:])) * (2 if dt == BF16 else 4)
        t = self.nc.alloc_sbuf_tensor_at(name, shape, dt, offset=self.at)
        self.at += (size + 31) // 32 * 32
        assert self.at <= self.end, (name, self.at, self.end)
        return t


def hybrid_step(nc, ins, outs):
    I = ins
    with ExitStack() as ctx:
        def sem(name):
            return ctx.enter_context(nc.semaphore(name))

        base = (nc.sbuf_base + 31) // 32 * 32
        whole = Region(nc, base, nc.sbuf_top)
        x = whole.put("x", [P, NC_D, T])
        raw = whole.put("raw", [P, RAW, 8, P])
        whi = whole.put("whi", [P, SPLIT, 8, P], F32R)
        wlo = whole.put("wlo", [P, SPLIT, 8, P], F32R)
        acc = whole.put("acc", [P, NTT * P])
        r = whole.put("r", [P, T])
        gn = whole.put("gn", [P, NG])
        cf = whole.put("cf", [P, NCF])
        cb = whole.put("cb", [P, NCB], BF16)
        sd = whole.put("sd", [P, 8])
        rc = whole.put("rc", [P, 8])
        eps = whole.put("eps", [P, 1])
        ptab0 = nc.alloc_sbuf_tensor_at("ptab", [P, NB * NPG], mybir.dt.int32, offset=whole.at)
        whole.at += 4 * NB * NPG
        whole_m0 = whole.put("m0", [P, NB])
        ident, ones, rope = cf[:, C_ID:C_ID + P], cf[:, C_ONE:C_ONE + 8], cf[:, C_ROPE:C_ROPE + T]
        idb = cb[:, B_ID:B_ID + P]
        X0 = whole.at
        xh = whole.put("xh", [P, NC_D, T], F32R)
        xl = whole.put("xl", [P, NC_D, T], F32R)
        X1 = whole.at
        uh = whole.put("uh", [P, NC_F, T], F32R)
        ul = whole.put("ul", [P, NC_F, T], F32R)
        TMP = whole.at
        tmp = Region(nc, TMP, whole.end)
        tA = tmp.put("tA", [P, T])
        sA = tmp.put("sA", [P, T])
        ub = tmp.put("ub", [P, T])
        sq = tmp.put("sq", [P, T])
        cbf = Region(nc, TMP + 4 * 2 * T, whole.end).put("cbf", [P, NCB])
        pg = Region(nc, X1, TMP)
        sg = pg.put("sg", [P, NC_D, T])
        pn = pg.put("pn", [P, NTT, PD])
        pth = pg.put("pth", [P, 2, T], F32R)
        ptl = pg.put("ptl", [P, 2, T], F32R)
        xin = Region(nc, X1, TMP).put("xin", [P, NTT, D])
        yT = Region(nc, X0, X1).put("yT", [P, NC_D, T])
        ps = nc.psum_tensor("ps", [P, 8, 512], F32)
        ps = ctx.enter_context(ps)
        flat = lambda b, n: ps[:, b:b + (n + 511) // 512, :].rearrange("p b n -> p (b n)")[:, 0:n]

        def half(t):
            return t.rearrange("p (h n) -> p h n", h=2)

        def slot(t):
            return ps[:, 2 * (t % 2):2 * (t % 2) + 2, 0:H]

        raw_ready = [sem(f"raw_ready{s}") for s in range(RAW)]
        whi_ready, wlo_ready = sem("whi_ready"), sem("wlo_ready")
        panel_used = sem("panel_used")
        tile_taken = sem("tile_taken")
        silu_done, u_ready = sem("silu_done"), sem("u_ready")
        xg_ready, acc_done = sem("xg_ready"), sem("acc_done")
        ss_ready, sd_ready, rc_ready, rb_ready = sem("ss_ready"), sem("sd_ready"), sem("rc_ready"), sem("rb_ready")
        in_ready, consts_ready, zeroed = [sem("in_ready0"), sem("in_ready1")], sem("consts_ready"), sem("zeroed")
        chain = sem("dve_chain")
        p_ready, pt_ready, pt_done, sg_ready = sem("p_ready"), sem("pt_ready"), sem("pt_done"), sem("sg_ready")
        y_ready, yt_ready, y_act, y_dve, stored = sem("y_ready"), sem("yt_ready"), sem("y_act"), sem("y_dve"), sem("stored")
        id_ready, x_turned, x_taken, x_sq = sem("id_ready"), sem("x_turned"), sem("x_taken"), sem("x_sq")

        NORMS = ["ffa0", "mix0", "ffb0", "ple0", "ffa1", "mix1", "ffb1", "ple1", "final"]
        XG = {n: 8 * i for i, n in enumerate(NORMS)}
        AC = {n: 8 * i + (5 if i > 1 else 0) for i, n in enumerate(NORMS)}
        AC["q"] = 16
        whole_ptab = ptab0
        mu = Region(nc, X1, TMP)
        oTh = mu.put("oTh", [P, NC_D, T], F32R)
        oTl = mu.put("oTl", [P, NC_D, T], F32R)
        ckv = mu.put("ckv", [P, 2, T])
        krT = mu.put("krT", [P, T])
        QA = mu.put("QA", [P, 3, NB * TB * NH])
        wuv = mu.put("wuv", [P, 2, NH * VD])
        mu1 = Region(nc, mu.at, TMP)
        zc = mu1.put("zc", [P, 6, T])
        cqh = mu1.put("cqh", [P, 3, T], F32R)
        cql = mu1.put("cql", [P, 3, T], F32R)
        Q = mu1.put("Q", [P, 2, T])
        mu2 = Region(nc, mu.at, TMP)
        KEYS = NPG * PAGE + TS
        S = mu2.put("S", [P, 2, KEYS + P - TS])
        KT = mu2.put("KT", [P, 2, 3, 512])
        QAb = mu2.put("QAb", [P, 2, 3, P])
        mx = mu2.put("mx", [P, 2, 8])
        mxx = Region(nc, X0, X1)
        PP = mxx.put("PP", [P, 2, 1280])
        PT = mxx.put("PT", [P, 2, 1280])
        Vp = mxx.put("Vp", [P, 4, P])
        Kp = mxx.put("Kp", [P, 2, TP])
        WT = mxx.put("WT", [P, 2, KR])
        st = mxx.put("st", [P, 2, 12])
        qtmp = mxx.put("qtmp", [P, T])
        pages = Region(nc, X0, X1).put("pages", [P, 2 * NPG, KR + ROPE])
        mt = Region(nc, TMP, whole.end)
        ckt = mt.put("ckt", [P, NTT, KR + ROPE])
        PTs = mt.put("PTs", [P, 2, 512])
        krS = mt.put("krS", [P, TS])
        ptab = whole_ptab
        rl, gql = sA, ub
        QT = [0, P, 3 * P, 6 * P]
        KO = [0, 4 * P, 7 * P, 9 * P]

        cq_ready, ckv_ready, kr_ready = sem("cq_ready"), sem("ckv_ready"), sem("kr_ready")
        ct_ready, ct_taken, wuv_ready = sem("ct_ready"), sem("ct_taken"), sem("wuv_ready")
        kv_ready, k_taken, v_taken, wt_taken = sem("kv_ready"), sem("k_taken"), sem("v_taken"), sem("wt_taken")
        qn_taken, qr_taken = sem("qn_taken"), sem("qr_taken")
        sc_ready, nm_ready, ex_ready, pp_ready = sem("sc_ready"), sem("nm_ready"), sem("ex_ready"), sem("pp_ready")
        qa_ready, qa_taken = sem("qa_ready"), sem("qa_taken")
        tr_ready, tr_act, tr_dve = sem("tr_ready"), sem("tr_act"), sem("tr_dve")
        pv_ready, ov_hi, ov_lo = sem("pv_ready"), sem("ov_hi"), sem("ov_lo")
        pg = [sem(f"page_ready{n}") for n in range(8)]
        kt_ready, kt_act, kt_dve = sem("kt_ready"), sem("kt_act"), sem("kt_dve")
        ss_sc, mx_dve, s_act, qab_ready = sem("sample_scores"), sem("mx_dve"), sem("s_act"), sem("qab_ready")
        snm, sex, sp_ready = sem("snm"), sem("sex"), sem("sample_p")
        s_inv, sp_pool = sem("s_inv"), sem("sample_p_pool")
        pts_ready, pts_taken, spv = sem("pts_ready"), sem("pts_taken"), sem("sample_pv")
        o_act, o_dve = sem("o_act"), sem("o_dve")
        sv_ready, sv_hi, sv_lo = sem("sv_ready"), sem("sv_hi"), sem("sv_lo")
        PM, PH, PO = P0["mla_in"], P0["mla_heads"], P0["mla_out"]

        def mla_loads(sp, load, square):
            w = I["w_mla_in"][0].rearrange("(c p) n -> p c n", p=P)
            sp.dma_start(ptab[0:1, :], I["page_table"].rearrange("(a b) n -> a (b n)", a=1)).then_inc(wuv_ready, 16)
            for m in range(5):
                load(PM + m, 0, lambda d: [(d, w[:, :, m * P:(m + 1) * P], UNIT)])
            last = w[:, :, QR + KR - 64:QR + KR + ROPE]
            load(PM + 5, 0, lambda d: [(d[:, :, 0:96], last, 48),
                                       (d[:, :, 96:112], w[:, :, QR + KR + 16:QR + KR + 32], 32),
                                       (d[:, :, 112:128], w[:, :, QR + KR:QR + KR + 16], 32)])
            uq = I["w_uq"][0].rearrange("(c p) h d -> p c (h d)", p=P)
            uk = I["w_uk"][0].rearrange("(c p) h d -> p c (h d)", p=P)

            def head(k, i, first=False):
                h = i * 4 + k
                e = NOPE + ROPE

                def parts(d):
                    out = [(d[:, 0:3, 0:e], uq[:, :, bass.ds(h * e, e)], 32),
                           (d[:, 0:3, 96:112], uq[:, :, bass.ds(h * e + 80, 16)], 16 if k % 2 == 0 else 32),
                           (d[:, 0:3, 112:128], uq[:, :, bass.ds(h * e + 64, 16)], 16 if k % 2 == 0 else 48)]
                    if k % 2 == 0:
                        out.append((d[:, 3:5, :], uk[:, :, bass.ds(h * NOPE, P)], 48))
                    return out
                if not first and k % 2 == 0:
                    sp.wait_ge(panel_used, PH + k - 2 + i * 4)
                load(PH + k, i * 4, parts, free=first or k % 2 == 1)
            for k in range(4):
                head(k, 0, True)
            sp.wait_ge(panel_used, PM + 6)
            sp.wait_ge(u_ready, 22)
            sp.dma_start(wuv[:, :, :], I["w_uv"][0].rearrange("(c p) h d -> p c (h d)", p=P)).then_inc(wuv_ready, 16)
            with sp.Fori(1, 4) as i:
                for k in range(4):
                    head(k, i)
            sp.wait_ge(ct_taken, 2 * NTT)
            for j in range(NTT):
                n = P if j < 4 else TS
                a = outs["ckv_prompt"][0, 0, j * P:(j + 1) * P, :] if j < 4 else outs["ckv_sample"][0].rearrange("b t r -> (b t) r")
                b = outs["kr_prompt"][0, 0, j * P:(j + 1) * P, :] if j < 4 else outs["kr_sample"][0].rearrange("b t r -> (b t) r")
                sp.dma_start(a, ckt[0:n, j, 0:KR]).then_inc(stored, 16)
                sp.dma_start(b, ckt[0:n, j, KR:KR + ROPE]).then_inc(stored, 16)
            wo = I["w_mla_out"][0].rearrange("(c p) n -> p c n", p=P)
            for k in range(4):
                if k % 2 == 0:
                    sp.wait_ge(panel_used, PO + k - 2)
                load(PO + k, 0, lambda d: [(d, wo[:, :, k * P:(k + 1) * P], UNIT)])

            def page_group(b, g, s):
                sp.wait_ge(wuv_ready, 32)
                for k in range(4):
                    page = sp.value_load(ptab[0:1, bass.ds(b * NPG + 4 * g + k, 1)], min_val=0,
                                         max_val=I["cache_ckv"].shape[1] - 1)
                    q = s * NPG + 4 * g + k
                    sp.dma_start(pages[:, q, 0:KR], I["cache_ckv"][0][bass.ds(page, 1), :, :].rearrange("a k r -> (a k) r")
                                 ).then_inc(pg[s * 4 + g], 16)
                    sp.dma_start(pages[:, q, KR:KR + ROPE],
                                 I["cache_krope"][0][bass.ds(page, 1), :, :].rearrange("a k r -> (a k) r")
                                 ).then_inc(pg[s * 4 + g], 16)
            sp.wait_ge(pv_ready, NH)
            sp.wait_ge(qa_taken, 2 * NH // 2)
            for b in range(2):
                for g in range(4):
                    page_group(b, g, b)
            with sp.Fori(0, 3) as i:
                for s in range(2):
                    for g in range(4):
                        sp.wait_ge(spv, 5 * s + g + 1 + i * 10)
                        page_group(i * 2 + s + 2, g, s)
            for k in range(4, 8):
                load(PO + k, 0, lambda d: [(d, wo[:, :, k * P:(k + 1) * P], UNIT)])

        def mla_lowers(pool, lower, stage):
            for k in range(6):
                lower(PM + k, 0, 8)
            stage("mla_heads", [3] * 4, 4)

            def scale(b, db):
                pool.wait_ge(s_inv, b + 1 + db)
                pool.tensor_tensor(S[:, b % 2, 512:KEYS], S[:, b % 2, 512:KEYS],
                                   mx[:, b % 2, 7:8].to_broadcast([P, KEYS - 512]), ALU.mult).then_inc(sp_pool, 1)
            lower(PO, 0, 8)
            with pool.Fori(0, NB // 2) as i:
                scale(0, i * 2)
                scale(1, i * 2)
            for k in range(1, 8):
                lower(PO + k, 0, 8)

        def mla_acts(act, upper, root, square, norm):
            for k in range(6):
                upper(PM + 1 + k, 0, 8 if k < 5 else 3)
                if k == 0:
                    root(norm, D); norm += 1
                if k == 4:
                    root(norm, QR); norm += 1
            root(norm, KR); norm += 1

            def softmax_exp(h, dyn, s, banks):
                for n in range(4):
                    act.wait_ge(nm_ready, 4 * h + max(n + 1, 2) + dyn * 4)
                    act.activation(PP[:, s, QT[n]:QT[n] + (n + 1) * P], banks[n], ACT.Exp, bias=st[:, s, n:n + 1],
                                   accum_out=st[:, s, 4 + n:5 + n]).then_inc(ex_ready, 1)

            with act.Fori(0, 4) as i:
                for j in (0, 1):
                    h = 2 * j
                    d4, d2 = i * 4, i * 2
                    upper(PH + 1 + h, i * 4, 3)
                    act.wait_ge(panel_used, PH + h + 1 + d4)
                    act.activation(Q[0:64, 0, :].rearrange("p (h n) -> p h n", h=2), ps[0:64, 0:2, 0:H], ACT.Copy).then_inc(qn_taken, 1)
                    act.wait_ge(kv_ready, 3 * j + 1 + i * 6)
                    act.activation(Kp[0:64, 0, :], ps[0:64, 2, :], ACT.Copy).then_inc(k_taken, 1)
                    act.activation(Kp[0:64, 1, :], ps[64:128, 2, :], ACT.Copy).then_inc(k_taken, 1)
                    upper(PH + 2 + h, i * 4, 3 if j == 0 else 8)
                    act.wait_ge(panel_used, PH + h + 2 + d4)
                    act.activation(Q[0:64, 1, :].rearrange("p (h n) -> p h n", h=2), ps[0:64, 0:2, 0:H], ACT.Copy).then_inc(qn_taken, 1)
                    for hh in (0, 1):
                        softmax_exp(h + hh, d4, hh, score_banks(hh))
                    for hh in (0, 1):
                        act.wait_ge(tr_ready, h + hh + 1 + d4)
                        act.activation(PT[:, hh, 0:512], ps[:, pt_banks[hh][0], :], ACT.Copy).then_inc(tr_act, 1)
                    for hh in (0, 1):
                        act.wait_ge(pv_ready, h + hh + 1 + d4)
                        rows = slice(64 * hh, 64 * hh + 64)
                        act.activation(oTh[rows, bass.ds(i * 2 + j, 1), 0:TP].rearrange("p a t -> p (a t)"),
                                       ps[rows, pv_bank[hh], :], ACT.Copy).then_inc(ov_hi, 1)

            def kt_copy(n, dn):
                act.wait_ge(kt_ready, n + 1 + dn)
                act.activation(KT[:, n % 2, 0, :], ps[:, 0, :], ACT.Copy)
                act.activation(KT[0:ROPE, n % 2, 2, :], ps[0:ROPE, 2, :], ACT.Copy).then_inc(kt_act, 1)

            def step(b, db, first, last):
                if not last:
                    for g in range(5):
                        if g < 3:
                            kt_copy(4 * b + g + 1, db * 4)
                        act.wait_ge(mx_dve, 5 * b + g + 1 + db * 5)
                        n = 512 if g < 4 else TS
                        act.activation(S[:, b % 2, g * 512:g * 512 + n], ps[:, 3 + (5 * b + g) % 2, 0:n], ACT.Copy
                                       ).then_inc(s_act, 1)
                if not first:
                    act.wait_ge(spv, 5 * b + db * 5)
                    act.activation(QA[:, 0, bass.ds((b - 1 + db) * P, P)], ps[:, 6, 0:P], ACT.Copy).then_inc(o_act, 1)
                if not last:
                    act.wait_ge(snm, b + 1 + db)
                    act.wait_ge(s_act, 5 * b + 5 + db * 5)
                    act.activation(S[:, b % 2, 0:KEYS], S[:, b % 2, 0:KEYS], ACT.Exp, bias=mx[:, b % 2, 5:6],
                                   accum_out=mx[:, b % 2, 6:7]).then_inc(sex, 1)
            step(0, 0, True, False)
            with act.Fori(0, 3) as i:
                step(1, i * 2, False, False)
                step(2, i * 2, False, False)
            step(7, 0, False, False)
            step(8, 0, False, True)
            for q in (0, 1):
                act.wait_ge(sv_ready, q + 1)
                for s in (0, 1):
                    rows = slice(64 * s, 64 * s + 64)
                    src = ps[rows, q, :].rearrange("p (j s t) -> p j s t", s=2, t=TS)[:, :, s, :]
                    act.activation(oTh[rows, 4 * q:4 * q + 4, TP:T], src, ACT.Copy).then_inc(sv_hi, 1)
            square("mla_out", 8)
            return norm

        def mla_dves(dve, v, link, rms, added):
            rms(D)
            cols = lambda c: gn[:, c:c + 1]
            link(dve.memset(krT[:, :], 0.0))
            link(dve.memset(acc[:, 0:T], 0.0))
            t0 = T0["mla_in"]
            a0 = AC["q"]
            link(dve.tensor_scalar(gql[:, 0:3], gn[:, GCOL["q"]:GCOL["q"] + 3], SCALE, None, ALU.mult))
            for k in range(6):
                dve.wait_ge(panel_used, PM + k + 1)
                dve.tensor_tensor(half(zc[:, k, :]), slot(t0 + k), half(r[:, :]), ALU.mult).then_inc(tile_taken, 1)
                dve.wait_ge(tile_taken, t0 + k + 1)
                if k == 3:
                    rms(QR, rl)
                    link(dve.memset(acc[:, 0:T], 0.0))
                if k < 5:
                    link(dve.tensor_tensor(sq[:, :], zc[:, k, :], zc[:, k, :], ALU.mult))
                    dve.tensor_tensor(acc[:, 0:T], acc[:, 0:T], sq[:, :], ALU.add).then_inc(acc_done, 1)
                    dve.wait_ge(acc_done, a0 + k + 1)
                if k == 3:
                    for c in range(3):
                        link(dve.scalar_tensor_tensor(out=zc[:, c, :], in0=zc[:, c, :], scalar=gql[:, c:c + 1], in1=rl[:, :],
                                                      op0=ALU.mult, op1=ALU.mult))
                        link(dve.tensor_copy(cqh[:, c, :], zc[:, c, :]))
                        dve.tensor_tensor(cql[:, c, :], zc[:, c, :], cqh[:, c, :].bitcast(F32), ALU.subtract).then_inc(cq_ready, 1)
            rms(KR, rl)
            for c in range(2):
                dve.scalar_tensor_tensor(out=ckv[:, c, :], in0=zc[:, 3 + c, :], scalar=cols(GCOL["kv"] + c),
                                         in1=rl[:, :], op0=ALU.mult, op1=ALU.mult).then_inc(ckv_ready, 1)
            link(dve.tensor_tensor(sq[64:96, :], zc[96:128, 5, :], rope[96:128, :], ALU.mult))
            link(dve.tensor_tensor(krT[64:96, :], zc[64:96, 5, :], rope[64:96, :], ALU.mult))
            link(dve.tensor_tensor(krT[64:96, :], krT[64:96, :], sq[64:96, :], ALU.add))
            for s in (0, 1):
                link(dve.tensor_copy(Kp[64:96, s, :], krT[64:96, 0:TP]))
            dve.tensor_copy(krS[0:ROPE, :], krT[64:96, TP:T]).then_inc(kr_ready, 1)
            for j in range(NTT):
                n = P if j < 4 else TS
                dve.wait_ge(ct_ready, j + 1)
                b = 2 + j % 2
                dve.tensor_copy(ckt[0:n, j, 0:KR], ps[0:n, b, 0:KR]).then_inc(ct_taken, 1)
                dve.tensor_copy(ckt[0:n, j, KR:KR + ROPE], ps[0:n, b, KR + 64:KR + 96]).then_inc(ct_taken, 1)
            dve.wait_ge(ct_taken, 2 * NTT)
            dve.memset(st[:, 0, 0:1], 0.0).then_inc(ov_lo, 1)

            def rope_query(h, hh, dh):
                dve.wait_ge(panel_used, PH + h + 1 + dh)
                link(dve.tensor_tensor(half(qtmp[64:96, :]), ps[96:128, 0:2, 0:H], half(rope[96:128, :]), ALU.mult))
                link(dve.tensor_tensor(half(Q[64:96, hh, :]), ps[64:96, 0:2, 0:H], half(rope[64:96, :]), ALU.mult))
                dve.tensor_tensor(Q[64:96, hh, :], Q[64:96, hh, :], qtmp[64:96, :], ALU.add).then_inc(qr_taken, 1)
                dve.wait_ge(qr_taken, h + 1 + dh)
                dst = QA[0:ROPE, 2, :].rearrange("p (t h) -> p t h", h=NH)[:, :, bass.ds(h + dh, 1)]
                link(dve.tensor_copy(dst, Q[64:96, hh, TP:T].rearrange("p (t a) -> p t a", a=1)))

            LP = 2 * 3 + 2
            c0 = v["chain"]
            with dve.Fori(0, 4) as i:
                v["dyn"] = i * (2 * LP)
                for j in (0, 1):
                    h, d4 = 2 * j, i * 4
                    assert v["chain"] == c0 + j * LP
                    rope_query(h, 0, d4)
                    dve.wait_ge(kv_ready, 3 * j + 2 + i * 6)
                    dve.tensor_copy(WT[0:64, 0, :], ps[0:64, 4, 0:KR]).then_inc(wt_taken, 1)
                    dve.tensor_copy(WT[0:64, 1, :], ps[64:128, 4, 0:KR]).then_inc(wt_taken, 1)
                    rope_query(h + 1, 1, d4)
                    for hh in (0, 1):
                        banks = score_banks(hh)
                        for n in range(4):
                            dve.wait_ge(sc_ready, 4 * (h + hh) + max(n + 1, 2) + d4 * 4)
                            dve.tensor_reduce(out=st[:, hh, n:n + 1], in_=banks[n], axis=AX.X, op=ALU.max,
                                              negate=True).then_inc(nm_ready, 1)
                    for hh in (0, 1):
                        dve.wait_ge(ex_ready, 4 * (h + hh) + 4 + d4 * 4)
                        link(dve.reciprocal(st[:, hh, 8:12], st[:, hh, 4:8]))
                        for n in range(4):
                            o = PP[:, hh, QT[n]:QT[n] + (n + 1) * P]
                            dve.tensor_scalar(o, o, st[:, hh, 8 + n:9 + n], None, ALU.mult).then_inc(pp_ready, 1)
                        if hh:
                            continue
                        dve.wait_ge(kv_ready, 3 * j + 3 + i * 6)
                        dve.tensor_copy(Vp[:, :, :].rearrange("p a d -> p (a d)"), ps[:, 1, :]).then_inc(v_taken, 1)
                        dve.wait_ge(qa_ready, j + 1 + i * 2)
                        for s in (0, 1):
                            dst = QA[:, 0:2, :].rearrange("p c (t h) -> p c t h", h=NH)[:, :, :, bass.ds(h + s + d4, 1)]
                            src = ps[:, 4, 256 + 128 * s:384 + 128 * s].rearrange("p (c t a) -> p c t a", c=2, a=1)
                            dve.tensor_copy(dst, src).then_inc(qa_taken, 1)
                    for hh in (0, 1):
                        dve.wait_ge(tr_ready, h + hh + 1 + d4)
                        b = pt_banks[hh]
                        dve.tensor_copy(PT[:, hh, KO[1]:KO[2]], ps[:, b[1], 0:384]).then_inc(tr_dve, 1)
                        dve.tensor_copy(PT[:, hh, KO[2]:1280], ps[:, b[2], 0:384]).then_inc(tr_dve, 1)
                    for hh in (0, 1):
                        dve.wait_ge(ov_hi, h + hh + 1 + d4)
                        rows = slice(64 * hh, 64 * hh + 64)
                        jj = i * 2 + j
                        dve.tensor_tensor(oTl[rows, bass.ds(jj, 1), 0:TP].rearrange("p a t -> p (a t)"),
                                          ps[rows, pv_bank[hh], :],
                                          oTh[rows, bass.ds(jj, 1), 0:TP].rearrange("p a t -> p (a t)").bitcast(F32),
                                          ALU.subtract).then_inc(ov_lo, 1)
            assert v["chain"] == c0 + 2 * LP
            v["chain"] = c0 + 8 * LP
            v["dyn"] = 0

            def kt_copy(n, dn):
                dve.wait_ge(kt_ready, n + 1 + dn)
                dve.tensor_copy(KT[:, n % 2, 1, :], ps[:, 1, :]).then_inc(kt_dve, 1)

            def pts_copy(n, dn, g):
                dve.wait_ge(pts_ready, n + 1 + dn)
                if g < 4:
                    dve.tensor_copy(PTs[:, n % 2, :], ps[:, 5, :]).then_inc(pts_taken, 1)
                else:
                    dve.tensor_copy(PTs[0:TS, n % 2, 0:P], ps[0:TS, 5, 0:P]).then_inc(pts_taken, 1)

            def ahead(b, db):
                dve.wait_ge(kt_ready, 4 * b + 1 + db * 4)
                dve.tensor_copy(KT[:, 0, 0, :], ps[:, 0, :])
                dve.tensor_copy(KT[0:ROPE, 0, 2, :], ps[0:ROPE, 2, :])
                dve.tensor_copy(KT[:, 0, 1, :], ps[:, 1, :]).then_inc(kt_dve, 1)
                link(dve.tensor_copy(QAb[:, b % 2, 0:2, :], QA[:, 0:2, bass.ds((b + db) * P, P)]))
                dve.tensor_copy(QAb[0:ROPE, b % 2, 2, :], QA[0:ROPE, 2, bass.ds((b + db) * P, P)]).then_inc(qab_ready, 1)

            def step(b, db, first, last):
                if not last:
                    kt_copy(4 * b + 1, db * 4)
                for g in range(5):
                    if not last and 0 < g < 3:
                        kt_copy(4 * b + g + 1, db * 4)
                    if not first and g:
                        pts_copy(5 * (b - 1) + g, db * 5, g)
                    if not last:
                        dve.wait_ge(ss_sc, 5 * b + g + 1 + db * 5)
                        n = 512 if g < 4 else TS
                        dve.reduce_max(mx[:, b % 2, g:g + 1], ps[:, 3 + (5 * b + g) % 2, 0:n], AX.X).then_inc(mx_dve, 1)
                    if not first and g == 0:
                        pts_copy(5 * (b - 1) + g, db * 5, g)
                if not first:
                    dve.wait_ge(spv, 5 * b + db * 5)
                    dve.tensor_copy(QA[:, 1, bass.ds((b - 1 + db) * P, P)], ps[:, 7, 0:P]).then_inc(o_dve, 1)
                if not last:
                    dve.wait_ge(mx_dve, 5 * b + 5 + db * 5)
                    dve.tensor_reduce(out=mx[:, b % 2, 5:6], in_=mx[:, b % 2, 0:5], axis=AX.X, op=ALU.max,
                                      negate=True).then_inc(snm, 1)
                    if b < NB - 1:
                        ahead(b + 1, db)
                    dve.wait_ge(sex, b + 1 + db)
                    dve.reciprocal(mx[:, b % 2, 7:8], mx[:, b % 2, 6:7]).then_inc(s_inv, 1)
                    dve.wait_ge(s_inv, b + 1 + db)
                    dve.tensor_scalar(S[:, b % 2, 0:512], S[:, b % 2, 0:512], mx[:, b % 2, 7:8], None, ALU.mult).then_inc(sp_ready, 1)
            ahead(0, 0)
            link(dve.memset(S[:, :, KEYS:KEYS + P - TS], 0.0))
            step(0, 0, True, False)
            c0 = v["chain"]
            with dve.Fori(0, 3) as i:
                v["dyn"] = i * 2
                step(1, i * 2, False, False)
                step(2, i * 2, False, False)
            assert v["chain"] == c0 + 2
            v["chain"], v["dyn"] = c0 + 6, 0
            step(7, 0, False, False)
            step(8, 0, False, True)
            for q in (0, 1):
                for s in (0, 1):
                    rows = slice(64 * s, 64 * s + 64)
                    dve.wait_ge(sv_hi, 2 * q + s + 1)
                    src = ps[rows, q, :].rearrange("p (j s t) -> p j s t", s=2, t=TS)[:, :, s, :]
                    dve.tensor_tensor(oTl[rows, 4 * q:4 * q + 4, TP:T], src,
                                      oTh[rows, 4 * q:4 * q + 4, TP:T].bitcast(F32), ALU.subtract).then_inc(sv_lo, 1)
            added("mla_out", "ffb0")

        pt_banks, pv_bank = [(7, 5, 6), (0, 2, 3)], [6, 7]

        def score_banks(hh):
            a, b, c = (5, 6, 7) if hh == 0 else (2, 3, 0)
            return [ps[:, c, 0:P], ps[:, c, P:3 * P], ps[:, b, 0:3 * P], ps[:, a, :]]

        def mla_pes(pe, v, products, sums, broadcast, tiles, xgh, xgl):
            mm, tr = nc.tensor.matmul, nc.tensor.transpose
            hooks = {1: {4: broadcast}, 4: {3: broadcast}, 5: {6: lambda: sums(2)}}
            for k in range(6):
                pe.wait_ge(tile_taken, T0["mla_in"] + k - 1)
                products(PM + k, 0, 8, xgh, xgl, slot(T0["mla_in"] + k),
                         waits=(lambda n: pe.wait_ge(xg_ready, XG["mix0"] + n + 1)) if k == 0 else None, at=hooks.get(k))
                if k in (0, 3):
                    sums(8 if k == 0 else 3)
            broadcast()
            pe.wait_ge(kr_ready, 1)
            pe.wait_ge(ckv_ready, 2)
            pe.wait_ge(tile_taken, T0["mla_in"] + 6)
            for j in range(NTT):
                n = P if j < 4 else TS
                b = 2 + j % 2
                if j >= 2:
                    pe.wait_ge(ct_taken, 2 * j - 2)
                for c in range(3):
                    src = ckv[:, c, j * P:j * P + n] if c < 2 else krT[:, j * P:j * P + n]
                    ins = tr(ps[0:n, b, c * P:(c + 1) * P], src, ident)
                ins.then_inc(ct_ready, 1)
            pe.wait_ge(cq_ready, 3)
            pe.wait_ge(wuv_ready, 32)
            pe.wait_ge(ov_lo, 1)
            with pe.Fori(0, 4) as i:
                for j in (0, 1):
                    h, d4, d2 = 2 * j, i * 4, i * 2

                    def query(hh):
                        products(PH + h + hh, d4, 3, lambda n: cqh[:, n, :], lambda n: cql[:, n, :], ps[:, 0:2, 0:H])
                    query(0)
                    rw = raw[:, (PH + h + 0) % RAW, :, :]
                    for c in range(2):
                        ins = mm(ps[:, 2, :], rw[:, 3 + c, :], ckv[:, c, 0:TP], start=c == 0, stop=c == 1)
                    ins.then_inc(kv_ready, 1)
                    for c in range(2):
                        ins = tr(ps[:, 4, c * P:(c + 1) * P], rw[:, 3 + c, :], ident)
                    ins.then_inc(kv_ready, 1)
                    pe.wait_ge(qn_taken, h + 1 + d4)
                    pe.wait_ge(qr_taken, h + 1 + d4)
                    query(1)

                    def scores(hh):
                        banks = score_banks(hh)
                        pe.wait_ge(qn_taken, h + hh + 1 + d4)
                        pe.wait_ge(qr_taken, h + hh + 1 + d4)
                        pe.wait_ge(k_taken, 2 * j + 2 + i * 4)
                        for n in range(4):
                            mm(banks[n], Q[0:96, hh, n * P:(n + 1) * P], Kp[0:96, hh, 0:(n + 1) * P], start=True, stop=False)
                            mm(banks[n][:, n * P:(n + 1) * P], idb, cb[:, B_CAUSAL:B_CAUSAL + P], start=False,
                               stop=True).then_inc(sc_ready, 1)
                    pe.wait_ge(ov_lo, h + 1 + d4)
                    scores(0)
                    scores(1)
                    for kt in range(4):
                        for c in range(2):
                            ins = mm(ps[:, 1, kt * P:(kt + 1) * P], ckv[:, c, kt * P:(kt + 1) * P],
                                     wuv[:, c, bass.ds((d2 + j) * P, P)], start=c == 0, stop=c == 1)
                    ins.then_inc(kv_ready, 1)
                    pe.wait_ge(wt_taken, 2 * j + 2 + i * 4)
                    pe.wait_ge(qn_taken, h + 2 + d4)
                    for s in (0, 1):
                        for c in (0, 1):
                            ins = mm(ps[:, 4, 256 + 128 * s + 64 * c:320 + 128 * s + 64 * c],
                                     WT[0:64, s, c * P:(c + 1) * P], Q[0:64, s, TP:T], start=True, stop=True)
                    ins.then_inc(qa_ready, 1)
                    for hh in (0, 1):
                        pe.wait_ge(pp_ready, 4 * (h + hh) + 4 + d4 * 4)
                        bank = pt_banks[hh]
                        where = [ps[:, bank[0], :], ps[:, bank[1], :], ps[:, bank[2], :], ps[:, bank[2], 256:512]]
                        for kt in range(4):
                            for n in range(kt, 4):
                                ins = tr(where[kt][:, (n - kt) * P:(n - kt + 1) * P],
                                         PP[:, hh, QT[n] + kt * P:QT[n] + (kt + 1) * P], ident)
                        ins.then_inc(tr_ready, 1)
                        if hh == 0:
                            continue
                        pe.wait_ge(v_taken, j + 1 + d2)
                        pe.wait_ge(qa_taken, 2 * j + 2 + i * 4)
                        for s in (0, 1):
                            pe.wait_ge(tr_act, h + s + 1 + d4)
                            pe.wait_ge(tr_dve, 2 * (h + s) + 2 + d4 * 2)
                            for kt in range(4):
                                ins = mm(ps[:, pv_bank[s], kt * P:512], Vp[:, kt, :], PT[:, s, KO[kt]:KO[kt] + (4 - kt) * P],
                                         start=kt == 0, stop=kt == 3)
                            ins.then_inc(pv_ready, 1)

            pe.wait_ge(ov_lo, NH + 1)

            def pages_t(b, db, g):
                n = 4 * b + g
                s = b % 2
                pe.wait_ge(pg[s * 4 + g], 128 * (b // 2 + 1) + (db // 2 if isinstance(db, int) else db) * 64)
                if n > 1:
                    pe.wait_ge(kt_act, 3 * b + max(g - 1, 0) + db * 3)
                if n:
                    pe.wait_ge(kt_dve, n + db * 4)
                for k in range(4):
                    for c in range(3):
                        w = P if c < 2 else ROPE
                        ins = tr(ps[0:w, c, k * P:(k + 1) * P], pages[:, s * NPG + 4 * g + k, c * P:c * P + w], ident)
                ins.then_inc(kt_ready, 1)

            def scores_s(b, db, g):
                m = 5 * b + g
                bank = ps[:, 3 + m % 2, :]
                s = b % 2
                if g == 0:
                    pe.wait_ge(qab_ready, b + 1 + db)
                if m >= 2:
                    pe.wait_ge(s_act, m - 1 + db * 5)
                    pe.wait_ge(mx_dve, m - 1 + db * 5)
                if g < 4:
                    if g:
                        pe.wait_ge(kt_act, 3 * b + g + db * 3)
                    pe.wait_ge(kt_dve, 4 * b + g + 1 + db * 4)
                    for c in range(3):
                        w = P if c < 2 else ROPE
                        ins = mm(bank, QAb[0:w, s, c, :], KT[0:w, g % 2, c, :], start=c == 0, stop=c == 2)
                else:
                    mm(bank[:, 0:TS], QAb[:, s, 0, :], ckv[:, 0, TP:T], start=True, stop=False)
                    mm(bank[:, 0:TS], QAb[:, s, 1, :], ckv[:, 1, TP:T], start=False, stop=False)
                    mm(bank[:, 0:TS], QAb[0:ROPE, s, 2, :], krS[0:ROPE, :], start=False, stop=False)
                    ins = mm(bank[:, 0:TS], idb, cb[:, bass.ds(B_SAMPLE + (b + db) * TS, TS)], start=False, stop=True)
                ins.then_inc(ss_sc, 1)

            def probs_t(b, db, g):
                n, s = 5 * (b - 1) + g, (b - 1) % 2
                if g == 0:
                    pe.wait_ge(sp_ready, b + db)
                if g == 1:
                    pe.wait_ge(sp_pool, b + db)
                if n:
                    pe.wait_ge(pts_taken, n + db * 5)
                if g < 4:
                    for k in range(4):
                        ins = tr(ps[:, 5, k * P:(k + 1) * P], S[:, s, g * 512 + k * P:g * 512 + (k + 1) * P], ident)
                else:
                    ins = tr(ps[:, 5, 0:P], S[:, s, 2048:2048 + P], ident)
                ins.then_inc(pts_ready, 1)

            def out_s(b, db, g):
                n, s = 5 * (b - 1) + g, (b - 1) % 2
                pe.wait_ge(pts_taken, n + 1 + db * 5)
                if g == 0 and b > 1:
                    pe.wait_ge(o_act, b - 1 + db)
                    pe.wait_ge(o_dve, b - 1 + db)
                if g < 4:
                    for k in range(4):
                        for c in (0, 1):
                            ins = mm(ps[:, 6 + c, 0:P], pages[:, s * NPG + 4 * g + k, c * P:(c + 1) * P],
                                     PTs[:, n % 2, k * P:(k + 1) * P], start=g == 0 and k == 0, stop=False)
                else:
                    for c in (0, 1):
                        ins = mm(ps[:, 6 + c, 0:P], ckt[0:TS, 4, c * P:(c + 1) * P], PTs[0:TS, n % 2, 0:P],
                                 start=False, stop=True)
                ins.then_inc(spv, 1)

            def step(b, db, first, last):
                if not last:
                    pages_t(b, db, 0)
                    pages_t(b, db, 1)
                    scores_s(b, db, 0)
                if not first:
                    probs_t(b, db, 0)
                for g in range(5):
                    if not last and g < 2:
                        pages_t(b, db, g + 2)
                    if not first:
                        out_s(b, db, g)
                        if g < 4:
                            probs_t(b, db, g + 1)
                    if not last and g < 4:
                        scores_s(b, db, g + 1)
            step(0, 0, True, False)
            with pe.Fori(0, 3) as i:
                step(1, i * 2, False, False)
                step(2, i * 2, False, False)
            step(7, 0, False, False)
            step(8, 0, False, True)
            pe.wait_ge(o_act, NB)
            pe.wait_ge(o_dve, NB)
            lat = QA[:, 0:2, :].rearrange("p c (t h) -> p c t h", h=NH)
            for q in (0, 1):
                for h in range(8 * q, 8 * q + 8):
                    for c in (0, 1):
                        ins = mm(ps[:, q, (h % 8) * TS:(h % 8 + 1) * TS], wuv[:, c, (h // 2) * P:(h // 2 + 1) * P],
                                 lat[:, c, :, h], start=c == 0, stop=c == 1)
                ins.then_inc(sv_ready, 1)
            pe.wait_ge(sv_lo, 4)
            tiles("mla_out", 8, 1, lambda n: oTh[:, n, :], lambda n: oTl[:, n, :], 2, 4)

        lu = Region(nc, X1, TMP)
        gTh = lu.put("gTh", [P, NC_D, T], F32R)
        gTl = lu.put("gTl", [P, NC_D, T], F32R)
        qT = lu.put("qT", [P, LH, T])
        kT = lu.put("kT", [P, LH, T])
        so = lu.put("so", [P, NC_D, T])
        Cb = lu.put("Cb", [P, NB, DV + 1])
        cols = lu.put("cols", [P, 64])
        nT = lu.put("nT", [P, NB * LH])
        nP = lu.put("nP", [P, LH])
        bg = lu.put("bg", [P, 2])
        den = lu.put("den", [P, 16])
        V0 = lu.at
        vT = lu.put("vT", [P, NC_D, T])
        lv = Region(nc, V0, TMP)
        Dm = lv.put("Dm", [P, 1280 + TS])
        SD = lv.put("SD", [P, 1280 + P])
        qd = lv.put("qd", [P, TS])
        qn = lv.put("qn", [P, P])
        kw = lv.put("kw", [P, 4, DK])
        nrow = lv.put("nrow", [P, P])
        nst = lv.put("nst", [NB * LH, DK])
        sqn = Region(nc, V0, TMP).put("sqn", [P, 2, NTT * P])
        lx = Region(nc, X0, X1)
        Vt = lx.put("Vt", [P, NTT, LH, DV + 1])
        kt = lx.put("kt", [P, NTT, LH, DK])
        kwb = lx.put("kwb", [P, NB, DK])
        wC = lx.put("wC", [P, NTT * LH])
        Wm = lx.put("Wm", [P, LH, NB])
        eC = lx.put("eC", [P, NTT * LH])
        lt = Region(nc, TMP, whole.end)
        RB = lt.put("RB", [P, T])
        lt2 = Region(nc, lt.at, whole.end)
        RA, RC, RD = (lt.put(n, [P, T]) for n in ("RA", "RC", "RD"))
        RE = lt.put("RE", [P, 2 * TS + NB])
        Mb = lt2.put("Mb", [P, T + TS + NB])
        Md = lt2.put("Md", [P, T])
        Co = lt2.put("Co", [P, DV + 1])
        m0 = whole_m0
        RX = Md
        nst0 = Region(nc, X1, TMP).put("nst0", [NB * LH, DK])
        SO = [0, 4 * P, 7 * P, 9 * P, 10 * P]
        GP, IP, LO = P0["mlstm_gates"], P0["mlstm_in"], P0["mlstm_out"]
        GT, IT = T0["mlstm_gates"], T0["mlstm_in"]
        st_ready, g_dve, g_act = sem("state_ready"), sem("g_dve"), sem("g_act")
        o_pre, o_sig, m_ready, kv_t, kv_c = sem("o_pre"), sem("o_sig"), sem("m_ready"), sem("kv_t"), sem("kv_c")
        ct2, cc2, wc_in, wc_ex = sem("cols_t"), sem("cols_c"), sem("wc_in"), sem("wc_ex")
        l_mb, l_md, l_dec, l_D = sem("l_mb"), sem("l_md"), sem("l_dec"), sem("l_D")
        l_S, l_SD, l_qn, l_num, l_den = sem("l_S"), sem("l_SD"), sem("l_qn"), sem("l_num"), sem("l_den")
        l_sq, l_ss, l_v, l_rs, l_gc, l_gb = sem("l_sq"), sem("l_ss"), sem("l_v"), sem("l_rs"), sem("l_gc"), sem("l_gb")
        l_kw, l_kwb, l_cp, l_co, l_cost = sem("l_kw"), sem("l_kwb"), sem("l_cp"), sem("l_co"), sem("l_cost")
        l_C, l_cs, l_cn, l_cst, l_out = sem("l_C"), sem("l_cs"), sem("l_cn"), sem("l_cst"), sem("l_out")
        l_nt, l_nc = sem("l_nt"), sem("l_nc")

        def mlstm_loads(sp, load, square):
            w = I["w_mlstm_in"][0].rearrange("(c p) n -> p c n", p=P)
            G = 2 * LH * DK + 2 * LH * DV
            load(GP, 0, lambda d: [(d[:, :, 0:8], w[:, :, G:G + 8], 16), (d[:, :, 8:32], w[:, :, 0:24], 16),
                                   (d[:, :, 32:36], w[:, :, G + 4:G + 8], 32), (d[:, :, 36:128], w[:, :, 0:92], 48)])
            with sp.Fori(0, 6) as i:
                for k in range(4):
                    load(IP + k, i * 4, lambda d: [(d, w[:, :, bass.ds((i * 4 + k) * P, P)], UNIT)])
            wo = I["w_mlstm_out"][0].rearrange("(c p) n -> p c n", p=P)
            for k in range(4):
                load(LO + k, 0, lambda d: [(d, wo[:, :, k * P:(k + 1) * P], UNIT)])
            sC = I["state_C"][0].rearrange("b h k v -> k b h v")
            oC = outs["C_sample"][0].rearrange("b h k v -> k b h v")
            with nc.allow_non_contiguous_dma(reason="four stabilisers a row"):
                sp.wait_ge(m_ready, 1)
                sp.dma_start(outs["m_prompt"][0].rearrange("b h -> h b"), RD[0:LH, TP - 1:TP]).then_inc(stored, 16)
                sp.dma_start(outs["m_sample"][0].rearrange("b h -> h b"),
                             RD[0:LH, TP:T].rearrange("h (b t) -> h b t", t=TB)[:, :, TB - 1]).then_inc(stored, 16)
            sp.wait_ge(st_ready, 64)
            for h in range(LH):
                if h:
                    sp.wait_ge(l_cn, NB * h)
                    sp.dma_start(oC[:, :, h - 1, :], Cb[:, :, 0:DV]).then_inc(l_cst, 16)
                    sp.wait_ge(l_cst, 16 * h)
                sp.dma_start(Cb[:, :, 0:DV], sC[:, :, h, :]).then_inc(l_C, 16)
                sp.wait_ge(l_co, 2 * h + 2)
                sp.dma_start(outs["C_prompt"][0, 0, h], Co[:, 0:DV]).then_inc(l_cost, 16)
            sp.wait_ge(l_cn, NB * LH)
            sp.dma_start(oC[:, :, LH - 1, :], Cb[:, :, 0:DV]).then_inc(l_cst, 16)
            sp.wait_ge(l_nc, 2)
            sp.dma_start(outs["n_prompt"][0, 0], nrow[0:LH, :]).then_inc(stored, 16)
            sp.dma_start(outs["n_sample"][0].rearrange("b h k -> (b h) k"), nst[:, :]).then_inc(stored, 16)
            sp.wait_ge(l_cst, 16 * LH)
            sp.wait_ge(l_cost, 16 * LH)
            for k in range(4, 8):
                load(LO + k, 0, lambda d: [(d, wo[:, :, k * P:(k + 1) * P], UNIT)])

        def mlstm_lowers(pool, lower, stage):
            lower(GP, 0, 8)
            stage("mlstm_in", [8] * 4, 6)
            lower(LO, 0, 8)
            pool.memset(den[:, 15:16], -0.5).then_inc(l_rs, 1)
            for h in range(LH):
                pool.wait_ge(l_v, h + 1)
                pool.wait_ge(l_rs, h + 1)
                pool.tensor_tensor(den[:, 10:15], den[:, 5:10], den[:, 15:16].to_broadcast([P, 5]), ALU.pow).then_inc(l_rs, 1)
            for k in range(1, 8):
                lower(LO + k, 0, 8)

        def mlstm_acts(act, upper, root, square, norm):
            upper(GP + 1, 0, 8)
            root(norm, D); norm += 1
            with nc.allow_non_contiguous_dma(reason="biases and stabilisers, a word each"):
                act.dma_start(bg[0:LH, 0:1], I["b_igate"].rearrange("a h -> h a")).then_inc(st_ready, 16)
                act.dma_start(bg[0:LH, 1:2], I["b_fgate"].rearrange("a h -> h a")).then_inc(st_ready, 16)
                act.dma_start(m0[0:LH, :], I["state_m"][0].rearrange("b h -> h b")).then_inc(st_ready, 16)
            act.wait_ge(panel_used, GP)
            act.dma_start(nst0[:, :], I["state_n"][0].rearrange("b h k -> (b h) k")).then_inc(st_ready, 16)
            upper(IP + 1, 0, 8)
            act.wait_ge(g_dve, 1)
            act.activation(RA[0:LH, :], RA[0:LH, :], ACT.Tanh, bias=bg[0:LH, 0:1], scale=1.0 / CAP)
            act.activation(RB[0:LH, :], RB[0:LH, :], ACT.Tanh, bias=bg[0:LH, 1:2], scale=1.0 / CAP).then_inc(g_act, 1)
            act.wait_ge(g_act, 1)
            act.activation(RC[0:LH, :], RB[0:LH, :], ACT.Exp, scale=-CAP).then_inc(g_act, 1)
            upper(IP + 2, 0, 8)
            act.wait_ge(g_dve, 2)
            act.activation(RB[0:LH, :], RD[0:LH, :], ACT.Ln).then_inc(g_act, 1)
            for k in range(2, 16):
                upper(IP + 1 + k, 0, 8)
            for c in range(NC_D):
                upper(IP + 17 + c, 0, 8)
                act.wait_ge(tile_taken, IT + 17 + c)
                act.activation(so[:, c, :], so[:, c, :], ACT.Sigmoid).then_inc(o_sig, 1)
            act.wait_ge(wc_in, 1)
            act.activation(wC[:, :], wC[:, :], ACT.Exp).then_inc(wc_ex, 1)
            act.activation(eC[:, :], cols[:, 20:40], ACT.Exp, scale=-1.0).then_inc(wc_ex, 1)
            for h in range(LH):
                act.wait_ge(l_mb, h + 1)
                act.activation(Mb[:, T:T + TS + NB], Mb[:, T:T + TS + NB], ACT.Exp).then_inc(l_dec, 1)
                act.wait_ge(l_md, h + 1)
                for s in range(NTT):
                    n = P if s < 4 else TS
                    ins = act.activation(Dm[0:n, SO[s]:SO[s] + n], Md[0:n, s * P:s * P + n], ACT.Exp,
                                         bias=cols[0:n, 4 * s + h:4 * s + h + 1], scale=-1.0)
                    if s < 3:
                        ins = act.activation(Dm[:, SO[s] + P:SO[s + 1]], Mb[:, (s + 1) * P:TP], ACT.Exp,
                                             bias=cols[:, 4 * s + h:4 * s + h + 1], scale=-1.0)
                    ins.then_inc(l_D, 1)
                for s in range(4):
                    ins = act.activation(kw[:, s, :], kt[:, s, h, :], ACT.Copy, scale=wC[:, 4 * s + h:4 * s + h + 1])
                ins.then_inc(l_kw, 1)
                for c in (0, 1):
                    act.wait_ge(l_num, 3 * h + c + 1)
                    act.wait_ge(l_SD, 5 * h + 5)
                    act.activation(sqn[:, c, 0:TP], ps[:, 6 + c, :], ACT.Square).then_inc(l_sq, 1)
                act.wait_ge(l_num, 3 * h + 3)
                act.activation(sqn[:, :, T:NTT * P], ident.rearrange("p (c t) -> p c t", c=2), ACT.Copy, scale=0.0)
                act.activation(sqn[:, :, TP:T], ps[:, 5, P:2 * P].rearrange("p (c t) -> p c t", c=2), ACT.Square).then_inc(l_sq, 1)
            square("mlstm_out", 8)
            return norm

        def mlstm_dves(dve, v, link, rms, added):
            rms(D)
            dve.wait_ge(st_ready, 64)
            link(dve.tensor_scalar(bg[0:LH, :], bg[0:LH, :], 1.0 / CAP, None, ALU.mult))
            link(dve.memset(cols[:, :], 0.0))
            dve.wait_ge(panel_used, GP + 1)
            tg = 2 * (GT % 2)
            link(dve.tensor_tensor(half(RA[0:LH, :]), ps[0:LH, tg:tg + 2, 0:H], half(r[0:LH, :]), ALU.mult))
            dve.tensor_tensor(half(RB[0:LH, :]), ps[32:32 + LH, tg:tg + 2, 0:H], half(r[32:32 + LH, :]), ALU.mult).then_inc(tile_taken, 1)
            dve.wait_ge(tile_taken, GT + 1)
            dve.memset(den[:, 0:1], 0.0).then_inc(g_dve, 1)

            rows = lambda t: t[0:LH, 0:TP]
            segs = lambda t: t[0:LH, TP:T].rearrange("h (b t) -> h b t", t=TB)

            def scan(n, src, dst, op):
                d = 1 << n
                link(dve.tensor_tensor(rows(dst)[:, d:], rows(src)[:, d:], rows(src)[:, 0:TP - d], op))
                link(dve.tensor_copy(rows(dst)[:, 0:d], rows(src)[:, 0:d]))
                if n < 3:
                    link(dve.tensor_tensor(segs(dst)[:, :, d:], segs(src)[:, :, d:], segs(src)[:, :, 0:TB - d], op))
                    link(dve.tensor_copy(segs(dst)[:, :, 0:d], segs(src)[:, :, 0:d]))

            def evacuate(t):
                dst = (qT[:, t, :] if t < 4 else kT[:, t - 4, :] if t < 8 else vT[:, t - 8, :] if t < 16
                       else so[:, t - 16, :])
                dve.wait_ge(panel_used, IP + t + 1)
                if t < 4:
                    dve.scalar_tensor_tensor(out=half(dst), in0=slot(IT + t), scalar=DK ** -0.5, in1=half(r[:, :]),
                                             op0=ALU.mult, op1=ALU.mult).then_inc(tile_taken, 1)
                else:
                    dve.tensor_tensor(half(dst), slot(IT + t), half(r[:, :]), ALU.mult).then_inc(tile_taken, 1)

            L = slice(0, LH)
            for t in range(24):
                evacuate(t)
                if t == 0:
                    dve.wait_ge(g_act, 2)
                    dve.tensor_scalar(RD[L, :], RC[L, :], 1.0, None, ALU.add).then_inc(g_dve, 1)
                    dve.wait_ge(g_dve, 2)
                if t == 1:
                    dve.wait_ge(g_act, 3)
                    link(dve.tensor_scalar(RD[L, :], RD[L, :], 1.0, None, ALU.subtract))
                    link(dve.reciprocal(RD[L, :], RD[L, :]))
                if t == 2:
                    link(dve.tensor_tensor(RC[L, :], RC[L, :], RD[L, :], ALU.mult))
                    link(dve.scalar_tensor_tensor(out=RB[L, :], in0=RB[L, :], scalar=-1.0, in1=RC[L, :],
                                                  op0=ALU.mult, op1=ALU.mult))
                if 3 <= t < 12:
                    n = t - 3
                    scan(n, (RB, RC)[n % 2], (RC, RB)[n % 2], ALU.add)
                    if n == 2:
                        link(dve.tensor_copy(RB[L, TP:T], RC[L, TP:T]))
                if t == 12:
                    link(dve.scalar_tensor_tensor(out=RA[L, :], in0=RA[L, :], scalar=CAP, in1=RC[L, :],
                                                  op0=ALU.mult, op1=ALU.subtract))
                    scan(0, RA, RB, ALU.max)
                if 13 <= t < 21:
                    n = t - 12
                    scan(n, (RB, RD)[(n - 1) % 2], (RD, RB)[(n - 1) % 2], ALU.max)
                if t == 21:
                    link(dve.tensor_scalar(rows(RB), rows(RB), 0.0, None, ALU.max))
                    mb = m0[0:LH, :].rearrange("h (b a) -> h b a", a=1).to_broadcast([LH, NB, TB])
                    link(dve.tensor_tensor(segs(RB), segs(RB), mb, ALU.max))
                    dve.tensor_tensor(RD[L, :], RC[L, :], RB[L, :], ALU.add).then_inc(m_ready, 1)
                    end = segs(RB)[:, :, TB - 1:TB]
                    link(dve.tensor_copy(RE[L, 0:TS].rearrange("h (b t) -> h b t", t=TB), end.to_broadcast([LH, NB, TB])))
                    link(dve.tensor_tensor(RE[L, TS:2 * TS].rearrange("h (b t) -> h b t", t=TB), mb, segs(RB), ALU.subtract))
                    link(dve.tensor_tensor(RE[L, 2 * TS:2 * TS + NB].rearrange("h (b a) -> h b a", a=1),
                                           m0[0:LH, :].rearrange("h (b a) -> h b a", a=1), end, ALU.subtract))
                    dve.memset(den[:, 1:2], 0.0).then_inc(g_dve, 1)
            dve.wait_ge(ct2, 1)
            link(dve.tensor_copy(cols[:, 0:16], ps[:, 4, 0:16]))
            link(dve.tensor_copy(cols[0:TS, 16:20], ps[0:TS, 4, 16:20]))
            link(dve.tensor_copy(cols[:, 20:36], ps[:, 4, 20:36]))
            link(dve.tensor_copy(cols[0:TS, 36:44], ps[0:TS, 4, 36:44]))
            link(dve.tensor_copy(cols[:, 44:48], ps[:, 4, 44:48]))
            link(dve.tensor_copy(nT[:, :], ps[:, 4, 64:96]))
            mt_ = cols[:, 44:48].rearrange("p (a h) -> p a h", a=1).to_broadcast([P, 4, LH])
            link(dve.memset(wC[:, 16:20], 0.0))
            link(dve.tensor_tensor(wC[:, 0:16].rearrange("p (s h) -> p s h", h=LH),
                                   cols[:, 0:16].rearrange("p (s h) -> p s h", h=LH), mt_, ALU.subtract))
            dve.tensor_tensor(wC[0:TS, 16:20], cols[0:TS, 16:20], cols[0:TS, 40:44], ALU.subtract).then_inc(wc_in, 1)
            link(dve.memset(Vt[:, :, :, DV:DV + 1], 1.0))
            for j in range(NTT):
                n = P if j < 4 else TS
                for q in range(3):
                    dve.wait_ge(kv_t, 3 * j + q + 1)
                    src = ps[0:n, 5 + q, :]
                    if q == 0:
                        dve.tensor_copy(kt[0:n, j, :, :].rearrange("p h d -> p (h d)"), src).then_inc(kv_c, 1)
                    else:
                        dve.tensor_copy(Vt[0:n, j, 2 * q - 2:2 * q, 0:DV], src.rearrange("p (h d) -> p h d", h=2)).then_inc(kv_c, 1)
            dve.wait_ge(kv_c, 3 * NTT)
            dve.wait_ge(wc_ex, 2)
            wm = wC[0:TS, 16:20].rearrange("p (h a) -> p h a", a=1).to_broadcast([TS, LH, NB])
            bm = cf[0:TS, C_BLK:C_BLK + NB].rearrange("p (a b) -> p a b", a=1).to_broadcast([TS, LH, NB])
            link(dve.tensor_tensor(Wm[0:TS, :, :], wm, bm, ALU.mult))
            link(dve.memset(SD[:, 1280:1280 + P], 0.0))
            link(dve.memset(qn[:, :], 0.0))
            tri = cf[:, C_TRI:C_TRI + P].rearrange("p (a t) -> p a t", a=1).to_broadcast([P, 4, P])
            for h in range(LH):
                dve.wait_ge(l_gb, 2 * h + 1)
                if h:
                    dve.wait_ge(l_D, NTT * h)
                dve.tensor_copy(Mb[:, :], flat(0, T + TS + NB)).then_inc(l_mb, 1)
                dve.wait_ge(l_mb, h + 1)
                link(dve.tensor_tensor(Md[:, 0:TP].rearrange("p (s t) -> p s t", s=4),
                                       Mb[:, 0:TP].rearrange("p (s t) -> p s t", s=4), tri, ALU.add))
                dve.tensor_tensor(Md[0:TS, TP:T], Mb[0:TS, TP:T], cf[0:TS, C_STRI:C_STRI + TS], ALU.add).then_inc(l_md, 1)
                for s in range(NTT):
                    dve.wait_ge(l_S, NTT * h + (s + 1 if s != 2 else 4))
                    dve.wait_ge(l_D, NTT * h + s + 1)
                    bank, o = (2, 0) if s == 0 else (3, 0) if s == 1 else (4, 0) if s == 2 else (4, 256) if s == 3 else (5, 0)
                    w, n = (SO[s + 1] - SO[s], P) if s < 4 else (TS, TS)
                    dve.tensor_tensor(SD[0:n, SO[s]:SO[s] + w], ps[0:n, bank, o:o + w], Dm[0:n, SO[s]:SO[s] + w],
                                      ALU.mult).then_inc(l_SD, 1)
                dve.wait_ge(l_dec, h + 1)
                link(dve.tensor_tensor(qd[:, :], qT[:, h, TP:T], Mb[:, T:T + TS], ALU.mult))
                nh = nT[:, :].rearrange("p (b h) -> p b h", h=LH)[:, :, h:h + 1].to_broadcast([P, NB, TB])
                dve.tensor_tensor(qn[:, 0:TS].rearrange("p (b t) -> p b t", t=TB),
                                  qd[:, :].rearrange("p (b t) -> p b t", t=TB), nh, ALU.mult).then_inc(l_qn, 1)
                ks = kt[0:TS, 4, h, :].rearrange("p (a d) -> p a d", a=1).to_broadcast([TS, NB, DK])
                ws = Wm[0:TS, h, :].rearrange("p (b a) -> p b a", a=1).to_broadcast([TS, NB, DK])
                dve.tensor_tensor(kwb[0:TS, :, :], ks, ws, ALU.mult).then_inc(l_kwb, 1)
                if h:
                    dve.wait_ge(l_cost, 16 * h)
                dve.wait_ge(l_cp, h + 1)
                dve.tensor_copy(Co[:, :], ps[:, 2, 0:DV + 1]).then_inc(l_co, 1)
                dve.wait_ge(l_co, 2 * h + 1)
                dve.tensor_copy(nP[:, h:h + 1], Co[:, DV:DV + 1]).then_inc(l_co, 1)
                dve.wait_ge(l_ss, h + 1)
                link(dve.tensor_copy(den[:, 0:10], ps[:, 1, 300:310]))
                link(dve.scalar_tensor_tensor(out=den[:, 0:5], in0=den[:, 0:5], scalar=-1.0, in1=den[:, 0:5],
                                              op0=ALU.mult, op1=ALU.max))
                eh = eC[:, :].rearrange("p (s h) -> p s h", h=LH)[:, :, h:h + 1]
                link(dve.tensor_tensor(den[:, 0:5].rearrange("p (s a) -> p s a", a=1),
                                       den[:, 0:5].rearrange("p (s a) -> p s a", a=1), eh, ALU.max))
                link(dve.reciprocal(den[:, 0:5], den[:, 0:5]))
                link(dve.tensor_tensor(den[:, 5:10], den[:, 5:10], den[:, 0:5], ALU.mult))
                link(dve.tensor_tensor(den[:, 5:10], den[:, 5:10], den[:, 0:5], ALU.mult))
                dve.tensor_scalar(den[:, 5:10], den[:, 5:10], 1.0 / DV, EPS, ALU.mult, ALU.add).then_inc(l_v, 1)
                dve.wait_ge(l_rs, h + 2)
                dve.tensor_tensor(den[:, 0:5], den[:, 0:5], den[:, 10:15], ALU.mult).then_inc(l_gc, 1)
                dve.wait_ge(l_gb, 2 * h + 2)
                link(dve.tensor_copy(r[:, :], flat(0, T)))
                for c in (0, 1):
                    gcol = gn[:, GCOL["head"] + 2 * h + c:GCOL["head"] + 2 * h + c + 1]
                    dve.wait_ge(l_sq, 3 * h + 3)
                    dve.scalar_tensor_tensor(out=RX[:, 0:TP], in0=ps[:, 6 + c, :], scalar=gcol, in1=r[:, 0:TP],
                                             op0=ALU.mult, op1=ALU.mult)
                    link(dve.scalar_tensor_tensor(out=RX[:, TP:T], in0=ps[:, 5, P + c * TS:P + (c + 1) * TS], scalar=gcol,
                                                  in1=r[:, TP:T], op0=ALU.mult, op1=ALU.mult))
                    dve.wait_ge(o_sig, 8)
                    link(dve.tensor_tensor(RX[:, :], RX[:, :], so[:, 2 * h + c, :], ALU.mult))
                    link(dve.tensor_copy(gTh[:, 2 * h + c, :], RX[:, :]))
                    dve.tensor_tensor(gTl[:, 2 * h + c, :], RX[:, :], gTh[:, 2 * h + c, :].bitcast(F32),
                                      ALU.subtract).then_inc(l_out, 1)
                    dve.wait_ge(l_out, 2 * h + c + 1)
                dve.wait_ge(l_C, 16 * (h + 1))
                link(dve.tensor_copy(Cb[:, :, DV:DV + 1], nT[:, :].rearrange("p (b h) -> p b h", h=LH)[:, :, h:h + 1]))
                for b in range(NB):
                    dve.wait_ge(l_cs, NB * h + b + 1)
                    dve.scalar_tensor_tensor(out=Cb[:, b, :], in0=Cb[:, b, :], scalar=Mb[:, T + TS + b:T + TS + b + 1],
                                             in1=ps[:, 3 + b % 2, 0:DV + 1], op0=ALU.mult, op1=ALU.add).then_inc(l_cn, 1)
                dve.wait_ge(l_cn, NB * (h + 1))
                link(dve.tensor_copy(nT[:, :].rearrange("p (b h) -> p b h", h=LH)[:, :, h:h + 1], Cb[:, :, DV:DV + 1]))
            dve.memset(den[:, 0:1], 0.0).then_inc(l_nt, 1)
            dve.wait_ge(l_nt, 2)
            dve.tensor_copy(nrow[0:LH, :], ps[0:LH, 0, 0:P]).then_inc(l_nc, 1)
            dve.tensor_copy(nst[:, :], ps[0:NB * LH, 0, P:2 * P]).then_inc(l_nc, 1)
            dve.wait_ge(l_cost, 16 * LH)
            dve.wait_ge(l_cst, 16 * LH)
            dve.wait_ge(stored, 16 * (2 * NTT + 4))
            added("mlstm_out", "ffb1")

        def mlstm_pes(pe, v, products, sums, broadcast, tiles, xgh, xgl):
            mm, tr = nc.tensor.matmul, nc.tensor.transpose
            pe.wait_ge(tile_taken, GT - 1)
            products(GP, 0, 8, xgh, xgl, slot(GT), waits=lambda n: pe.wait_ge(xg_ready, XG["mix1"] + n + 1))
            sums(8)
            tiles("mlstm_in", 8, 1, xgh, xgl, 6, 4, at0={4: broadcast})
            pe.wait_ge(g_dve, 3)
            pe.wait_ge(m_ready, 1)
            pe.wait_ge(tile_taken, IT + 24)
            for o, src in ((0, RA), (20, RD)):
                for j in range(NTT):
                    n = P if j < 4 else TS
                    tr(ps[0:n, 4, o + 4 * j:o + 4 * j + 4], src[0:LH, j * P:j * P + n], ident[0:LH, 0:LH])
            tr(ps[0:TS, 4, 40:44], RE[0:LH, 0:TS], ident[0:LH, 0:LH])
            for h in range(LH):
                mm(ps[:, 4, 44 + h:45 + h], cf[0:LH, C_SEL + h * P:C_SEL + (h + 1) * P], RB[0:LH, TP - 1:TP],
                   start=True, stop=True)
            pe.wait_ge(st_ready, 64)
            tr(ps[:, 4, 64:96], nst0[:, :], ident[0:NB * LH, 0:NB * LH]).then_inc(ct2, 1)
            for j in range(NTT):
                n = P if j < 4 else TS
                for q in range(3):
                    if j:
                        pe.wait_ge(kv_c, 3 * (j - 1) + q + 1)
                    for e in range(4):
                        src = kT[:, e, :] if q == 0 else vT[:, 4 * (q - 1) + e, :]
                        ins = tr(ps[0:n, 5 + q, e * P:(e + 1) * P], src[:, j * P:j * P + n], ident)
                    ins.then_inc(kv_t, 1)
            pe.wait_ge(kv_c, 3 * NTT)
            for h in range(LH):
                sel = cf[0:LH, C_SEL + h * P:C_SEL + (h + 1) * P]
                if h:
                    pe.wait_ge(l_out, 2 * h)
                mm(ps[:, 0, :], sel, RB[0:LH, 0:TP], start=True, stop=True)
                mm(ps[:, 1, 0:TS], sel, RB[0:LH, TP:T], start=True, stop=True)
                mm(ps[:, 1, TS:2 * TS + NB], sel, RE[0:LH, TS:2 * TS + NB], start=True, stop=True).then_inc(l_gb, 1)
                if h:
                    pe.wait_ge(l_cn, NB * h)
                for s in range(4):
                    bank, o = [(2, 0), (3, 0), (4, 0), (4, 256)][s]
                    mm(ps[:, bank, o:o + TP - s * P], kT[:, h, s * P:(s + 1) * P], qT[:, h, s * P:TP],
                       start=True, stop=True).then_inc(l_S, 1)
                mm(ps[0:TS, 5, 0:TS], kT[:, h, TP:T], qT[:, h, TP:T], start=True, stop=True).then_inc(l_S, 1)
                pe.wait_ge(l_SD, NTT * (h + 1))
                for c in (0, 1):
                    for s in range(4):
                        ins = mm(ps[:, 6 + c, s * P:TP], Vt[:, s, h, c * P:(c + 1) * P], SD[:, SO[s]:SO[s + 1]],
                                 start=s == 0, stop=s == 3)
                    ins.then_inc(l_num, 1)
                pe.wait_ge(l_qn, h + 1)
                pe.wait_ge(l_C, 16 * (h + 1))
                for c in (0, 1):
                    o = P + c * TS
                    mm(ps[:, 5, o:o + TS], Vt[0:TS, 4, h, c * P:(c + 1) * P], SD[0:TS, 1280:1280 + TS], start=True, stop=False)
                    for b in range(NB):
                        ins = mm(ps[:, 5, o + b * TB:o + (b + 1) * TB], Cb[:, b, c * P:(c + 1) * P],
                                 qd[:, b * TB:(b + 1) * TB], start=False, stop=b == NB - 1)
                ins.then_inc(l_num, 1)
                pe.wait_ge(l_mb, h + 1)
                for j in range(NTT):
                    for s in range(j + 1 if j < 4 else 0):
                        mm(ps[:, 1, 300 + j:301 + j], SD[:, SO[s] + (j - s) * P:SO[s] + (j - s + 1) * P], ones[:, 0:1],
                           start=s == 0, stop=s == j)
                mm(ps[:, 1, 304:305], SD[0:TS, 1280:1280 + P], ones[0:TS, 0:1], start=True, stop=False)
                mm(ps[:, 1, 304:305], qn[:, :], ones[:, 0:1], start=False, stop=True)
                pe.wait_ge(l_kw, h + 1)
                for s in range(4):
                    ins = mm(ps[:, 2, 0:DV + 1], kw[:, s, :], Vt[:, s, h, :], start=s == 0, stop=s == 3)
                ins.then_inc(l_cp, 1)
                pe.wait_ge(l_sq, 3 * (h + 1))
                for j in range(NTT):
                    for c in (0, 1):
                        ins = mm(ps[:, 1, 305 + j:306 + j], sqn[:, c, j * P:(j + 1) * P], ones[:, 0:1], start=c == 0, stop=c == 1)
                ins.then_inc(l_ss, 1)
                pe.wait_ge(l_gc, h + 1)
                for j in range(NTT):
                    w = P if j < 4 else TS
                    ins = mm(flat(0, T)[:, j * P:j * P + w], den[:, j:j + 1].to_broadcast([P, P]), ident[:, 0:w],
                             start=True, stop=True)
                ins.then_inc(l_gb, 1)
                pe.wait_ge(l_kwb, h + 1)
                for b in range(NB):
                    if b >= 2:
                        pe.wait_ge(l_cn, NB * h + b - 1)
                    mm(ps[:, 3 + b % 2, 0:DV + 1], kwb[0:TS, b, :], Vt[0:TS, 4, h, :], start=True, stop=True).then_inc(l_cs, 1)
            pe.wait_ge(l_nt, 1)
            pe.wait_ge(l_co, 2 * LH)
            tr(ps[0:LH, 0, 0:P], nP[:, :], ident)
            tr(ps[0:NB * LH, 0, P:2 * P], nT[:, :], ident).then_inc(l_nt, 1)
            pe.wait_ge(l_nc, 2)
            tiles("mlstm_out", 8, 1, lambda n: gTh[:, n, :], lambda n: gTl[:, n, :], 2, 4)


        mixer_loads, mixer_lowers = [mla_loads, mlstm_loads], [mla_lowers, mlstm_lowers]
        mixer_acts, mixer_dves, mixer_pes = [mla_acts, mlstm_acts], [mla_dves, mlstm_dves], [mla_pes, mlstm_pes]

        block = ctx.enter_context(nc.Block())
        @block.sync
        def _(sp):
            def load(p, dyn, parts, free=True):
                s = p % RAW
                if free:
                    sp.wait_ge(wlo_ready, p - RAW - 7 + dyn)
                for dst, src, inc in parts(raw[:, s, :, :]):
                    sp.dma_start(dst, src).then_inc(raw_ready[s], inc)

            def ffn_in(name, w):
                v = w.rearrange("(c p) n -> p c n", p=P)
                p0 = P0[name]

                def pair(i, k, dyn, free=True):
                    for half_ in (0, 1):
                        col = half_ * FF + (i * 2 + k) * P
                        load(p0 + 2 * k + half_, dyn, lambda d: [(d, v[:, :, bass.ds(col, P)], UNIT)], free)
                if p0 == 8:
                    pair(0, 0, 0, False)
                    sp.wait_ge(in_ready[1], 16 * NTT)
                    pair(0, 1, 0, False)
                with sp.Fori(1 if p0 == 8 else 0, NC_F // 2) as i:
                    for k in (0, 1):
                        pair(i, k, i * 4)

            def ffn_out(name, w):
                v = w.rearrange("(c p) n -> p c n", p=P)
                with sp.Fori(0, NC_D // 2) as i:
                    for k in (0, 1):
                        for q, (a, b) in enumerate(FF_PARTS):
                            load(P0[name] + 4 * k + q, i * 8,
                                 lambda d: [(d[:, 0:b - a, :], v[:, a:b, bass.ds((i * 2 + k) * P, P)], UNIT)])

            def square(name, w, n_chunks, n_tiles, first=0):
                v = w.rearrange("(c p) n -> p c n", p=P)
                with sp.Fori(0, n_tiles // 4) as i:
                    for k in range(4):
                        load(P0[name] + k, i * 4,
                             lambda d: [(d[:, 0:n_chunks, :], v[:, :, bass.ds((i * 4 + k) * P, P)], UNIT)])

            for l in (0, 1):
                ffn_in(f"ffa{l}_in", I["w_ffa_in"][l])
                ffn_out(f"ffa{l}_out", I["w_ffa_out"][l])
                mixer_loads[l](sp, load, square)
                ffn_in(f"ffb{l}_in", I["w_ffb_in"][l])
                ffn_out(f"ffb{l}_out", I["w_ffb_out"][l])
                square(f"gate{l}", I["w_ple_gate"][l], 8, 8)
                square(f"proj{l}", I["w_ple_proj"][l], 2, 8)
            for j in range(NTT):
                dst = outs["y_prompt"][0, j * P:(j + 1) * P, :] if j < 4 else \
                    outs["y_sample"].rearrange("b t d -> (b t) d")
                for q, y_row in enumerate((y_act, y_dve)):
                    sp.wait_ge(y_row, j + 1)
                    sp.dma_start(dst[:, q * 512:(q + 1) * 512],
                                 xin[0:(P if j < 4 else TS), j, q * 512:(q + 1) * 512]).then_inc(stored, 16)
            sp.wait_ge(stored, 16 * (2 * NTT + 4 + 2 * NTT))

        @block.gpsimd
        def _(pool):
            def lower(p, dyn, n):
                pool.wait_ge(whi_ready, p - 7 + dyn)
                pool.tensor_tensor(wlo[:, p % SPLIT, 0:n, :], raw[:, p % RAW, 0:n, :],
                                   whi[:, p % SPLIT, 0:n, :].bitcast(F32), ALU.subtract).then_inc(wlo_ready, 1)

            def stage(name, counts, iters):
                with pool.Fori(0, iters) as i:
                    for k, n in enumerate(counts):
                        lower(P0[name] + k, i * len(counts), n)

            sizes = [b - a for a, b in FF_PARTS]
            for l in (0, 1):
                stage(f"ffa{l}_in", [8] * 4, 11)
                stage(f"ffa{l}_out", sizes * 2, 4)
                mixer_lowers[l](pool, lower, stage)
                stage(f"ffb{l}_in", [8] * 4, 11)
                stage(f"ffb{l}_out", sizes * 2, 4)
                stage(f"gate{l}", [8] * 4, 2)
                stage(f"proj{l}", [2] * 4, 2)

        @block.scalar
        def _(act):
            xr = [I["x_prompt"][0, j * P:(j + 1) * P, :] for j in range(4)] + \
                [I["x_sample"].rearrange("b t d -> (b t) d")]
            act.dma_start(cf[:, 0:C_ROPE], I["cf"][:, 0:C_ROPE]).then_inc(id_ready, 16)
            act.dma_start(gn[:, :], I["gains"]).then_inc(id_ready, 16)
            for q in (0, 1):
                for j in range(NTT):
                    act.dma_start(xin[0:(P if j < 4 else TS), j, q * 512:(q + 1) * 512],
                                  xr[j][:, q * 512:(q + 1) * 512]).then_inc(in_ready[q], 16)
            act.dma_start(cf[:, C_ROPE:], I["cf"][:, C_ROPE:]).then_inc(consts_ready, 16)
            act.dma_start(cbf[:, :], I["cb"]).then_inc(consts_ready, 16)

            def upper(p, dyn, n):
                act.wait_ge(raw_ready[p % RAW], UNIT * (p // RAW - 1) + dyn * (UNIT // RAW))
                act.wait_ge(panel_used, p - 1 + dyn)
                act.activation(whi[:, p % SPLIT, 0:n, :], raw[:, p % RAW, 0:n, :], ACT.Copy).then_inc(whi_ready, 1)

            def root(n, width):
                act.wait_ge(ss_ready, n + 1)
                act.activation(sd[:, 0:NTT], ps[:, 5, 100:100 + NTT], ACT.Sqrt, bias=eps[:, 0:1],
                               scale=1.0 / width).then_inc(sd_ready, 1)

            def ffn_in(name, norm):
                p0, t0 = P0[name], T0[name]

                def pair(k, dyn, first):
                    upper(p0 + 2 * k + 1, dyn, 8)
                    if first:
                        root(norm, D)
                    upper(p0 + 2 * k + 2, dyn, 8)
                    act.wait_ge(tile_taken, t0 + 2 * k + 1 + dyn)
                    act.activation(sA[:, :], tA[:, :], ACT.Silu).then_inc(silu_done, 1)
                pair(0, 0, True)
                pair(1, 0, False)
                with act.Fori(1, NC_F // 2) as i:
                    for k in (0, 1):
                        pair(k, i * 4, False)

            def ffn_out(name):
                sizes = [b - a for a, b in FF_PARTS]
                nxt = (sizes * 2)[1:] + [8]
                with act.Fori(0, NC_D // 2) as i:
                    for k in range(8):
                        upper(P0[name] + 1 + k, i * 8, nxt[k])

            def square(name, n):
                with act.Fori(0, 2) as i:
                    for k in range(4):
                        upper(P0[name] + 1 + k, i * 4, n if k < 3 else 8)

            act.wait_ge(zeroed, 2)
            for c in range(NC_D):
                act.wait_ge(x_turned, c + 1)
                act.activation(x[:, c, :], flat(4 + 2 * (c % 2), T), ACT.Copy).then_inc(x_taken, 1)
                act.wait_ge(x_taken, c + 1)
                if c >= 2:
                    act.wait_ge(acc_done, c - 1)
                act.activation((tA, sA)[c % 2][:, :], x[:, c, :], ACT.Square).then_inc(x_sq, 1)
                if c == 0:
                    upper(8, 0, 8)
            norm = 0
            for l in (0, 1):
                ffn_in(f"ffa{l}_in", norm); norm += 1
                ffn_out(f"ffa{l}_out")
                norm = mixer_acts[l](act, upper, root, square, norm)
                ffn_in(f"ffb{l}_in", norm); norm += 1
                ffn_out(f"ffb{l}_out")
                act.wait_ge(panel_used, P0[f"gate{l}"])
                pr = [I["p_prompt"][l, 0, j * P:(j + 1) * P, :] for j in range(4)] + \
                    [I["p_sample"][l].rearrange("b t d -> (b t) d")]
                for j in range(NTT):
                    act.dma_start(pn[0:(P if j < 4 else TS), j, :], pr[j]).then_inc(p_ready, 16)
                for c in range(NC_D):
                    upper(P0[f"gate{l}"] + 1 + c, 0, 8)
                    if c == 0:
                        root(norm, D); norm += 1
                    act.wait_ge(tile_taken, T0[f"gate{l}"] + c + 1)
                    act.activation(sg[:, c, :], sg[:, c, :], ACT.Sigmoid).then_inc(sg_ready, 1)
                square(f"proj{l}", 2) if l == 0 else None
                if l == 1:
                    for k in range(7):
                        upper(P0["proj1"] + 1 + k, 0, 2)
            root(norm, D)
            act.wait_ge(rc_ready, norm + 1)
            for j in range(NTT):
                n = P if j < 4 else TS
                act.wait_ge(yt_ready, j + 1 if j < 4 else 9)
                act.activation(xin[0:n, j, 0:512], ps[0:n, 2 * j % 8, :], ACT.Copy, scale=rc[0:n, j:j + 1]).then_inc(y_act, 1)

        @block.vector
        def _(dve):
            v = {"chain": 0, "norm": 0, "dyn": 0}

            def link(ins):
                v["chain"] += 1
                ins.then_inc(chain, 1)
                dve.wait_ge(chain, v["chain"] + v["dyn"])

            def rms(width, out=r):
                n = v["norm"]; v["norm"] += 1
                dve.wait_ge(sd_ready, n + 1)
                dve.reciprocal(rc[:, 0:NTT], sd[:, 0:NTT]).then_inc(rc_ready, 1)
                dve.wait_ge(rb_ready, n + 1)
                link(dve.tensor_copy(out[:, :], flat(4, T)))

            def after_x(xc, c, name, dyn, k, cdyn, cl, has_xg=True):
                g = gn[:, bass.ds(c + GCOL[name], 1)]
                xf = x[:, bass.ds(c, 1), :].rearrange("p a t -> p (a t)")
                if has_xg:
                    hc = xh[:, bass.ds(c, 1), :].rearrange("p a t -> p (a t)")
                    lc = xl[:, bass.ds(c, 1), :].rearrange("p a t -> p (a t)")
                    dve.tensor_scalar(hc, xf, g, None, ALU.mult).then_inc(chain, 1)
                else:
                    yc = yT[:, bass.ds(c, 1), :].rearrange("p a t -> p (a t)")
                    dve.tensor_scalar(yc, xf, g, None, ALU.mult).then_inc(y_ready, 1)
                dve.tensor_tensor(sq[:, :], xf, xf, ALU.mult).then_inc(chain, 1)
                if has_xg:
                    dve.wait_ge(chain, cl + 1 + cdyn)
                    dve.scalar_tensor_tensor(out=lc, in0=xf, scalar=g, in1=hc.bitcast(F32),
                                             op0=ALU.mult, op1=ALU.subtract).then_inc(xg_ready, 1)
                dve.wait_ge(chain, cl + 2 + cdyn)
                dve.wait_ge(acc_done, AC[name] + k + dyn)
                dve.tensor_tensor(acc[:, 0:T], acc[:, 0:T], sq[:, :], ALU.add).then_inc(acc_done, 1)

            def clear_acc():
                link(dve.memset(acc[:, 0:T], 0.0))

            def chunks(t0, name, tiles_ready, update, links, has_xg=True, fixed=None):
                clear_acc()
                if XG[name] == 0:
                    raise AssertionError
                c0 = v["chain"]
                with dve.Fori(0, NC_D // 2) as i:
                    for k in (0, 1):
                        c = i * 2 + k
                        tiles_ready(i, k)
                        xf = x[:, bass.ds(c, 1), :].rearrange("p a t -> p (a t)")
                        update(i, k, c, xf, t0 + k, c0 + k * links + 0, i * (2 * links))
                        dve.wait_ge(tile_taken, t0 + k + 1 + i * 2)
                        after_x(xf, c, name, i * 2, k, i * (2 * links), c0 + k * links + links - 2, has_xg)
                v["chain"] += 8 * links

            def ffn_in(name, ubase):
                p0, t0 = P0[name], T0[name]
                c0 = v["chain"]
                with dve.Fori(0, NC_F // 2) as i:
                    for k in (0, 1):
                        pa, ta, j, cl = p0 + 2 * k, t0 + 2 * k, i * 2 + k, c0 + 2 * k
                        dve.wait_ge(panel_used, pa + 1 + i * 4)
                        dve.tensor_tensor(half(tA[:, :]), slot(ta), half(r[:, :]), ALU.mult).then_inc(tile_taken, 1)
                        dve.wait_ge(silu_done, ubase + k + 1 + i * 2)
                        dve.tensor_tensor(sA[:, :], sA[:, :], r[:, :], ALU.mult).then_inc(chain, 1)
                        dve.wait_ge(panel_used, pa + 2 + i * 4)
                        dve.wait_ge(chain, cl + 1 + i * 4)
                        dve.tensor_tensor(half(ub[:, :]), slot(ta + 1), half(sA[:, :]), ALU.mult).then_inc(tile_taken, 1)
                        dve.wait_ge(tile_taken, ta + 2 + i * 4)
                        hj = uh[:, bass.ds(j, 1), :].rearrange("p a t -> p (a t)")
                        lj = ul[:, bass.ds(j, 1), :].rearrange("p a t -> p (a t)")
                        dve.tensor_copy(hj, ub[:, :]).then_inc(chain, 1)
                        dve.wait_ge(chain, cl + 2 + i * 4)
                        dve.tensor_tensor(lj, ub[:, :], hj.bitcast(F32), ALU.subtract).then_inc(u_ready, 1)
                v["chain"] += NC_F * 2

            def ffn_out(name, nxt):
                def ready(i, k):
                    dve.wait_ge(panel_used, P0[name] + 4 * (k + 1) + i * 8)

                def update(i, k, c, xf, t, cl, cdyn):
                    dve.scalar_tensor_tensor(out=half(xf), in0=slot(t), scalar=0.5, in1=half(xf),
                                             op0=ALU.mult, op1=ALU.add).then_inc(tile_taken, 1)
                chunks(T0[name], nxt, ready, update, 2)

            def added(name, nxt):
                def ready(i, k):
                    dve.wait_ge(panel_used, P0[name] + k + 1 + i * 2)

                def update(i, k, c, xf, t, cl, cdyn):
                    dve.tensor_tensor(half(xf), slot(t), half(xf), ALU.add).then_inc(tile_taken, 1)
                chunks(T0[name], nxt, ready, update, 2)

            def ple(l, nxt):
                g0, t0 = P0[f"gate{l}"], T0[f"gate{l}"]
                with dve.Fori(0, 4) as i:
                    for k in (0, 1):
                        dve.wait_ge(panel_used, g0 + k + 1 + i * 2)
                        gc = sg[:, bass.ds(i * 2 + k, 1), :].rearrange("p a t -> p (a t)")
                        dve.tensor_tensor(half(gc), slot(t0 + k), half(r[:, :]), ALU.mult).then_inc(tile_taken, 1)
                t1 = T0[f"pe{l}"]
                for c in (0, 1):
                    dve.wait_ge(pt_ready, 2 * l + c + 1)
                    b = 2 * ((t1 + c) % 2)
                    link(dve.tensor_copy(pth[:, c, :], flat(b, T)))
                    dve.tensor_tensor(ptl[:, c, :], flat(b, T), pth[:, c, :].bitcast(F32),
                                      ALU.subtract).then_inc(tile_taken, 1)

                def ready(i, k):
                    dve.wait_ge(panel_used, P0[f"proj{l}"] + k + 1 + i * 2)
                    dve.wait_ge(sg_ready, 8 * l + 8)

                def update(i, k, c, xf, t, cl, cdyn):
                    gc = sg[:, bass.ds(c, 1), :].rearrange("p a t -> p (a t)")
                    dve.tensor_tensor(half(ub[:, :]), slot(t), half(gc), ALU.mult).then_inc(chain, 1)
                    dve.wait_ge(chain, cl + 1 + cdyn)
                    dve.tensor_tensor(xf, ub[:, :], xf, ALU.add).then_inc(tile_taken, 1)
                chunks(T0[f"proj{l}"], nxt, ready, update, 3 if l == 0 else 2, has_xg=(l == 0))

            dve.memset(eps[:, :], EPS).then_inc(zeroed, 1)
            dve.memset(acc[:, :], 0.0).then_inc(zeroed, 1)
            dve.wait_ge(zeroed, 2)
            dve.wait_ge(id_ready, 32)
            for c in range(NC_D):
                dve.wait_ge(x_taken, c + 1)
                g = gn[:, c:c + 1]
                dve.tensor_scalar(xh[:, c, :], x[:, c, :], g, None, ALU.mult).then_inc(tile_taken, 1)
                dve.wait_ge(tile_taken, c + 1)
                dve.scalar_tensor_tensor(out=xl[:, c, :], in0=x[:, c, :], scalar=g, in1=xh[:, c, :].bitcast(F32),
                                         op0=ALU.mult, op1=ALU.subtract).then_inc(xg_ready, 1)
                dve.wait_ge(x_sq, c + 1)
                if c:
                    dve.wait_ge(acc_done, c)
                dve.tensor_tensor(acc[:, 0:T], acc[:, 0:T], (tA, sA)[c % 2][:, :], ALU.add).then_inc(acc_done, 1)
            dve.wait_ge(consts_ready, 32)
            link(dve.tensor_copy(cb[:, :], cbf[:, :]))
            for l in (0, 1):
                rms(D)
                ffn_in(f"ffa{l}_in", 44 * l)
                ffn_out(f"ffa{l}_out", f"mix{l}")
                mixer_dves[l](dve, v, link, rms, added)
                rms(D)
                ffn_in(f"ffb{l}_in", 44 * l + 22)
                ffn_out(f"ffb{l}_out", f"ple{l}")
                rms(D)
                ple(l, "ffa1" if l == 0 else "final")
            dve.wait_ge(sd_ready, v["norm"] + 1)
            dve.reciprocal(rc[:, 0:NTT], sd[:, 0:NTT]).then_inc(rc_ready, 1)
            dve.wait_ge(rc_ready, v["norm"] + 1)
            for j in range(NTT):
                n = P if j < 4 else TS
                dve.wait_ge(yt_ready, j + 5 if j < 4 else 10)
                dve.tensor_scalar(xin[0:n, j, 512:1024], ps[0:n, (2 * j + 1) % 8, :], rc[0:n, j:j + 1], None,
                                  ALU.mult).then_inc(y_dve, 1)

        @block.tensor
        def _(pe):
            mm = nc.tensor.matmul
            v = {"norm": 0, "acc": 0}

            def products(p, dyn, n_chunks, mh, ml, out, first=True, last=True, waits=None, at=None):
                s = p % SPLIT
                pe.wait_ge(whi_ready, p - 7 + dyn)
                pe.wait_ge(wlo_ready, p - 7 + dyn)
                for n in range(n_chunks):
                    if at and n in at:
                        at[n]()
                    if waits:
                        waits(n)
                    h0, l0 = half(mh(n)), half(ml(n))
                    for q in (0, 1):
                        mm(out[:, q, :], whi[:, s, n, :], h0[:, q, :], start=first and n == 0, stop=False)
                    for q in (0, 1):
                        mm(out[:, q, :], whi[:, s, n, :], l0[:, q, :], start=False, stop=False)
                    end = last and n == n_chunks - 1
                    for q in (0, 1):
                        ins = mm(out[:, q, :], wlo[:, s, n, :], h0[:, q, :], start=False, stop=end)
                ins.then_inc(panel_used, 1)

            def sums(n_acc):
                v["acc"] += n_acc
                pe.wait_ge(acc_done, v["acc"])
                for j in range(NTT):
                    ins = mm(ps[:, 5, 100 + j:101 + j], acc[:, j * P:(j + 1) * P], ones[:, 0:1], start=True, stop=True)
                ins.then_inc(ss_ready, 1)

            def broadcast():
                n = v["norm"]; v["norm"] += 1
                pe.wait_ge(rc_ready, n + 1)
                for j in range(NTT):
                    w = P if j < 4 else TS
                    ins = mm(flat(4, T)[:, j * P:j * P + w], rc[:, j:j + 1].to_broadcast([P, P]), ident[:, 0:w],
                             start=True, stop=True)
                ins.then_inc(rb_ready, 1)

            def tiles(name, n_chunks, per_tile, mh, ml, iters, per, xg0=None, at0=None):
                def tile(k, dyn, waits=None, at=None):
                    if waits is not turned:
                        pe.wait_ge(tile_taken, T0[name] + k - 1 + dyn)
                    products(P0[name] + k, dyn, n_chunks, mh, ml, slot(T0[name] + k), waits=waits, at=at)
                if xg0 is not None:
                    tile(0, 0, turned if xg0 == 0 else lambda n: pe.wait_ge(xg_ready, xg0 + n + 1))
                    sums(8)
                    tile(1, 0, at={4: broadcast})
                    for k in range(2, per):
                        tile(k, 0)
                elif at0:
                    for k in range(per):
                        tile(k, 0, at=at0 if k == 0 else None)
                with pe.Fori(0 if xg0 is None and at0 is None else 1, iters) as i:
                    for k in range(per):
                        tile(k, i * per)

            def ffn_out(name, ubase):
                with pe.Fori(0, NC_D // 2) as i:
                    for k in (0, 1):
                        pe.wait_ge(tile_taken, T0[name] + k - 1 + i * 2)
                        for q, (a, b) in enumerate(FF_PARTS):
                            products(P0[name] + 4 * k + q, i * 8, b - a, lambda n: uh[:, a + n, :],
                                     lambda n: ul[:, a + n, :], slot(T0[name] + k), q == 0, q == 3,
                                     (lambda n: pe.wait_ge(u_ready, ubase + a + n + 1)) if k == 0 else None)

            xgh, xgl = (lambda n: xh[:, n, :]), (lambda n: xl[:, n, :])
            pe.wait_ge(id_ready, 32)

            def turn(c):
                pe.wait_ge(in_ready[c // 4], 16 * NTT)
                if c >= 2:
                    pe.wait_ge(x_taken, c - 1)
                for j in range(NTT):
                    n = P if j < 4 else TS
                    ins = nc.tensor.transpose(flat(4 + 2 * (c % 2), T)[:, j * P:j * P + n],
                                              xin[0:n, j, c * P:(c + 1) * P], ident[0:n, 0:n])
                    if c == 0 and j == 0:
                        ins.then_inc(panel_used, NC_D)
                ins.then_inc(x_turned, 1)

            def turned(n):
                if n + 2 < NC_D:
                    turn(n + 2)
                pe.wait_ge(xg_ready, n + 1)
            turn(0)
            turn(1)
            for l in (0, 1):
                tiles(f"ffa{l}_in", 8, 1, xgh, xgl, 11, 4, XG[f"ffa{l}"])
                ffn_out(f"ffa{l}_out", 44 * l)
                mixer_pes[l](pe, v, products, sums, broadcast, tiles, xgh, xgl)
                tiles(f"ffb{l}_in", 8, 1, xgh, xgl, 11, 4, XG[f"ffb{l}"])
                ffn_out(f"ffb{l}_out", 44 * l + 22)
                tiles(f"gate{l}", 8, 1, xgh, xgl, 2, 4, XG[f"ple{l}"])
                pe.wait_ge(p_ready, 16 * NTT * (l + 1))
                for c in (0, 1):
                    t = T0[f"pe{l}"] + c
                    pe.wait_ge(tile_taken, t - 1)
                    for j in range(NTT):
                        n = P if j < 4 else TS
                        ins = nc.tensor.transpose(flat(2 * (t % 2), T)[:, j * P:j * P + n],
                                                  pn[0:n, j, c * P:(c + 1) * P], ident[0:n, 0:n])
                    ins.then_inc(pt_ready, 1)
                pe.wait_ge(tile_taken, T0[f"pe{l}"] + 2)
                tiles(f"proj{l}", 2, 1, lambda n: pth[:, n, :], lambda n: ptl[:, n, :], 2, 4)
            pe.wait_ge(tile_taken, T0["proj1"] + 8)
            for q, j in [(0, j) for j in range(4)] + [(1, j) for j in range(4)] + [(0, 4), (1, 4)]:
                n, b = P if j < 4 else TS, (2 * j + q) % 8
                if j == 0:
                    pe.wait_ge(y_ready, 4 * q + 4)
                    if q:
                        sums(8)
                if b == 5:
                    pe.wait_ge(sd_ready, v["norm"] + 1)
                if j == 4:
                    pe.wait_ge((y_act, y_dve)[q], 1)
                for c in range(4):
                    ins = nc.tensor.transpose(ps[0:n, b, c * P:(c + 1) * P], yT[:, 4 * q + c, j * P:j * P + n], ident)
                ins.then_inc(yt_ready, 1)


_INS = ['x_prompt', 'x_sample', 'cache_ckv', 'cache_krope', 'state_C', 'state_n', 'state_m', 'page_table',
        'p_prompt', 'p_sample', 'w_ffa_in', 'w_ffa_out', 'w_ffb_in', 'w_ffb_out', 'w_ple_gate', 'w_ple_proj',
        'w_mla_in', 'w_uq', 'w_uk', 'w_uv', 'w_mla_out', 'w_mlstm_in', 'b_igate', 'b_fgate', 'w_mlstm_out']
_OUTS = [("y_prompt", (1, 512, 1024)), ("y_sample", (8, 8, 1024)), ("ckv_prompt", (1, 1, 512, 256)),
         ("kr_prompt", (1, 1, 512, 32)), ("ckv_sample", (1, 8, 8, 256)), ("kr_sample", (1, 8, 8, 32)),
         ("C_prompt", (1, 1, 4, 128, 256)), ("n_prompt", (1, 1, 4, 128)), ("m_prompt", (1, 1, 4)),
         ("C_sample", (1, 8, 4, 128, 256)), ("n_sample", (1, 8, 4, 128)), ("m_sample", (1, 8, 4))]
_PAST = 2048


def constants():
    cf = np.zeros((P, NCF), np.float32)
    cf[:, C_ID:C_ID + P] = np.eye(P)
    cf[:, C_ONE:C_ONE + 8] = 1.0
    half = ROPE // 2
    inv = (np.float32(10000.0) ** (-np.arange(half, dtype=np.float32) / np.float32(half))).astype(np.float32)
    pos = np.concatenate([np.arange(TP), np.tile(_PAST + np.arange(TB), NB)]).astype(np.float32)
    ang = inv[:, None] * pos[None, :]
    cos, sin = np.cos(ang.astype(np.float64)), np.sin(ang.astype(np.float64))
    cf[64:80, C_ROPE:C_ROPE + T] = cos
    cf[80:96, C_ROPE:C_ROPE + T] = cos
    cf[96:112, C_ROPE:C_ROPE + T] = -sin
    cf[112:128, C_ROPE:C_ROPE + T] = sin
    s = np.arange(TS)
    cf[0:TS, C_BLK:C_BLK + NB] = (s[:, None] // TB == np.arange(NB)[None, :])
    for h in range(LH):
        cf[h, C_SEL + h * P:C_SEL + (h + 1) * P] = 1.0
    k = np.arange(P)
    cf[:, C_TRI:C_TRI + P] = np.where(k[:, None] <= k[None, :], 0.0, -NEG)
    ok = (s[:, None] // TB == s[None, :] // TB) & (s[:, None] <= s[None, :])
    cf[0:TS, C_STRI:C_STRI + TS] = np.where(ok, 0.0, -NEG)
    cb = np.zeros((P, NCB), np.float32)
    cb[:, B_ID:B_ID + P] = np.eye(P)
    cb[:, B_CAUSAL:B_CAUSAL + P] = np.where(k[None, :] <= k[:, None], 0.0, NEG)
    t = np.arange(P) // NH
    for b in range(NB):
        ok = (s[None, :] // TB == b) & (s[None, :] % TB <= t[:, None])
        cb[:, B_SAMPLE + b * TS:B_SAMPLE + (b + 1) * TS] = np.where(ok, 0.0, NEG)
    return cf, cb


def layout(inputs):
    a = {n: np.ascontiguousarray(inputs[n]) for n in _INS}
    g = np.asarray
    rows = [g(inputs["g_ffa"])[0], g(inputs["g_mix"])[0], g(inputs["g_ffb"])[0], g(inputs["g_ple"])[0],
            g(inputs["g_ffa"])[1], g(inputs["g_mix"])[1], g(inputs["g_ffb"])[1], g(inputs["g_ple"])[1],
            g(inputs["g_final"]), g(inputs["g_mlstm_head"])[0], g(inputs["g_q_lat"])[0], g(inputs["g_kv_lat"])[0]]
    a["gains"] = np.ascontiguousarray(np.concatenate([r.reshape(-1, P) for r in rows]).T)
    a["cf"], a["cb"] = constants()
    return a


def kernel(**inputs):
    import concourse.bacc as _bacc
    from concourse.bass_utils import run_bass_kernel_spmd as _run

    nc = _bacc.Bacc("TRN2", target_bir_lowering=False, num_devices=1)
    arrays, ins, outs = {}, {}, {}
    for name, a in layout(inputs).items():
        arrays[f"in_{name}"] = a
        ins[name] = nc.dram_tensor(f"in_{name}", a.shape, mybir.dt.from_np(a.dtype), kind="ExternalInput").ap()
    for name, shape in _OUTS:
        outs[name] = nc.dram_tensor(f"out_{name}", shape, F32, kind="ExternalOutput").ap()
    hybrid_step(nc, ins, outs)
    got = _run(nc, [arrays], core_ids=[0]).results[0]
    return tuple(got[f"out_{n}"] for n, _ in _OUTS)
```

```python
from contextlib import ExitStack

import numpy as np

import concourse.bass as bass
from concourse import mybir

ACT = mybir.ActivationFunctionType
ALU = mybir.AluOpType
AX = mybir.AxisListType
F32 = mybir.dt.float32
F32R = mybir.dt.float32r
BF16 = mybir.dt.bfloat16

P = 128
D = 1024
NC_D = D // P
FF = 2816
NC_F = FF // P
TP, TS = 512, 64
T = TP + TS
H = T // 2
NB, TB = 8, 8
NTT = 5
EPS = 1e-6
NH, NOPE, ROPE, VD = 16, 64, 32, 64
QR, KR = 384, 256
PAGE, NPG = 128, 16
SCALE = (NOPE + ROPE) ** -0.5
LH, DK, DV = 4, 128, 256
CAP = 15.0
PD = 256
UNIT = 112
RAW, SPLIT = 4, 2
NEG = -1e30
FF_PARTS = [(0, 6), (6, 12), (12, 17), (17, 22)]

GAINS = ["ffa0", "mix0", "ffb0", "ple0", "ffa1", "mix1", "ffb1", "ple1", "final", "head"]
GCOL = {n: i * NC_D for i, n in enumerate(GAINS)}
GCOL["q"], GCOL["kv"] = 80, 83
NG = 85
C_ID, C_ONE, C_ROPE, C_BLK, C_SEL, C_TRI, C_STRI = 0, 128, 136, 712, 720, 1232, 1360
NCF = 1424
B_ID, B_CAUSAL, B_SAMPLE = 0, 128, 256
NCB = 768

STAGES = [("embed", 8, 8)]
for _l in (0, 1):
    STAGES += [(f"ffa{_l}_in", 44, 44), (f"ffa{_l}_out", 32, 8)]
    STAGES += [("mla_in", 6, 6), ("mla_heads", 16, 0), ("mla_out", 8, 8)] if _l == 0 else \
        [("mlstm_gates", 1, 1), ("mlstm_in", 24, 24), ("mlstm_out", 8, 8)]
    STAGES += [(f"ffb{_l}_in", 44, 44), (f"ffb{_l}_out", 32, 8), (f"ple{_l}", 16, 18)]
P0, T0 = {}, {}
_p = _t = 0
for _n, _a, _b in STAGES:
    P0[_n], T0[_n] = _p, _t
    _p, _t = _p + _a, _t + _b
NPANEL = _p


class Region:

    def __init__(self, nc, start, end):
        self.nc, self.start, self.at, self.end = nc, start, start, end

    def put(self, name, shape, dt=F32):
        size = int(np.prod(shape[1:])) * (2 if dt == BF16 else 4)
        t = self.nc.alloc_sbuf_tensor_at(name, shape, dt, offset=self.at)
        self.at += (size + 31) // 32 * 32
        assert self.at <= self.end, (name, self.at, self.end)
        return t


def hybrid_step(nc, ins, outs):
    I = ins
    with ExitStack() as ctx:
        def sem(name):
            return ctx.enter_context(nc.semaphore(name))

        base = (nc.sbuf_base + 31) // 32 * 32
        whole = Region(nc, base, nc.sbuf_top)
        x = whole.put("x", [P, NC_D, T])
        raw = whole.put("raw", [P, RAW, 8, P])
        whi = whole.put("whi", [P, SPLIT, 8, P], F32R)
        wlo = whole.put("wlo", [P, SPLIT, 8, P], F32R)
        acc = whole.put("acc", [P, NTT * P])
        r = whole.put("r", [P, T])
        gn = whole.put("gn", [P, NG])
        cf = whole.put("cf", [P, NCF])
        cb = whole.put("cb", [P, NCB], BF16)
        sd = whole.put("sd", [P, 8])
        rc = whole.put("rc", [P, 8])
        eps = whole.put("eps", [P, 1])
        ptab0 = nc.alloc_sbuf_tensor_at("ptab", [P, NB * NPG], mybir.dt.int32, offset=whole.at)
        whole.at += 4 * NB * NPG
        whole_m0 = whole.put("m0", [P, NB])
        ident, ones, rope = cf[:, C_ID:C_ID + P], cf[:, C_ONE:C_ONE + 8], cf[:, C_ROPE:C_ROPE + T]
        idb = cb[:, B_ID:B_ID + P]
        X0 = whole.at
        xh = whole.put("xh", [P, NC_D, T], F32R)
        xl = whole.put("xl", [P, NC_D, T], F32R)
        X1 = whole.at
        uh = whole.put("uh", [P, NC_F, T], F32R)
        ul = whole.put("ul", [P, NC_F, T], F32R)
        TMP = whole.at
        tmp = Region(nc, TMP, whole.end)
        tA = tmp.put("tA", [P, T])
        sA = tmp.put("sA", [P, T])
        ub = tmp.put("ub", [P, T])
        sq = tmp.put("sq", [P, T])
        cbf = Region(nc, TMP + 4 * 2 * T, whole.end).put("cbf", [P, NCB])
        pg = Region(nc, X1, TMP)
        sg = pg.put("sg", [P, NC_D, T])
        pn = pg.put("pn", [P, NTT, PD])
        pth = pg.put("pth", [P, 2, T], F32R)
        ptl = pg.put("ptl", [P, 2, T], F32R)
        jhi = pg.put("jhi", [P, SPLIT, 2, P], F32R)
        jlo = pg.put("jlo", [P, SPLIT, 2, P], F32R)
        xin = pg.put("xin", [P, NTT, D])
        yT = pg.put("yT", [P, NC_D, T])
        ps = nc.psum_tensor("ps", [P, 8, 512], F32)
        ps = ctx.enter_context(ps)
        flat = lambda b, n: ps[:, b:b + (n + 511) // 512, :].rearrange("p b n -> p (b n)")[:, 0:n]

        def ple_split(l, c, proj):
            s = c % SPLIT if proj else (P0[f"ple{l}"] + c) % SPLIT
            return (jhi[:, s, :, :], jlo[:, s, :, :]) if proj else (whi[:, s, :, :], wlo[:, s, :, :])

        def half(t):
            return t.rearrange("p (h n) -> p h n", h=2)

        def slot(t):
            return ps[:, 2 * (t % 2):2 * (t % 2) + 2, 0:H]

        raw_ready = [sem(f"raw_ready{s}") for s in range(RAW)]
        whi_ready, wlo_ready = sem("whi_ready"), sem("wlo_ready")
        panel_used = sem("panel_used")
        tile_taken = sem("tile_taken")
        silu_done, u_ready = sem("silu_done"), sem("u_ready")
        xg_ready, acc_done = sem("xg_ready"), sem("acc_done")
        ss_ready, sd_ready, rc_ready, rb_ready = sem("ss_ready"), sem("sd_ready"), sem("rc_ready"), sem("rb_ready")
        in_ready, consts_ready, zeroed = [sem("in_ready0"), sem("in_ready1")], sem("consts_ready"), sem("zeroed")
        chain = sem("dve_chain")
        p_ready, pt_ready, pt_done, sg_ready = sem("p_ready"), sem("pt_ready"), sem("pt_done"), sem("sg_ready")
        y_ready, yt_ready, y_act, y_dve, stored = sem("y_ready"), sem("yt_ready"), sem("y_act"), sem("y_dve"), sem("stored")
        xh_act, gn_ready = sem("xh_act"), sem("gn_ready")
        id_ready, x_turned, x_taken, x_sq = sem("id_ready"), sem("x_turned"), sem("x_taken"), sem("x_sq")

        NORMS = ["ffa0", "mix0", "ffb0", "ple0", "ffa1", "mix1", "ffb1", "ple1", "final"]
        XG = {n: 8 * i for i, n in enumerate(NORMS)}
        AC = {n: 8 * i + (5 if i > 1 else 0) for i, n in enumerate(NORMS)}
        AC["q"] = 16
        whole_ptab = ptab0
        mu = Region(nc, X1, TMP)
        oTh = mu.put("oTh", [P, NC_D, T], F32R)
        oTl = mu.put("oTl", [P, NC_D, T], F32R)
        ckv = mu.put("ckv", [P, 2, T])
        krT = mu.put("krT", [P, T])
        QA = mu.put("QA", [P, 3, NB * TB * NH])
        wuv = mu.put("wuv", [P, 2, NH * VD])
        mu1 = Region(nc, mu.at, TMP)
        zc = mu1.put("zc", [P, 6, T])
        cqh = mu1.put("cqh", [P, 3, T], F32R)
        cql = mu1.put("cql", [P, 3, T], F32R)
        Q = mu1.put("Q", [P, 2, T])
        mu2 = Region(nc, X0, X1)
        KEYS = NPG * PAGE + TS
        S = mu2.put("S", [P, 2, KEYS + P - TS])
        KT = mu2.put("KT", [P, 2, 3, 512])
        QAb = mu2.put("QAb", [P, 2, 3, P])
        mx = mu2.put("mx", [P, 2, 8])
        mxx = Region(nc, X0, X1)
        PP = mxx.put("PP", [P, 2, 1280])
        PT = mxx.put("PT", [P, 2, 1280])
        Vp = mxx.put("Vp", [P, 4, P])
        Kp = mxx.put("Kp", [P, 2, TP])
        WT = mxx.put("WT", [P, 2, KR])
        st = mxx.put("st", [P, 2, 12])
        qtmp = mxx.put("qtmp", [P, T])
        pages = Region(nc, mu.at, TMP).put("pages", [P, 2 * NPG, KR + ROPE])
        mt = Region(nc, TMP, whole.end)
        ckt = mt.put("ckt", [P, NTT, KR + ROPE])
        PTs = mt.put("PTs", [P, 2, 512])
        krS = mt.put("krS", [P, TS])
        ptab = whole_ptab
        rl, gql = sA, ub
        QT = [0, P, 3 * P, 6 * P]
        KO = [0, 4 * P, 7 * P, 9 * P]

        cq_ready, ckv_ready, kr_ready = sem("cq_ready"), sem("ckv_ready"), sem("kr_ready")
        ct_ready, ct_taken, wuv_ready = sem("ct_ready"), sem("ct_taken"), sem("wuv_ready")
        kv_ready, k_taken, v_taken, wt_taken = sem("kv_ready"), sem("k_taken"), sem("v_taken"), sem("wt_taken")
        qn_taken, qr_taken = sem("qn_taken"), sem("qr_taken")
        sc_ready, nm_ready, ex_ready, pp_ready = sem("sc_ready"), sem("nm_ready"), sem("ex_ready"), sem("pp_ready")
        qa_ready, qa_taken = sem("qa_ready"), sem("qa_taken")
        tr_ready, tr_act, tr_dve = sem("tr_ready"), sem("tr_act"), sem("tr_dve")
        pv_ready, ov_hi, ov_lo = sem("pv_ready"), sem("ov_hi"), sem("ov_lo")
        pg = [sem(f"page_ready{n}") for n in range(8)]
        kt_ready, kt_act, kt_dve = sem("kt_ready"), sem("kt_act"), sem("kt_dve")
        ss_sc, mx_dve, s_act, qab_ready = sem("sample_scores"), sem("mx_dve"), sem("s_act"), sem("qab_ready")
        snm, sex, sp_ready = sem("snm"), sem("sex"), sem("sample_p")
        s_inv, sp_pool = sem("s_inv"), sem("sample_p_pool")
        pts_ready, pts_taken, spv = sem("pts_ready"), sem("pts_taken"), sem("sample_pv")
        o_act, o_dve = sem("o_act"), sem("o_dve")
        zq_ready, cqh_act = sem("zq_ready"), sem("cqh_act")
        sv_ready, sv_hi, sv_lo = sem("sv_ready"), sem("sv_hi"), sem("sv_lo")
        PM, PH, PO = P0["mla_in"], P0["mla_heads"], P0["mla_out"]

        def mla_loads(sp, load):
            w = I["w_mla_in"][0].rearrange("(c p) n -> p c n", p=P)
            sp.dma_start(ptab[0:1, :], I["page_table"].rearrange("(a b) n -> a (b n)", a=1)).then_inc(wuv_ready, 16)
            for m in range(5):
                load(PM + m, 0, lambda d: [(d, w[:, :, m * P:(m + 1) * P], UNIT)])
            last = w[:, :, QR + KR - 64:QR + KR + ROPE]
            load(PM + 5, 0, lambda d: [(d[:, :, 0:96], last, 48),
                                       (d[:, :, 96:112], w[:, :, QR + KR + 16:QR + KR + 32], 32),
                                       (d[:, :, 112:128], w[:, :, QR + KR:QR + KR + 16], 32)])
            uq = I["w_uq"][0].rearrange("(c p) h d -> p c (h d)", p=P)
            uk = I["w_uk"][0].rearrange("(c p) h d -> p c (h d)", p=P)

            def head(k, i, first=False):
                h = i * 4 + k
                e = NOPE + ROPE

                def parts(d):
                    out = [(d[:, 0:3, 0:e], uq[:, :, bass.ds(h * e, e)], 32),
                           (d[:, 0:3, 96:112], uq[:, :, bass.ds(h * e + 80, 16)], 16 if k % 2 == 0 else 32),
                           (d[:, 0:3, 112:128], uq[:, :, bass.ds(h * e + 64, 16)], 16 if k % 2 == 0 else 48)]
                    if k % 2 == 0:
                        out.append((d[:, 3:5, :], uk[:, :, bass.ds(h * NOPE, P)], 48))
                    return out
                if not first and k % 2 == 0:
                    sp.wait_ge(panel_used, PH + k - 2 + i * 4)
                load(PH + k, i * 4, parts, free=first or k % 2 == 1)
            for k in range(4):
                head(k, 0, True)
            sp.wait_ge(panel_used, PM + 6)
            sp.wait_ge(u_ready, 22)
            sp.dma_start(wuv[:, :, :], I["w_uv"][0].rearrange("(c p) h d -> p c (h d)", p=P)).then_inc(wuv_ready, 16)
            def page_group(b, g, s):
                sp.wait_ge(wuv_ready, 32)
                for k in range(4):
                    page = sp.value_load(ptab[0:1, bass.ds(b * NPG + 4 * g + k, 1)], min_val=0,
                                         max_val=I["cache_ckv"].shape[1] - 1)
                    q = s * NPG + 4 * g + k
                    sp.dma_start(pages[:, q, 0:KR], I["cache_ckv"][0][bass.ds(page, 1), :, :].rearrange("a k r -> (a k) r")
                                 ).then_inc(pg[s * 4 + g], 16)
                    sp.dma_start(pages[:, q, KR:KR + ROPE],
                                 I["cache_krope"][0][bass.ds(page, 1), :, :].rearrange("a k r -> (a k) r")
                                 ).then_inc(pg[s * 4 + g], 16)
            sp.wait_ge(kr_ready, 1)
            for g in range(3):
                page_group(0, g, 0)
            with sp.Fori(1, 4) as i:
                for k in range(4):
                    head(k, i)
            sp.wait_ge(ct_taken, 2 * NTT)
            for j in range(NTT):
                n = P if j < 4 else TS
                a = outs["ckv_prompt"][0, 0, j * P:(j + 1) * P, :] if j < 4 else outs["ckv_sample"][0].rearrange("b t r -> (b t) r")
                b = outs["kr_prompt"][0, 0, j * P:(j + 1) * P, :] if j < 4 else outs["kr_sample"][0].rearrange("b t r -> (b t) r")
                sp.dma_start(a, ckt[0:n, j, 0:KR]).then_inc(stored, 16)
                sp.dma_start(b, ckt[0:n, j, KR:KR + ROPE]).then_inc(stored, 16)
            wo = I["w_mla_out"][0].rearrange("(c p) n -> p c n", p=P)
            for k in range(4):
                if k % 2 == 0:
                    sp.wait_ge(panel_used, PO + k - 2)
                load(PO + k, 0, lambda d: [(d, wo[:, :, k * P:(k + 1) * P], UNIT)])

            sp.wait_ge(pv_ready, NH)
            sp.wait_ge(qa_taken, 2 * NH // 2)
            for b in range(2):
                for g in range(3 if b == 0 else 0, 4):
                    page_group(b, g, b)
            with sp.Fori(0, 3) as i:
                for s in range(2):
                    for g in range(4):
                        sp.wait_ge(spv, 5 * s + g + 1 + i * 10)
                        page_group(i * 2 + s + 2, g, s)
            for k in range(4, 8):
                load(PO + k, 0, lambda d: [(d, wo[:, :, k * P:(k + 1) * P], UNIT)])

        def mla_lowers(pool, lower, stage):
            for k in range(6):
                lower(PM + k, 0, 8)
            stage("mla_heads", [3] * 4, 4)

            def scale(b, db):
                pool.wait_ge(s_inv, b + 1 + db)
                pool.tensor_tensor(S[:, b % 2, 512:KEYS], S[:, b % 2, 512:KEYS],
                                   mx[:, b % 2, 7:8].to_broadcast([P, KEYS - 512]), ALU.mult).then_inc(sp_pool, 1)
            lower(PO, 0, 8)
            with pool.Fori(0, NB // 2) as i:
                scale(0, i * 2)
                scale(1, i * 2)
            for k in range(1, 8):
                lower(PO + k, 0, 8)

        def mla_acts(act, upper, root, square, norm):
            for k in range(6):
                upper(PM + 1 + k, 0, 8 if k < 5 else 3)
                if k == 0:
                    root(norm, D); norm += 1
                if k == 4:
                    root(norm, QR); norm += 1
                    for c in range(3):
                        act.wait_ge(zq_ready, c + 1)
                        act.activation(cqh[:, c, :], zc[:, c, :], ACT.Copy).then_inc(cqh_act, 1)
            root(norm, KR); norm += 1

            def softmax_exp(h, dyn, s, banks):
                for n in range(4):
                    act.wait_ge(nm_ready, 4 * h + max(n + 1, 2) + dyn * 4)
                    act.activation(PP[:, s, QT[n]:QT[n] + (n + 1) * P], banks[n], ACT.Exp, bias=st[:, s, n:n + 1],
                                   accum_out=st[:, s, 4 + n:5 + n]).then_inc(ex_ready, 1)

            with act.Fori(0, 4) as i:
                for j in (0, 1):
                    h = 2 * j
                    d4, d2 = i * 4, i * 2
                    upper(PH + 1 + h, i * 4, 3)
                    act.wait_ge(panel_used, PH + h + 1 + d4)
                    act.activation(Q[0:64, 0, :].rearrange("p (h n) -> p h n", h=2), ps[0:64, 0:2, 0:H], ACT.Copy).then_inc(qn_taken, 1)
                    act.wait_ge(kv_ready, 3 * j + 1 + i * 6)
                    act.activation(Kp[0:64, 0, :], ps[0:64, 2, :], ACT.Copy).then_inc(k_taken, 1)
                    act.activation(Kp[0:64, 1, :], ps[64:128, 2, :], ACT.Copy).then_inc(k_taken, 1)
                    upper(PH + 2 + h, i * 4, 3 if j == 0 else 8)
                    act.wait_ge(panel_used, PH + h + 2 + d4)
                    act.activation(Q[0:64, 1, :].rearrange("p (h n) -> p h n", h=2), ps[0:64, 0:2, 0:H], ACT.Copy).then_inc(qn_taken, 1)
                    for hh in (0, 1):
                        softmax_exp(h + hh, d4, hh, score_banks(hh))
                    for hh in (0, 1):
                        act.wait_ge(tr_ready, h + hh + 1 + d4)
                        act.activation(PT[:, hh, 0:512], ps[:, pt_banks[hh][0], :], ACT.Copy).then_inc(tr_act, 1)
                    for hh in (0, 1):
                        act.wait_ge(pv_ready, h + hh + 1 + d4)
                        rows = slice(64 * hh, 64 * hh + 64)
                        act.activation(oTh[rows, bass.ds(i * 2 + j, 1), 0:TP].rearrange("p a t -> p (a t)"),
                                       ps[rows, pv_bank[hh], :], ACT.Copy).then_inc(ov_hi, 1)

            def kt_copy(n, dn):
                act.wait_ge(kt_ready, n + 1 + dn)
                act.activation(KT[:, n % 2, 0, :], ps[:, 0, :], ACT.Copy)
                act.activation(KT[0:ROPE, n % 2, 2, :], ps[0:ROPE, 2, :], ACT.Copy).then_inc(kt_act, 1)

            def step(b, db, first, last):
                if not last:
                    for g in range(5):
                        if g < 3:
                            kt_copy(4 * b + g + 1, db * 4)
                        if g == 4 and b < NB - 1:
                            kt_copy(4 * b + 4, db * 4)
                        act.wait_ge(mx_dve, 5 * b + g + 1 + db * 5)
                        n = 512 if g < 4 else TS
                        act.activation(S[:, b % 2, g * 512:g * 512 + n], ps[:, 3 + (5 * b + g) % 2, 0:n], ACT.Copy
                                       ).then_inc(s_act, 1)
                if not first:
                    act.wait_ge(spv, 5 * b + db * 5)
                    act.activation(QA[:, 0, bass.ds((b - 1 + db) * P, P)], ps[:, 6, 0:P], ACT.Copy).then_inc(o_act, 1)
                if not last:
                    act.wait_ge(snm, b + 1 + db)
                    act.wait_ge(s_act, 5 * b + 5 + db * 5)
                    act.activation(S[:, b % 2, 0:KEYS], S[:, b % 2, 0:KEYS], ACT.Exp, bias=mx[:, b % 2, 5:6],
                                   accum_out=mx[:, b % 2, 6:7]).then_inc(sex, 1)
            kt_copy(0, 0)
            step(0, 0, True, False)
            with act.Fori(0, 3) as i:
                step(1, i * 2, False, False)
                step(2, i * 2, False, False)
            step(7, 0, False, False)
            step(8, 0, False, True)
            for q in (0, 1):
                act.wait_ge(sv_ready, q + 1)
                for s in (0, 1):
                    rows = slice(64 * s, 64 * s + 64)
                    src = ps[rows, q, :].rearrange("p (j s t) -> p j s t", s=2, t=TS)[:, :, s, :]
                    act.activation(oTh[rows, 4 * q:4 * q + 4, TP:T], src, ACT.Copy).then_inc(sv_hi, 1)
            square("mla_out", 8)
            return norm

        def mla_dves(dve, v, link, rms, inverse, spread, added):
            rms()
            cols = lambda c: gn[:, c:c + 1]
            link(dve.memset(krT[:, :], 0.0))
            link(dve.memset(acc[:, 0:T], 0.0))
            t0 = T0["mla_in"]
            a0 = AC["q"]
            link(dve.tensor_scalar(gql[:, 0:3], gn[:, GCOL["q"]:GCOL["q"] + 3], SCALE, None, ALU.mult))
            for k in range(6):
                dve.wait_ge(panel_used, PM + k + 1)
                dve.tensor_tensor(half(zc[:, k, :]), slot(t0 + k), half(r[:, :]), ALU.mult).then_inc(tile_taken, 1)
                dve.wait_ge(tile_taken, t0 + k + 1)
                if k == 3:
                    rms(rl)
                    link(dve.memset(acc[:, 0:T], 0.0))
                if k < 5:
                    link(dve.tensor_tensor(sq[:, :], zc[:, k, :], zc[:, k, :], ALU.mult))
                    dve.tensor_tensor(acc[:, 0:T], acc[:, 0:T], sq[:, :], ALU.add).then_inc(acc_done, 1)
                    dve.wait_ge(acc_done, a0 + k + 1)
                if k == 3:
                    for c in range(3):
                        dve.scalar_tensor_tensor(out=zc[:, c, :], in0=zc[:, c, :], scalar=gql[:, c:c + 1], in1=rl[:, :],
                                                 op0=ALU.mult, op1=ALU.mult).then_inc(zq_ready, 1)
                if k == 4:
                    for c in range(3):
                        dve.wait_ge(cqh_act, c + 1)
                        dve.tensor_tensor(cql[:, c, :], zc[:, c, :], cqh[:, c, :].bitcast(F32), ALU.subtract).then_inc(cq_ready, 1)
                    inverse()
            link(dve.tensor_tensor(sq[64:96, :], zc[96:128, 5, :], rope[96:128, :], ALU.mult))
            link(dve.tensor_tensor(krT[64:96, :], zc[64:96, 5, :], rope[64:96, :], ALU.mult))
            link(dve.tensor_tensor(krT[64:96, :], krT[64:96, :], sq[64:96, :], ALU.add))
            spread(rl)
            for c in range(2):
                dve.scalar_tensor_tensor(out=ckv[:, c, :], in0=zc[:, 3 + c, :], scalar=cols(GCOL["kv"] + c),
                                         in1=rl[:, :], op0=ALU.mult, op1=ALU.mult).then_inc(ckv_ready, 1)
            for s in (0, 1):
                link(dve.tensor_copy(Kp[64:96, s, :], krT[64:96, 0:TP]))
            dve.tensor_copy(krS[0:ROPE, :], krT[64:96, TP:T]).then_inc(kr_ready, 1)
            for j in range(NTT):
                n = P if j < 4 else TS
                dve.wait_ge(ct_ready, j + 1)
                b = 2 + j % 2
                dve.tensor_copy(ckt[0:n, j, 0:KR], ps[0:n, b, 0:KR]).then_inc(ct_taken, 1)
                dve.tensor_copy(ckt[0:n, j, KR:KR + ROPE], ps[0:n, b, KR + 64:KR + 96]).then_inc(ct_taken, 1)
            dve.wait_ge(ct_taken, 2 * NTT)
            dve.memset(st[:, 0, 0:1], 0.0).then_inc(ov_lo, 1)

            def rope_query(h, hh, dh):
                dve.wait_ge(panel_used, PH + h + 1 + dh)
                link(dve.tensor_tensor(half(qtmp[64:96, :]), ps[96:128, 0:2, 0:H], half(rope[96:128, :]), ALU.mult))
                link(dve.tensor_tensor(half(Q[64:96, hh, :]), ps[64:96, 0:2, 0:H], half(rope[64:96, :]), ALU.mult))
                dve.tensor_tensor(Q[64:96, hh, :], Q[64:96, hh, :], qtmp[64:96, :], ALU.add).then_inc(qr_taken, 1)
                dve.wait_ge(qr_taken, h + 1 + dh)
                dst = QA[0:ROPE, 2, :].rearrange("p (t h) -> p t h", h=NH)[:, :, bass.ds(h + dh, 1)]
                link(dve.tensor_copy(dst, Q[64:96, hh, TP:T].rearrange("p (t a) -> p t a", a=1)))

            LP = 2 * 3 + 2
            c0 = v["chain"]
            with dve.Fori(0, 4) as i:
                v["dyn"] = i * (2 * LP)
                for j in (0, 1):
                    h, d4 = 2 * j, i * 4
                    assert v["chain"] == c0 + j * LP
                    rope_query(h, 0, d4)
                    dve.wait_ge(kv_ready, 3 * j + 2 + i * 6)
                    dve.tensor_copy(WT[0:64, 0, :], ps[0:64, 4, 0:KR]).then_inc(wt_taken, 1)
                    dve.tensor_copy(WT[0:64, 1, :], ps[64:128, 4, 0:KR]).then_inc(wt_taken, 1)
                    rope_query(h + 1, 1, d4)
                    for hh in (0, 1):
                        banks = score_banks(hh)
                        for n in range(4):
                            dve.wait_ge(sc_ready, 4 * (h + hh) + max(n + 1, 2) + d4 * 4)
                            dve.tensor_reduce(out=st[:, hh, n:n + 1], in_=banks[n], axis=AX.X, op=ALU.max,
                                              negate=True).then_inc(nm_ready, 1)
                    for hh in (0, 1):
                        dve.wait_ge(ex_ready, 4 * (h + hh) + 4 + d4 * 4)
                        link(dve.reciprocal(st[:, hh, 8:12], st[:, hh, 4:8]))
                        for n in range(4):
                            o = PP[:, hh, QT[n]:QT[n] + (n + 1) * P]
                            dve.tensor_scalar(o, o, st[:, hh, 8 + n:9 + n], None, ALU.mult).then_inc(pp_ready, 1)
                        if hh:
                            continue
                        dve.wait_ge(kv_ready, 3 * j + 3 + i * 6)
                        dve.tensor_copy(Vp[:, :, :].rearrange("p a d -> p (a d)"), ps[:, 1, :]).then_inc(v_taken, 1)
                        dve.wait_ge(qa_ready, j + 1 + i * 2)
                        for s in (0, 1):
                            dst = QA[:, 0:2, :].rearrange("p c (t h) -> p c t h", h=NH)[:, :, :, bass.ds(h + s + d4, 1)]
                            src = ps[:, 4, 256 + 128 * s:384 + 128 * s].rearrange("p (c t a) -> p c t a", c=2, a=1)
                            dve.tensor_copy(dst, src).then_inc(qa_taken, 1)
                    for hh in (0, 1):
                        dve.wait_ge(tr_ready, h + hh + 1 + d4)
                        b = pt_banks[hh]
                        dve.tensor_copy(PT[:, hh, KO[1]:KO[2]], ps[:, b[1], 0:384]).then_inc(tr_dve, 1)
                        dve.tensor_copy(PT[:, hh, KO[2]:1280], ps[:, b[2], 0:384]).then_inc(tr_dve, 1)
                    for hh in (0, 1):
                        dve.wait_ge(ov_hi, h + hh + 1 + d4)
                        rows = slice(64 * hh, 64 * hh + 64)
                        jj = i * 2 + j
                        dve.tensor_tensor(oTl[rows, bass.ds(jj, 1), 0:TP].rearrange("p a t -> p (a t)"),
                                          ps[rows, pv_bank[hh], :],
                                          oTh[rows, bass.ds(jj, 1), 0:TP].rearrange("p a t -> p (a t)").bitcast(F32),
                                          ALU.subtract).then_inc(ov_lo, 1)
            assert v["chain"] == c0 + 2 * LP
            v["chain"] = c0 + 8 * LP
            v["dyn"] = 0

            def kt_copy(n, dn):
                dve.wait_ge(kt_ready, n + 1 + dn)
                dve.tensor_copy(KT[:, n % 2, 1, :], ps[:, 1, :]).then_inc(kt_dve, 1)

            def pts_copy(n, dn, g):
                dve.wait_ge(pts_ready, n + 1 + dn)
                if g < 4:
                    dve.tensor_copy(PTs[:, n % 2, :], ps[:, 5, :]).then_inc(pts_taken, 1)
                else:
                    dve.tensor_copy(PTs[0:TS, n % 2, 0:P], ps[0:TS, 5, 0:P]).then_inc(pts_taken, 1)

            def ahead(b, db):
                link(dve.tensor_copy(QAb[:, b % 2, 0:2, :], QA[:, 0:2, bass.ds((b + db) * P, P)]))
                dve.tensor_copy(QAb[0:ROPE, b % 2, 2, :], QA[0:ROPE, 2, bass.ds((b + db) * P, P)]).then_inc(qab_ready, 1)

            def step(b, db, first, last):
                if not last:
                    kt_copy(4 * b + 1, db * 4)
                for g in range(5):
                    if not last and 0 < g < 3:
                        kt_copy(4 * b + g + 1, db * 4)
                    if not last and g == 4 and b < NB - 1:
                        kt_copy(4 * b + 4, db * 4)
                    if not first and g:
                        pts_copy(5 * (b - 1) + g, db * 5, g)
                    if not last:
                        dve.wait_ge(ss_sc, 5 * b + g + 1 + db * 5)
                        n = 512 if g < 4 else TS
                        dve.reduce_max(mx[:, b % 2, g:g + 1], ps[:, 3 + (5 * b + g) % 2, 0:n], AX.X).then_inc(mx_dve, 1)
                    if not first and g == 0:
                        pts_copy(5 * (b - 1) + g, db * 5, g)
                if not first:
                    dve.wait_ge(spv, 5 * b + db * 5)
                    dve.tensor_copy(QA[:, 1, bass.ds((b - 1 + db) * P, P)], ps[:, 7, 0:P]).then_inc(o_dve, 1)
                if not last:
                    dve.wait_ge(mx_dve, 5 * b + 5 + db * 5)
                    dve.tensor_reduce(out=mx[:, b % 2, 5:6], in_=mx[:, b % 2, 0:5], axis=AX.X, op=ALU.max,
                                      negate=True).then_inc(snm, 1)
                    if b < NB - 1:
                        ahead(b + 1, db)
                    dve.wait_ge(sex, b + 1 + db)
                    dve.reciprocal(mx[:, b % 2, 7:8], mx[:, b % 2, 6:7]).then_inc(s_inv, 1)
                    dve.wait_ge(s_inv, b + 1 + db)
                    dve.tensor_scalar(S[:, b % 2, 0:512], S[:, b % 2, 0:512], mx[:, b % 2, 7:8], None, ALU.mult).then_inc(sp_ready, 1)
            ahead(0, 0)
            kt_copy(0, 0)
            link(dve.memset(S[:, :, KEYS:KEYS + P - TS], 0.0))
            step(0, 0, True, False)
            c0 = v["chain"]
            with dve.Fori(0, 3) as i:
                v["dyn"] = i * 2
                step(1, i * 2, False, False)
                step(2, i * 2, False, False)
            assert v["chain"] == c0 + 2
            v["chain"], v["dyn"] = c0 + 6, 0
            step(7, 0, False, False)
            step(8, 0, False, True)
            for q in (0, 1):
                for s in (0, 1):
                    rows = slice(64 * s, 64 * s + 64)
                    dve.wait_ge(sv_hi, 2 * q + s + 1)
                    src = ps[rows, q, :].rearrange("p (j s t) -> p j s t", s=2, t=TS)[:, :, s, :]
                    dve.tensor_tensor(oTl[rows, 4 * q:4 * q + 4, TP:T], src,
                                      oTh[rows, 4 * q:4 * q + 4, TP:T].bitcast(F32), ALU.subtract).then_inc(sv_lo, 1)
            added("mla_out", "ffb0")

        pt_banks, pv_bank = [(7, 5, 6), (0, 2, 3)], [6, 7]

        def score_banks(hh):
            a, b, c = (5, 6, 7) if hh == 0 else (2, 3, 0)
            return [ps[:, c, 0:P], ps[:, c, P:3 * P], ps[:, b, 0:3 * P], ps[:, a, :]]

        def mla_pes(pe, v, products, sums, broadcast, tiles, xgh, xgl):
            mm, tr = nc.tensor.matmul, nc.tensor.transpose
            hooks = {1: {4: broadcast}, 4: {3: broadcast}, 5: {6: lambda: sums(2)}}
            for k in range(6):
                pe.wait_ge(tile_taken, T0["mla_in"] + k - 1)
                products(PM + k, 0, 8, xgh, xgl, slot(T0["mla_in"] + k),
                         waits=(lambda n: pe.wait_ge(xg_ready, XG["mix0"] + n + 1)) if k == 0 else None, at=hooks.get(k))
                if k in (0, 3):
                    sums(8 if k == 0 else 3)
            broadcast()
            pe.wait_ge(ckv_ready, 2)
            pe.wait_ge(tile_taken, T0["mla_in"] + 6)
            for j in range(NTT):
                n = P if j < 4 else TS
                b = 2 + j % 2
                if j >= 2:
                    pe.wait_ge(ct_taken, 2 * j - 2)
                for c in range(3):
                    src = ckv[:, c, j * P:j * P + n] if c < 2 else krT[:, j * P:j * P + n]
                    ins = tr(ps[0:n, b, c * P:(c + 1) * P], src, ident)
                ins.then_inc(ct_ready, 1)
            pe.wait_ge(cq_ready, 3)
            pe.wait_ge(wuv_ready, 32)
            pe.wait_ge(ov_lo, 1)
            with pe.Fori(0, 4) as i:
                for j in (0, 1):
                    h, d4, d2 = 2 * j, i * 4, i * 2

                    def query(hh):
                        products(PH + h + hh, d4, 3, lambda n: cqh[:, n, :], lambda n: cql[:, n, :], ps[:, 0:2, 0:H])
                    query(0)
                    rw = raw[:, (PH + h + 0) % RAW, :, :]
                    for c in range(2):
                        ins = mm(ps[:, 2, :], rw[:, 3 + c, :], ckv[:, c, 0:TP], start=c == 0, stop=c == 1)
                    ins.then_inc(kv_ready, 1)
                    for c in range(2):
                        ins = tr(ps[:, 4, c * P:(c + 1) * P], rw[:, 3 + c, :], ident)
                    ins.then_inc(kv_ready, 1)
                    pe.wait_ge(qn_taken, h + 1 + d4)
                    pe.wait_ge(qr_taken, h + 1 + d4)
                    query(1)

                    def scores(hh):
                        banks = score_banks(hh)
                        pe.wait_ge(qn_taken, h + hh + 1 + d4)
                        pe.wait_ge(qr_taken, h + hh + 1 + d4)
                        pe.wait_ge(k_taken, 2 * j + 2 + i * 4)
                        for n in range(4):
                            mm(banks[n], Q[0:96, hh, n * P:(n + 1) * P], Kp[0:96, hh, 0:(n + 1) * P], start=True, stop=False)
                            mm(banks[n][:, n * P:(n + 1) * P], idb, cb[:, B_CAUSAL:B_CAUSAL + P], start=False,
                               stop=True).then_inc(sc_ready, 1)
                    pe.wait_ge(ov_lo, h + 1 + d4)
                    scores(0)
                    scores(1)
                    for kt in range(4):
                        for c in range(2):
                            ins = mm(ps[:, 1, kt * P:(kt + 1) * P], ckv[:, c, kt * P:(kt + 1) * P],
                                     wuv[:, c, bass.ds((d2 + j) * P, P)], start=c == 0, stop=c == 1)
                    ins.then_inc(kv_ready, 1)
                    pe.wait_ge(wt_taken, 2 * j + 2 + i * 4)
                    pe.wait_ge(qn_taken, h + 2 + d4)
                    for s in (0, 1):
                        for c in (0, 1):
                            ins = mm(ps[:, 4, 256 + 128 * s + 64 * c:320 + 128 * s + 64 * c],
                                     WT[0:64, s, c * P:(c + 1) * P], Q[0:64, s, TP:T], start=True, stop=True)
                    ins.then_inc(qa_ready, 1)
                    for hh in (0, 1):
                        pe.wait_ge(pp_ready, 4 * (h + hh) + 4 + d4 * 4)
                        bank = pt_banks[hh]
                        where = [ps[:, bank[0], :], ps[:, bank[1], :], ps[:, bank[2], :], ps[:, bank[2], 256:512]]
                        for kt in range(4):
                            for n in range(kt, 4):
                                ins = tr(where[kt][:, (n - kt) * P:(n - kt + 1) * P],
                                         PP[:, hh, QT[n] + kt * P:QT[n] + (kt + 1) * P], ident)
                        ins.then_inc(tr_ready, 1)
                        if hh == 0:
                            continue
                        pe.wait_ge(v_taken, j + 1 + d2)
                        pe.wait_ge(qa_taken, 2 * j + 2 + i * 4)
                        for s in (0, 1):
                            pe.wait_ge(tr_act, h + s + 1 + d4)
                            pe.wait_ge(tr_dve, 2 * (h + s) + 2 + d4 * 2)
                            for kt in range(4):
                                ins = mm(ps[:, pv_bank[s], kt * P:512], Vp[:, kt, :], PT[:, s, KO[kt]:KO[kt] + (4 - kt) * P],
                                         start=kt == 0, stop=kt == 3)
                            ins.then_inc(pv_ready, 1)

            pe.wait_ge(ov_lo, NH + 1)

            def pages_t(b, db, g):
                n = 4 * b + g
                s = b % 2
                pe.wait_ge(pg[s * 4 + g], 128 * (b // 2 + 1) + (db // 2 if isinstance(db, int) else db) * 64)
                if n:
                    pe.wait_ge(kt_act, n + db * 4)
                    pe.wait_ge(kt_dve, n + db * 4)
                for k in range(4):
                    for c in range(3):
                        w = P if c < 2 else ROPE
                        ins = tr(ps[0:w, c, k * P:(k + 1) * P], pages[:, s * NPG + 4 * g + k, c * P:c * P + w], ident)
                ins.then_inc(kt_ready, 1)

            def scores_s(b, db, g):
                m = 5 * b + g
                bank = ps[:, 3 + m % 2, :]
                s = b % 2
                if g == 0:
                    pe.wait_ge(qab_ready, b + 1 + db)
                if m >= 2:
                    pe.wait_ge(s_act, m - 1 + db * 5)
                    pe.wait_ge(mx_dve, m - 1 + db * 5)
                if g < 4:
                    pe.wait_ge(kt_act, 4 * b + g + 1 + db * 4)
                    pe.wait_ge(kt_dve, 4 * b + g + 1 + db * 4)
                    for c in range(3):
                        w = P if c < 2 else ROPE
                        ins = mm(bank, QAb[0:w, s, c, :], KT[0:w, g % 2, c, :], start=c == 0, stop=c == 2)
                else:
                    mm(bank[:, 0:TS], QAb[:, s, 0, :], ckv[:, 0, TP:T], start=True, stop=False)
                    mm(bank[:, 0:TS], QAb[:, s, 1, :], ckv[:, 1, TP:T], start=False, stop=False)
                    mm(bank[:, 0:TS], QAb[0:ROPE, s, 2, :], krS[0:ROPE, :], start=False, stop=False)
                    ins = mm(bank[:, 0:TS], idb, cb[:, bass.ds(B_SAMPLE + (b + db) * TS, TS)], start=False, stop=True)
                ins.then_inc(ss_sc, 1)

            def probs_t(b, db, g):
                n, s = 5 * (b - 1) + g, (b - 1) % 2
                if g == 0:
                    pe.wait_ge(sp_ready, b + db)
                if g == 1:
                    pe.wait_ge(sp_pool, b + db)
                if n:
                    pe.wait_ge(pts_taken, n + db * 5)
                if g < 4:
                    for k in range(4):
                        ins = tr(ps[:, 5, k * P:(k + 1) * P], S[:, s, g * 512 + k * P:g * 512 + (k + 1) * P], ident)
                else:
                    ins = tr(ps[:, 5, 0:P], S[:, s, 2048:2048 + P], ident)
                ins.then_inc(pts_ready, 1)

            def out_s(b, db, g):
                n, s = 5 * (b - 1) + g, (b - 1) % 2
                pe.wait_ge(pts_taken, n + 1 + db * 5)
                if g == 0 and b > 1:
                    pe.wait_ge(o_act, b - 1 + db)
                    pe.wait_ge(o_dve, b - 1 + db)
                if g < 4:
                    for k in range(4):
                        for c in (0, 1):
                            ins = mm(ps[:, 6 + c, 0:P], pages[:, s * NPG + 4 * g + k, c * P:(c + 1) * P],
                                     PTs[:, n % 2, k * P:(k + 1) * P], start=g == 0 and k == 0, stop=False)
                else:
                    for c in (0, 1):
                        ins = mm(ps[:, 6 + c, 0:P], ckt[0:TS, 4, c * P:(c + 1) * P], PTs[0:TS, n % 2, 0:P],
                                 start=False, stop=True)
                ins.then_inc(spv, 1)

            def step(b, db, first, last):
                if not last:
                    pages_t(b, db, 1)
                    scores_s(b, db, 0)
                if not first:
                    probs_t(b, db, 0)
                for g in range(5):
                    if not last and g < 2:
                        pages_t(b, db, g + 2)
                    if not last and g == 3 and b < NB - 1:
                        pages_t(b + 1, db, 0)
                    if last and g < 4:
                        probs_t(b, db, g + 1)
                    if not first:
                        out_s(b, db, g)
                        if g < 4 and not last:
                            probs_t(b, db, g + 1)
                    if not last and g < 4:
                        scores_s(b, db, g + 1)
            pages_t(0, 0, 0)
            step(0, 0, True, False)
            with pe.Fori(0, 3) as i:
                step(1, i * 2, False, False)
                step(2, i * 2, False, False)
            step(7, 0, False, False)
            step(8, 0, False, True)
            pe.wait_ge(o_act, NB)
            pe.wait_ge(o_dve, NB)
            lat = QA[:, 0:2, :].rearrange("p c (t h) -> p c t h", h=NH)
            for q in (0, 1):
                for h in range(8 * q, 8 * q + 8):
                    for c in (0, 1):
                        ins = mm(ps[:, q, (h % 8) * TS:(h % 8 + 1) * TS], wuv[:, c, (h // 2) * P:(h // 2 + 1) * P],
                                 lat[:, c, :, h], start=c == 0, stop=c == 1)
                ins.then_inc(sv_ready, 1)
            pe.wait_ge(sv_lo, 4)
            tiles("mla_out", 8, 1, lambda n: oTh[:, n, :], lambda n: oTl[:, n, :], 2, 4)

        lu = Region(nc, X1, TMP)
        gTh = lu.put("gTh", [P, NC_D, T], F32R)
        gTl = lu.put("gTl", [P, NC_D, T], F32R)
        qT = lu.put("qT", [P, LH, T])
        kT = lu.put("kT", [P, LH, T])
        so = lu.put("so", [P, NC_D, T])
        Cb = lu.put("Cb", [P, NB, DV + 1])
        cols = lu.put("cols", [P, 64])
        nT = lu.put("nT", [P, NB * LH])
        nP = lu.put("nP", [P, LH])
        bg = lu.put("bg", [P, 2])
        den = lu.put("den", [P, 16])
        V0 = lu.at
        vT = lu.put("vT", [P, NC_D, T])
        lv = Region(nc, V0, TMP)
        Dm = lv.put("Dm", [P, 1280 + TS])
        SD = lv.put("SD", [P, 1280 + P])
        qd = lv.put("qd", [P, TS])
        qn = lv.put("qn", [P, P])
        kw = lv.put("kw", [P, 4, DK])
        RX = lv.put("RX", [P, 2, T])
        late = Region(nc, V0, TMP)
        nrow = late.put("nrow", [P, P])
        nst = late.put("nst", [NB * LH, DK])
        sqn = Region(nc, V0, TMP).put("sqn", [P, 2, NTT * P])
        lx = Region(nc, X0, X1)
        Vt = lx.put("Vt", [P, NTT, LH, DV + 1])
        kt = lx.put("kt", [P, NTT, LH, DK])
        kwb = lx.put("kwb", [P, NB, DK])
        wC = lx.put("wC", [P, NTT * LH])
        Wm = lx.put("Wm", [P, LH, NB])
        eC = lx.put("eC", [P, NTT * LH])
        lt = Region(nc, TMP, whole.end)
        RB = lt.put("RB", [P, T])
        lt2 = Region(nc, lt.at, whole.end)
        RA, RC, RD = (lt.put(n, [P, T]) for n in ("RA", "RC", "RD"))
        RE = lt.put("RE", [P, 2 * TS + NB])
        Mb = lt2.put("Mb", [P, T + TS + NB])
        Md = lt2.put("Md", [P, T])
        Co = lt2.put("Co", [P, DV + 1])
        m0 = whole_m0
        nst0 = Region(nc, X1, TMP).put("nst0", [NB * LH, DK])
        SO = [0, 4 * P, 7 * P, 9 * P, 10 * P]
        GP, IP, LO = P0["mlstm_gates"], P0["mlstm_in"], P0["mlstm_out"]
        GT, IT = T0["mlstm_gates"], T0["mlstm_in"]
        st_ready, g_dve, g_act = sem("state_ready"), sem("g_dve"), sem("g_act")
        o_pre, o_sig, m_ready, kv_t, kv_c = sem("o_pre"), sem("o_sig"), sem("m_ready"), sem("kv_t"), sem("kv_c")
        ct2, cc2, wc_in, wc_ex = sem("cols_t"), sem("cols_c"), sem("wc_in"), sem("wc_ex")
        l_mb, l_md, l_dec, l_D = sem("l_mb"), sem("l_md"), sem("l_dec"), sem("l_D")
        l_S, l_SD, l_qn, l_num, l_den = sem("l_S"), sem("l_SD"), sem("l_qn"), sem("l_num"), sem("l_den")
        l_sq, l_ss, l_v, l_rs, l_gc, l_gb = sem("l_sq"), sem("l_ss"), sem("l_v"), sem("l_rs"), sem("l_gc"), sem("l_gb")
        l_kw, l_kwb, l_cp, l_co, l_cost = sem("l_kw"), sem("l_kwb"), sem("l_cp"), sem("l_co"), sem("l_cost")
        l_C, l_cs, l_cn, l_cst, l_out = sem("l_C"), sem("l_cs"), sem("l_cn"), sem("l_cst"), sem("l_out")
        l_nt, l_nc = sem("l_nt"), sem("l_nc")
        l_rc, l_rx, l_hi, l_lo = sem("l_rc"), sem("l_rx"), sem("l_hi"), sem("l_lo")

        def mlstm_loads(sp, load):
            w = I["w_mlstm_in"][0].rearrange("(c p) n -> p c n", p=P)
            G = 2 * LH * DK + 2 * LH * DV
            load(GP, 0, lambda d: [(d[:, :, 0:8], w[:, :, G:G + 8], 16), (d[:, :, 8:32], w[:, :, 0:24], 16),
                                   (d[:, :, 32:36], w[:, :, G + 4:G + 8], 32), (d[:, :, 36:128], w[:, :, 0:92], 48)])
            with sp.Fori(0, 6) as i:
                for k in range(4):
                    load(IP + k, i * 4, lambda d: [(d, w[:, :, bass.ds((i * 4 + k) * P, P)], UNIT)])
            wo = I["w_mlstm_out"][0].rearrange("(c p) n -> p c n", p=P)
            for k in range(4):
                load(LO + k, 0, lambda d: [(d, wo[:, :, k * P:(k + 1) * P], UNIT)])
            sC = I["state_C"][0].rearrange("b h k v -> k b h v")
            oC = outs["C_sample"][0].rearrange("b h k v -> k b h v")
            with nc.allow_non_contiguous_dma(reason="four stabilisers a row"):
                sp.wait_ge(m_ready, 1)
                sp.dma_start(outs["m_prompt"][0].rearrange("b h -> h b"), RD[0:LH, TP - 1:TP]).then_inc(stored, 16)
                sp.dma_start(outs["m_sample"][0].rearrange("b h -> h b"),
                             RD[0:LH, TP:T].rearrange("h (b t) -> h b t", t=TB)[:, :, TB - 1]).then_inc(stored, 16)
            sp.wait_ge(st_ready, 64)
            for h in range(LH):
                if h:
                    sp.wait_ge(l_cn, NB * h)
                    sp.dma_start(oC[:, :, h - 1, :], Cb[:, :, 0:DV]).then_inc(l_cst, 16)
                    sp.wait_ge(l_cst, 16 * h)
                sp.dma_start(Cb[:, :, 0:DV], sC[:, :, h, :]).then_inc(l_C, 16)
                sp.wait_ge(l_co, 2 * h + 2)
                sp.dma_start(outs["C_prompt"][0, 0, h], Co[:, 0:DV]).then_inc(l_cost, 16)
            sp.wait_ge(l_cn, NB * LH)
            sp.dma_start(oC[:, :, LH - 1, :], Cb[:, :, 0:DV]).then_inc(l_cst, 16)
            sp.wait_ge(l_nc, 2)
            sp.dma_start(outs["n_prompt"][0, 0], nrow[0:LH, :]).then_inc(stored, 16)
            sp.dma_start(outs["n_sample"][0].rearrange("b h k -> (b h) k"), nst[:, :]).then_inc(stored, 16)
            sp.wait_ge(l_cst, 16 * LH)
            sp.wait_ge(l_cost, 16 * LH)
            for k in range(4, 8):
                load(LO + k, 0, lambda d: [(d, wo[:, :, k * P:(k + 1) * P], UNIT)])

        def mlstm_lowers(pool, lower, stage):
            lower(GP, 0, 8)
            stage("mlstm_in", [8] * 4, 6)
            lower(LO, 0, 8)
            pool.memset(den[:, 15:16], -0.5).then_inc(l_rs, 1)
            for h in range(LH):
                pool.wait_ge(l_v, h + 1)
                pool.wait_ge(l_rs, h + 1)
                pool.tensor_tensor(den[:, 10:15], den[:, 5:10], den[:, 15:16].to_broadcast([P, 5]), ALU.pow).then_inc(l_rs, 1)
                for c in (0, 1):
                    pool.wait_ge(l_hi, 2 * h + c + 1)
                    pool.tensor_tensor(gTl[:, 2 * h + c, :], RX[:, c, :], gTh[:, 2 * h + c, :].bitcast(F32),
                                       ALU.subtract).then_inc(l_lo, 1)
            for k in range(1, 8):
                lower(LO + k, 0, 8)

        def mlstm_acts(act, upper, root, square, norm):
            upper(GP + 1, 0, 8)
            root(norm, D); norm += 1
            with nc.allow_non_contiguous_dma(reason="biases and stabilisers, a word each"):
                act.dma_start(bg[0:LH, 0:1], I["b_igate"].rearrange("a h -> h a")).then_inc(st_ready, 16)
                act.dma_start(bg[0:LH, 1:2], I["b_fgate"].rearrange("a h -> h a")).then_inc(st_ready, 16)
                act.dma_start(m0[0:LH, :], I["state_m"][0].rearrange("b h -> h b")).then_inc(st_ready, 16)
            act.wait_ge(panel_used, GP)
            act.dma_start(nst0[:, :], I["state_n"][0].rearrange("b h k -> (b h) k")).then_inc(st_ready, 16)
            upper(IP + 1, 0, 8)
            act.wait_ge(g_dve, 1)
            act.activation(RA[0:LH, :], RA[0:LH, :], ACT.Tanh, bias=bg[0:LH, 0:1], scale=1.0 / CAP)
            act.activation(RB[0:LH, :], RB[0:LH, :], ACT.Tanh, bias=bg[0:LH, 1:2], scale=1.0 / CAP).then_inc(g_act, 1)
            act.wait_ge(g_act, 1)
            act.activation(RC[0:LH, :], RB[0:LH, :], ACT.Exp, scale=-CAP).then_inc(g_act, 1)
            upper(IP + 2, 0, 8)
            act.wait_ge(g_dve, 2)
            act.activation(RB[0:LH, :], RD[0:LH, :], ACT.Ln).then_inc(g_act, 1)
            for k in range(2, 16):
                upper(IP + 1 + k, 0, 8)
            for c in range(NC_D):
                upper(IP + 17 + c, 0, 8)
                act.wait_ge(tile_taken, IT + 17 + c)
                act.activation(so[:, c, :], so[:, c, :], ACT.Sigmoid).then_inc(o_sig, 1)
            act.wait_ge(wc_in, 1)
            act.activation(wC[:, :], wC[:, :], ACT.Exp).then_inc(wc_ex, 1)
            act.activation(eC[:, :], cols[:, 20:40], ACT.Exp, scale=-1.0).then_inc(wc_ex, 1)
            def upper_part(h):
                for c in (0, 1):
                    act.wait_ge(l_rx, 2 * h + c + 1)
                    act.activation(gTh[:, 2 * h + c, :], RX[:, c, :], ACT.Copy).then_inc(l_hi, 1)
            for h in range(LH):
                act.wait_ge(l_mb, h + 1)
                act.activation(Mb[:, T:T + TS + NB], Mb[:, T:T + TS + NB], ACT.Exp).then_inc(l_dec, 1)
                act.wait_ge(l_md, h + 1)
                for s in range(NTT):
                    n = P if s < 4 else TS
                    ins = act.activation(Dm[0:n, SO[s]:SO[s] + n], Md[0:n, s * P:s * P + n], ACT.Exp,
                                         bias=cols[0:n, 4 * s + h:4 * s + h + 1], scale=-1.0)
                    if s < 3:
                        ins = act.activation(Dm[:, SO[s] + P:SO[s + 1]], Mb[:, (s + 1) * P:TP], ACT.Exp,
                                             bias=cols[:, 4 * s + h:4 * s + h + 1], scale=-1.0)
                    ins.then_inc(l_D, 1)
                if h:
                    upper_part(h - 1)
                for s in range(4):
                    ins = act.activation(kw[:, s, :], kt[:, s, h, :], ACT.Copy, scale=wC[:, 4 * s + h:4 * s + h + 1])
                ins.then_inc(l_kw, 1)
                for c in (0, 1):
                    act.wait_ge(l_num, 3 * h + c + 1)
                    act.wait_ge(l_SD, 5 * h + 5)
                    act.activation(sqn[:, c, 0:TP], ps[:, 6 + c, :], ACT.Square).then_inc(l_sq, 1)
                act.wait_ge(l_num, 3 * h + 3)
                act.activation(sqn[:, :, T:NTT * P], ident.rearrange("p (c t) -> p c t", c=2), ACT.Copy, scale=0.0)
                act.activation(sqn[:, :, TP:T], ps[:, 5, P:2 * P].rearrange("p (c t) -> p c t", c=2), ACT.Square).then_inc(l_sq, 1)
            upper_part(LH - 1)
            square("mlstm_out", 8)
            return norm

        def mlstm_dves(dve, v, link, rms, inverse, spread, added):
            rms()
            dve.wait_ge(st_ready, 64)
            link(dve.tensor_scalar(bg[0:LH, :], bg[0:LH, :], 1.0 / CAP, None, ALU.mult))
            link(dve.memset(cols[:, :], 0.0))
            dve.wait_ge(panel_used, GP + 1)
            tg = 2 * (GT % 2)
            link(dve.tensor_tensor(half(RA[0:LH, :]), ps[0:LH, tg:tg + 2, 0:H], half(r[0:LH, :]), ALU.mult))
            dve.tensor_tensor(half(RB[0:LH, :]), ps[32:32 + LH, tg:tg + 2, 0:H], half(r[32:32 + LH, :]), ALU.mult).then_inc(tile_taken, 1)
            dve.wait_ge(tile_taken, GT + 1)
            dve.memset(den[:, 0:1], 0.0).then_inc(g_dve, 1)

            rows = lambda t: t[0:LH, 0:TP]
            segs = lambda t: t[0:LH, TP:T].rearrange("h (b t) -> h b t", t=TB)

            def scan(n, src, dst, op):
                d = 1 << n
                link(dve.tensor_tensor(rows(dst)[:, d:], rows(src)[:, d:], rows(src)[:, 0:TP - d], op))
                link(dve.tensor_copy(rows(dst)[:, 0:d], rows(src)[:, 0:d]))
                if n < 3:
                    link(dve.tensor_tensor(segs(dst)[:, :, d:], segs(src)[:, :, d:], segs(src)[:, :, 0:TB - d], op))
                    link(dve.tensor_copy(segs(dst)[:, :, 0:d], segs(src)[:, :, 0:d]))

            def evacuate(t):
                dst = (qT[:, t, :] if t < 4 else kT[:, t - 4, :] if t < 8 else vT[:, t - 8, :] if t < 16
                       else so[:, t - 16, :])
                dve.wait_ge(panel_used, IP + t + 1)
                if t < 4:
                    dve.scalar_tensor_tensor(out=half(dst), in0=slot(IT + t), scalar=DK ** -0.5, in1=half(r[:, :]),
                                             op0=ALU.mult, op1=ALU.mult).then_inc(tile_taken, 1)
                else:
                    dve.tensor_tensor(half(dst), slot(IT + t), half(r[:, :]), ALU.mult).then_inc(tile_taken, 1)

            L = slice(0, LH)
            for t in range(24):
                evacuate(t)
                if t == 0:
                    dve.wait_ge(g_act, 2)
                    dve.tensor_scalar(RD[L, :], RC[L, :], 1.0, None, ALU.add).then_inc(g_dve, 1)
                    dve.wait_ge(g_dve, 2)
                if t == 1:
                    dve.wait_ge(g_act, 3)
                    link(dve.tensor_scalar(RD[L, :], RD[L, :], 1.0, None, ALU.subtract))
                    link(dve.reciprocal(RD[L, :], RD[L, :]))
                if t == 2:
                    link(dve.tensor_tensor(RC[L, :], RC[L, :], RD[L, :], ALU.mult))
                    link(dve.scalar_tensor_tensor(out=RB[L, :], in0=RB[L, :], scalar=-1.0, in1=RC[L, :],
                                                  op0=ALU.mult, op1=ALU.mult))
                if 3 <= t < 12:
                    n = t - 3
                    scan(n, (RB, RC)[n % 2], (RC, RB)[n % 2], ALU.add)
                    if n == 2:
                        link(dve.tensor_copy(RB[L, TP:T], RC[L, TP:T]))
                if t == 12:
                    link(dve.scalar_tensor_tensor(out=RA[L, :], in0=RA[L, :], scalar=CAP, in1=RC[L, :],
                                                  op0=ALU.mult, op1=ALU.subtract))
                    scan(0, RA, RB, ALU.max)
                if 13 <= t < 21:
                    n = t - 12
                    scan(n, (RB, RD)[(n - 1) % 2], (RD, RB)[(n - 1) % 2], ALU.max)
                if t == 21:
                    link(dve.tensor_scalar(rows(RB), rows(RB), 0.0, None, ALU.max))
                    mb = m0[0:LH, :].rearrange("h (b a) -> h b a", a=1).to_broadcast([LH, NB, TB])
                    link(dve.tensor_tensor(segs(RB), segs(RB), mb, ALU.max))
                    dve.tensor_tensor(RD[L, :], RC[L, :], RB[L, :], ALU.add).then_inc(m_ready, 1)
                    end = segs(RB)[:, :, TB - 1:TB]
                    link(dve.tensor_copy(RE[L, 0:TS].rearrange("h (b t) -> h b t", t=TB), end.to_broadcast([LH, NB, TB])))
                    link(dve.tensor_tensor(RE[L, TS:2 * TS].rearrange("h (b t) -> h b t", t=TB), mb, segs(RB), ALU.subtract))
                    link(dve.tensor_tensor(RE[L, 2 * TS:2 * TS + NB].rearrange("h (b a) -> h b a", a=1),
                                           m0[0:LH, :].rearrange("h (b a) -> h b a", a=1), end, ALU.subtract))
                    dve.memset(den[:, 1:2], 0.0).then_inc(g_dve, 1)
            dve.wait_ge(ct2, 1)
            link(dve.tensor_copy(cols[:, 0:16], ps[:, 4, 0:16]))
            link(dve.tensor_copy(cols[0:TS, 16:20], ps[0:TS, 4, 16:20]))
            link(dve.tensor_copy(cols[:, 20:36], ps[:, 4, 20:36]))
            link(dve.tensor_copy(cols[0:TS, 36:44], ps[0:TS, 4, 36:44]))
            link(dve.tensor_copy(cols[:, 44:48], ps[:, 4, 44:48]))
            link(dve.tensor_copy(nT[:, :], ps[:, 4, 64:96]))
            mt_ = cols[:, 44:48].rearrange("p (a h) -> p a h", a=1).to_broadcast([P, 4, LH])
            link(dve.memset(wC[:, 16:20], 0.0))
            link(dve.tensor_tensor(wC[:, 0:16].rearrange("p (s h) -> p s h", h=LH),
                                   cols[:, 0:16].rearrange("p (s h) -> p s h", h=LH), mt_, ALU.subtract))
            dve.tensor_tensor(wC[0:TS, 16:20], cols[0:TS, 16:20], cols[0:TS, 40:44], ALU.subtract).then_inc(wc_in, 1)
            link(dve.memset(Vt[:, :, :, DV:DV + 1], 1.0))
            for j in range(NTT):
                n = P if j < 4 else TS
                for q in range(3):
                    dve.wait_ge(kv_t, 3 * j + q + 1)
                    src = ps[0:n, 5 + q, :]
                    if q == 0:
                        dve.tensor_copy(kt[0:n, j, :, :].rearrange("p h d -> p (h d)"), src).then_inc(kv_c, 1)
                    else:
                        dve.tensor_copy(Vt[0:n, j, 2 * q - 2:2 * q, 0:DV], src.rearrange("p (h d) -> p h d", h=2)).then_inc(kv_c, 1)
            dve.wait_ge(kv_c, 3 * NTT)
            dve.wait_ge(wc_ex, 2)
            wm = wC[0:TS, 16:20].rearrange("p (h a) -> p h a", a=1).to_broadcast([TS, LH, NB])
            bm = cf[0:TS, C_BLK:C_BLK + NB].rearrange("p (a b) -> p a b", a=1).to_broadcast([TS, LH, NB])
            link(dve.tensor_tensor(Wm[0:TS, :, :], wm, bm, ALU.mult))
            link(dve.memset(SD[:, 1280:1280 + P], 0.0))
            link(dve.memset(qn[:, :], 0.0))
            tri = cf[:, C_TRI:C_TRI + P].rearrange("p (a t) -> p a t", a=1).to_broadcast([P, 4, P])
            nTh = lambda h: nT[:, :].rearrange("p (b h) -> p b h", h=LH)[:, :, h:h + 1]

            def stabilisers(h):
                dve.wait_ge(l_gb, 2 * h + 1)
                if h:
                    dve.wait_ge(l_D, NTT * h)
                dve.tensor_copy(Mb[:, :], flat(0, T + TS + NB)).then_inc(l_mb, 1)
                dve.wait_ge(l_mb, h + 1)
                link(dve.tensor_tensor(Md[:, 0:TP].rearrange("p (s t) -> p s t", s=4),
                                       Mb[:, 0:TP].rearrange("p (s t) -> p s t", s=4), tri, ALU.add))
                dve.tensor_tensor(Md[0:TS, TP:T], Mb[0:TS, TP:T], cf[0:TS, C_STRI:C_STRI + TS], ALU.add).then_inc(l_md, 1)

            stabilisers(0)
            for h in range(LH):
                for s in range(NTT):
                    dve.wait_ge(l_S, NTT * h + (s + 1 if s != 2 else 4))
                    dve.wait_ge(l_D, NTT * h + s + 1)
                    bank, o = (2, 0) if s == 0 else (3, 0) if s == 1 else (4, 0) if s == 2 else (4, 256) if s == 3 else (5, 0)
                    w, n = (SO[s + 1] - SO[s], P) if s < 4 else (TS, TS)
                    dve.tensor_tensor(SD[0:n, SO[s]:SO[s] + w], ps[0:n, bank, o:o + w], Dm[0:n, SO[s]:SO[s] + w],
                                      ALU.mult).then_inc(l_SD, 1)
                dve.wait_ge(l_dec, h + 1)
                link(dve.tensor_tensor(qd[:, :], qT[:, h, TP:T], Mb[:, T:T + TS], ALU.mult))
                dve.tensor_tensor(qn[:, 0:TS].rearrange("p (b t) -> p b t", t=TB),
                                  qd[:, :].rearrange("p (b t) -> p b t", t=TB), nTh(h).to_broadcast([P, NB, TB]),
                                  ALU.mult).then_inc(l_qn, 1)
                ks = kt[0:TS, 4, h, :].rearrange("p (a d) -> p a d", a=1).to_broadcast([TS, NB, DK])
                ws = Wm[0:TS, h, :].rearrange("p (b a) -> p b a", a=1).to_broadcast([TS, NB, DK])
                dve.tensor_tensor(kwb[0:TS, :, :], ks, ws, ALU.mult).then_inc(l_kwb, 1)
                dve.wait_ge(l_C, 16 * (h + 1))
                link(dve.tensor_copy(Cb[:, :, DV:DV + 1], nTh(h)))
                for b in range(NB):
                    if b == 4:
                        if h:
                            dve.wait_ge(l_cost, 16 * h)
                        dve.wait_ge(l_cp, h + 1)
                        dve.tensor_copy(Co[:, :], ps[:, 2, 0:DV + 1]).then_inc(l_co, 1)
                        dve.wait_ge(l_co, 2 * h + 1)
                        dve.tensor_copy(nP[:, h:h + 1], Co[:, DV:DV + 1]).then_inc(l_co, 1)
                    dve.wait_ge(l_cs, NB * h + b + 1)
                    dve.scalar_tensor_tensor(out=Cb[:, b, :], in0=Cb[:, b, :], scalar=Mb[:, T + TS + b:T + TS + b + 1],
                                             in1=ps[:, 3 + b % 2, 0:DV + 1], op0=ALU.mult, op1=ALU.add).then_inc(l_cn, 1)
                dve.wait_ge(l_cn, NB * (h + 1))
                link(dve.tensor_copy(nTh(h), Cb[:, :, DV:DV + 1]))
                dve.wait_ge(l_ss, h + 1)
                link(dve.tensor_copy(den[:, 0:10], ps[:, 1, 300:310]))
                link(dve.scalar_tensor_tensor(out=den[:, 0:5], in0=den[:, 0:5], scalar=-1.0, in1=den[:, 0:5],
                                              op0=ALU.mult, op1=ALU.max))
                eh = eC[:, :].rearrange("p (s h) -> p s h", h=LH)[:, :, h:h + 1]
                link(dve.tensor_tensor(den[:, 0:5].rearrange("p (s a) -> p s a", a=1),
                                       den[:, 0:5].rearrange("p (s a) -> p s a", a=1), eh, ALU.max))
                link(dve.reciprocal(den[:, 0:5], den[:, 0:5]))
                link(dve.tensor_tensor(den[:, 5:10], den[:, 5:10], den[:, 0:5], ALU.mult))
                link(dve.tensor_tensor(den[:, 5:10], den[:, 5:10], den[:, 0:5], ALU.mult))
                dve.tensor_scalar(den[:, 5:10], den[:, 5:10], 1.0 / DV, EPS, ALU.mult, ALU.add).then_inc(l_v, 1)
                dve.wait_ge(l_rs, h + 2)
                dve.tensor_tensor(den[:, 0:5], den[:, 0:5], den[:, 10:15], ALU.mult).then_inc(l_gc, 1)
                dve.wait_ge(l_gb, 2 * h + 2)
                dve.tensor_copy(r[:, :], flat(0, T)).then_inc(l_rc, 1)
                dve.wait_ge(l_rc, h + 1)
                if h == 0:
                    dve.wait_ge(o_sig, 8)
                else:
                    dve.wait_ge(l_lo, 2 * h)
                for c in (0, 1):
                    gcol = gn[:, GCOL["head"] + 2 * h + c:GCOL["head"] + 2 * h + c + 1]
                    dve.wait_ge(l_sq, 3 * h + 3)
                    dve.scalar_tensor_tensor(out=RX[:, c, 0:TP], in0=ps[:, 6 + c, :], scalar=gcol, in1=r[:, 0:TP],
                                             op0=ALU.mult, op1=ALU.mult)
                    dve.scalar_tensor_tensor(out=RX[:, c, TP:T], in0=ps[:, 5, P + c * TS:P + (c + 1) * TS], scalar=gcol,
                                             in1=r[:, TP:T], op0=ALU.mult, op1=ALU.mult).then_inc(l_out, 1)
                if h < LH - 1:
                    stabilisers(h + 1)
                dve.wait_ge(l_out, 2 * h + 2)
                for c in (0, 1):
                    dve.tensor_tensor(RX[:, c, :], RX[:, c, :], so[:, 2 * h + c, :], ALU.mult).then_inc(l_rx, 1)
            dve.memset(den[:, 0:1], 0.0).then_inc(l_nt, 1)
            dve.wait_ge(l_nt, 2)
            dve.tensor_copy(nrow[0:LH, :], ps[0:LH, 0, 0:P]).then_inc(l_nc, 1)
            dve.tensor_copy(nst[:, :], ps[0:NB * LH, 0, P:2 * P]).then_inc(l_nc, 1)
            dve.wait_ge(l_cost, 16 * LH)
            dve.wait_ge(l_cst, 16 * LH)
            dve.wait_ge(stored, 16 * (2 * NTT + 4))
            added("mlstm_out", "ffb1")

        def mlstm_pes(pe, v, products, sums, broadcast, tiles, xgh, xgl):
            mm, tr = nc.tensor.matmul, nc.tensor.transpose
            pe.wait_ge(tile_taken, GT - 1)
            products(GP, 0, 8, xgh, xgl, slot(GT), waits=lambda n: pe.wait_ge(xg_ready, XG["mix1"] + n + 1))
            sums(8)
            tiles("mlstm_in", 8, 1, xgh, xgl, 6, 4, at0={4: broadcast})
            pe.wait_ge(g_dve, 3)
            pe.wait_ge(m_ready, 1)
            pe.wait_ge(tile_taken, IT + 24)
            for o, src in ((0, RA), (20, RD)):
                for j in range(NTT):
                    n = P if j < 4 else TS
                    tr(ps[0:n, 4, o + 4 * j:o + 4 * j + 4], src[0:LH, j * P:j * P + n], ident[0:LH, 0:LH])
            tr(ps[0:TS, 4, 40:44], RE[0:LH, 0:TS], ident[0:LH, 0:LH])
            for h in range(LH):
                mm(ps[:, 4, 44 + h:45 + h], cf[0:LH, C_SEL + h * P:C_SEL + (h + 1) * P], RB[0:LH, TP - 1:TP],
                   start=True, stop=True)
            pe.wait_ge(st_ready, 64)
            tr(ps[:, 4, 64:96], nst0[:, :], ident[0:NB * LH, 0:NB * LH]).then_inc(ct2, 1)
            for j in range(NTT):
                n = P if j < 4 else TS
                for q in range(3):
                    if j:
                        pe.wait_ge(kv_c, 3 * (j - 1) + q + 1)
                    for e in range(4):
                        src = kT[:, e, :] if q == 0 else vT[:, 4 * (q - 1) + e, :]
                        ins = tr(ps[0:n, 5 + q, e * P:(e + 1) * P], src[:, j * P:j * P + n], ident)
                    ins.then_inc(kv_t, 1)
            pe.wait_ge(kv_c, 3 * NTT)
            def stabilisers(h):
                sel = cf[0:LH, C_SEL + h * P:C_SEL + (h + 1) * P]
                mm(ps[:, 0, :], sel, RB[0:LH, 0:TP], start=True, stop=True)
                mm(ps[:, 1, 0:TS], sel, RB[0:LH, TP:T], start=True, stop=True)
                mm(ps[:, 1, TS:2 * TS + NB], sel, RE[0:LH, TS:2 * TS + NB], start=True, stop=True).then_inc(l_gb, 1)

            def scores(h):
                for s in range(4):
                    bank, o = [(2, 0), (3, 0), (4, 0), (4, 256)][s]
                    mm(ps[:, bank, o:o + TP - s * P], kT[:, h, s * P:(s + 1) * P], qT[:, h, s * P:TP],
                       start=True, stop=True).then_inc(l_S, 1)

            def states(h, b):
                if b >= 2:
                    pe.wait_ge(l_cn, NB * h + b - 1)
                mm(ps[:, 3 + b % 2, 0:DV + 1], kwb[0:TS, b, :], Vt[0:TS, 4, h, :], start=True, stop=True).then_inc(l_cs, 1)

            def squares(j):
                for c in (0, 1):
                    ins = mm(ps[:, 1, 305 + j:306 + j], sqn[:, c, j * P:(j + 1) * P], ones[:, 0:1], start=c == 0, stop=c == 1)
                return ins

            stabilisers(0)
            scores(0)
            for h in range(LH):
                if h:
                    pe.wait_ge(l_out, 2 * h)
                mm(ps[0:TS, 5, 0:TS], kT[:, h, TP:T], qT[:, h, TP:T], start=True, stop=True).then_inc(l_S, 1)
                pe.wait_ge(l_SD, NTT * (h + 1))
                for c in (0, 1):
                    for s in range(4):
                        ins = mm(ps[:, 6 + c, s * P:TP], Vt[:, s, h, c * P:(c + 1) * P], SD[:, SO[s]:SO[s + 1]],
                                 start=s == 0, stop=s == 3)
                    ins.then_inc(l_num, 1)
                pe.wait_ge(l_qn, h + 1)
                pe.wait_ge(l_C, 16 * (h + 1))
                for c in (0, 1):
                    o = P + c * TS
                    mm(ps[:, 5, o:o + TS], Vt[0:TS, 4, h, c * P:(c + 1) * P], SD[0:TS, 1280:1280 + TS], start=True, stop=False)
                    for b in range(NB):
                        ins = mm(ps[:, 5, o + b * TB:o + (b + 1) * TB], Cb[:, b, c * P:(c + 1) * P],
                                 qd[:, b * TB:(b + 1) * TB], start=False, stop=b == NB - 1)
                ins.then_inc(l_num, 1)
                pe.wait_ge(l_kwb, h + 1)
                states(h, 0)
                states(h, 1)
                pe.wait_ge(l_mb, h + 1)
                for j in range(NTT):
                    for s in range(j + 1 if j < 4 else 0):
                        mm(ps[:, 1, 300 + j:301 + j], SD[:, SO[s] + (j - s) * P:SO[s] + (j - s + 1) * P], ones[:, 0:1],
                           start=s == 0, stop=s == j)
                mm(ps[:, 1, 304:305], SD[0:TS, 1280:1280 + P], ones[0:TS, 0:1], start=True, stop=False)
                mm(ps[:, 1, 304:305], qn[:, :], ones[:, 0:1], start=False, stop=True)
                states(h, 2)
                states(h, 3)
                pe.wait_ge(l_kw, h + 1)
                for s in range(4):
                    ins = mm(ps[:, 2, 0:DV + 1], kw[:, s, :], Vt[:, s, h, :], start=s == 0, stop=s == 3)
                ins.then_inc(l_cp, 1)
                states(h, 4)
                states(h, 5)
                pe.wait_ge(l_sq, 3 * (h + 1))
                squares(0)
                squares(1)
                states(h, 6)
                states(h, 7)
                squares(2)
                squares(3)
                squares(4).then_inc(l_ss, 1)
                if h < LH - 1:
                    pe.wait_ge(l_cn, NB * (h + 1))
                    pe.wait_ge(l_co, 2 * h + 2)
                    scores(h + 1)
                pe.wait_ge(l_gc, h + 1)
                for j in range(NTT):
                    w = P if j < 4 else TS
                    ins = mm(flat(0, T)[:, j * P:j * P + w], den[:, j:j + 1].to_broadcast([P, P]), ident[:, 0:w],
                             start=True, stop=True)
                ins.then_inc(l_gb, 1)
                if h < LH - 1:
                    pe.wait_ge(l_rc, h + 1)
                    stabilisers(h + 1)
            pe.wait_ge(l_nt, 1)
            pe.wait_ge(l_co, 2 * LH)
            tr(ps[0:LH, 0, 0:P], nP[:, :], ident)
            tr(ps[0:NB * LH, 0, P:2 * P], nT[:, :], ident).then_inc(l_nt, 1)
            pe.wait_ge(l_nc, 2)
            pe.wait_ge(l_lo, 2 * LH)
            tiles("mlstm_out", 8, 1, lambda n: gTh[:, n, :], lambda n: gTl[:, n, :], 2, 4)


        mixer_loads, mixer_lowers = [mla_loads, mlstm_loads], [mla_lowers, mlstm_lowers]
        mixer_acts, mixer_dves, mixer_pes = [mla_acts, mlstm_acts], [mla_dves, mlstm_dves], [mla_pes, mlstm_pes]

        xr = [I["x_prompt"][0, j * P:(j + 1) * P, :] for j in range(4)] + [I["x_sample"].rearrange("b t d -> (b t) d")]

        block = ctx.enter_context(nc.Block())
        @block.sync
        def _(sp):
            def load(p, dyn, parts, free=True):
                s = p % RAW
                if free:
                    sp.wait_ge(wlo_ready, p - RAW - 7 + dyn)
                for dst, src, inc in parts(raw[:, s, :, :]):
                    sp.dma_start(dst, src).then_inc(raw_ready[s], inc)

            def ffn_in(name, w):
                v = w.rearrange("(c p) n -> p c n", p=P)
                p0 = P0[name]

                def pair(i, k, dyn, free=True):
                    for half_ in (0, 1):
                        col = half_ * FF + (i * 2 + k) * P
                        load(p0 + 2 * k + half_, dyn, lambda d: [(d, v[:, :, bass.ds(col, P)], UNIT)], free)
                if p0 == 8:
                    pair(0, 0, 0, False)
                    pair(0, 1, 0, False)
                with sp.Fori(1 if p0 == 8 else 0, NC_F // 2) as i:
                    for k in (0, 1):
                        pair(i, k, i * 4)

            def ffn_out(name, w):
                v = w.rearrange("(c p) n -> p c n", p=P)
                with sp.Fori(0, NC_D // 2) as i:
                    for k in (0, 1):
                        for q, (a, b) in enumerate(FF_PARTS):
                            load(P0[name] + 4 * k + q, i * 8,
                                 lambda d: [(d[:, 0:b - a, :], v[:, a:b, bass.ds((i * 2 + k) * P, P)], UNIT)])

            def ple(l):
                p0 = P0[f"ple{l}"]
                g = I["w_ple_gate"][l].rearrange("(c p) n -> p c n", p=P)
                w = I["w_ple_proj"][l].rearrange("(c p) n -> p c n", p=P)

                def gate(p, c, dyn):
                    load(p, dyn, lambda d: [(d, g[:, :, bass.ds(c * P, P)], UNIT)])

                def proj(p, c, dyn):
                    load(p, dyn, lambda d: [(d[:, 0:2, :], w[:, :, bass.ds(c * P, P)], UNIT)])
                gate(p0, 0, 0)
                gate(p0 + 1, 1, 0)
                proj(p0 + 2, 0, 0)
                with sp.Fori(0, 3) as i:
                    for k in (0, 1):
                        gate(p0 + 3 + 2 * k, i * 2 + 2 + k, i * 4)
                        proj(p0 + 4 + 2 * k, i * 2 + 1 + k, i * 4)
                proj(p0 + 15, 7, 0)

            sp.dma_start(gn[:, :], I["gains"]).then_inc(gn_ready, 16)
            for j in range(NTT):
                sp.dma_start(xin[0:(P if j < 4 else TS), j, 512:1024], xr[j][:, 512:1024]).then_inc(in_ready[1], 16)
            for l in (0, 1):
                ffn_in(f"ffa{l}_in", I["w_ffa_in"][l])
                ffn_out(f"ffa{l}_out", I["w_ffa_out"][l])
                mixer_loads[l](sp, load)
                ffn_in(f"ffb{l}_in", I["w_ffb_in"][l])
                ffn_out(f"ffb{l}_out", I["w_ffb_out"][l])
                ple(l)
            for j in range(NTT):
                dst = outs["y_prompt"][0, j * P:(j + 1) * P, :] if j < 4 else \
                    outs["y_sample"].rearrange("b t d -> (b t) d")
                for q, y_row in enumerate((y_act, y_dve)):
                    sp.wait_ge(y_row, j + 1)
                    sp.dma_start(dst[:, q * 512:(q + 1) * 512],
                                 xin[0:(P if j < 4 else TS), j, q * 512:(q + 1) * 512]).then_inc(stored, 16)
            sp.wait_ge(stored, 16 * (2 * NTT + 4 + 2 * NTT))

        @block.gpsimd
        def _(pool):
            def lower(p, dyn, n, place=None):
                hi, lo = place or (whi[:, p % SPLIT, :, :], wlo[:, p % SPLIT, :, :])
                pool.wait_ge(whi_ready, p - 7 + dyn)
                pool.tensor_tensor(lo[:, 0:n, :], raw[:, p % RAW, 0:n, :], hi[:, 0:n, :].bitcast(F32),
                                   ALU.subtract).then_inc(wlo_ready, 1)

            def stage(name, counts, iters):
                with pool.Fori(0, iters) as i:
                    for k, n in enumerate(counts):
                        lower(P0[name] + k, i * len(counts), n)

            sizes = [b - a for a, b in FF_PARTS]
            for l in (0, 1):
                stage(f"ffa{l}_in", [8] * 4, 11)
                stage(f"ffa{l}_out", sizes * 2, 4)
                mixer_lowers[l](pool, lower, stage)
                stage(f"ffb{l}_in", [8] * 4, 11)
                stage(f"ffb{l}_out", sizes * 2, 4)
                p0 = P0[f"ple{l}"]
                lower(p0, 0, 8)
                lower(p0 + 1, 0, 8)
                lower(p0 + 2, 0, 2, ple_split(l, 0, True))
                with pool.Fori(0, 3) as i:
                    for k in (0, 1):
                        lower(p0 + 3 + 2 * k, i * 4, 8, ple_split(l, 2 + k, False))
                        lower(p0 + 4 + 2 * k, i * 4, 2, ple_split(l, 1 + k, True))
                lower(p0 + 15, 0, 2, ple_split(l, 7, True))

        @block.scalar
        def _(act):
            act.dma_start(cf[:, 0:C_ROPE], I["cf"][:, 0:C_ROPE]).then_inc(id_ready, 16)
            for j in range(NTT):
                act.dma_start(xin[0:(P if j < 4 else TS), j, 0:512], xr[j][:, 0:512]).then_inc(in_ready[0], 16)
            act.dma_start(cf[:, C_ROPE:], I["cf"][:, C_ROPE:]).then_inc(consts_ready, 16)
            act.dma_start(cbf[:, :], I["cb"]).then_inc(consts_ready, 16)

            def upper(p, dyn, n, place=None, back=1):
                hi = place[0] if place else whi[:, p % SPLIT, :, :]
                act.wait_ge(raw_ready[p % RAW], UNIT * (p // RAW - 1) + dyn * (UNIT // RAW))
                act.wait_ge(panel_used, p - back + dyn)
                act.activation(hi[:, 0:n, :], raw[:, p % RAW, 0:n, :], ACT.Copy).then_inc(whi_ready, 1)

            def root(n, width):
                act.wait_ge(ss_ready, n + 1)
                act.activation(sd[:, 0:NTT], ps[:, 5, 100:100 + NTT], ACT.Sqrt, bias=eps[:, 0:1],
                               scale=1.0 / width).then_inc(sd_ready, 1)

            def ffn_in(name, norm):
                p0, t0 = P0[name], T0[name]

                def pair(k, dyn, first):
                    upper(p0 + 2 * k + 1, dyn, 8)
                    if first:
                        root(norm, D)
                    upper(p0 + 2 * k + 2, dyn, 8)
                    act.wait_ge(tile_taken, t0 + 2 * k + 1 + dyn)
                    act.activation(sA[:, :], tA[:, :], ACT.Silu).then_inc(silu_done, 1)
                pair(0, 0, True)
                pair(1, 0, False)
                with act.Fori(1, NC_F // 2) as i:
                    for k in (0, 1):
                        pair(k, i * 4, False)

            def ffn_out(name):
                sizes = [b - a for a, b in FF_PARTS]
                nxt = (sizes * 2)[1:] + [8]
                with act.Fori(0, NC_D // 2) as i:
                    for k in range(8):
                        upper(P0[name] + 1 + k, i * 8, nxt[k])

            def square(name, n):
                with act.Fori(0, 2) as i:
                    for k in range(4):
                        upper(P0[name] + 1 + k, i * 4, n if k < 3 else 8)

            act.wait_ge(zeroed, 2)
            for c in range(NC_D):
                act.wait_ge(x_turned, c + 1)
                act.activation(x[:, c, :], flat(4 + 2 * (c % 2), T), ACT.Copy).then_inc(x_taken, 1)
                act.wait_ge(x_taken, c + 1)
                if c >= 2:
                    act.wait_ge(acc_done, c - 1)
                act.activation((tA, sA)[c % 2][:, :], x[:, c, :], ACT.Square).then_inc(x_sq, 1)
                if c == 0:
                    upper(8, 0, 8)
            norm = 0
            for l in (0, 1):
                ffn_in(f"ffa{l}_in", norm); norm += 1
                ffn_out(f"ffa{l}_out")
                norm = mixer_acts[l](act, upper, root, square, norm)
                ffn_in(f"ffb{l}_in", norm); norm += 1
                ffn_out(f"ffb{l}_out")
                p0, t0 = P0[f"ple{l}"], T0[f"ple{l}"]
                act.wait_ge(panel_used, p0)
                pr = [I["p_prompt"][l, 0, j * P:(j + 1) * P, :] for j in range(4)] + \
                    [I["p_sample"][l].rearrange("b t d -> (b t) d")]
                for j in range(NTT):
                    act.dma_start(pn[0:(P if j < 4 else TS), j, :], pr[j]).then_inc(p_ready, 16)

                def sigmoid(c, t, dyn):
                    act.wait_ge(tile_taken, t + 1 + dyn)
                    gc = sg[:, bass.ds(c, 1), :]
                    act.activation(gc, gc, ACT.Sigmoid).then_inc(sg_ready, 1)
                upper(p0 + 1, 0, 8)
                root(norm, D); norm += 1
                sigmoid(0, t0, 0)
                upper(p0 + 2, 0, 2, ple_split(l, 0, True))
                upper(p0 + 3, 0, 8, ple_split(l, 2, False), back=2)
                sigmoid(1, t0 + 1, 0)

                def turn(k, dyn, c, last=False):
                    upper(p0 + 4 + 2 * k, dyn, 2, ple_split(l, 1 + k, True), back=3)
                    if last:
                        upper(p0 + 15, 0, 2, ple_split(l, 7, True), back=2)
                    else:
                        upper(p0 + 5 + 2 * k, dyn, 8, ple_split(l, 3 + k, False), back=3)
                    sigmoid(c, t0 + 5 + 2 * k, dyn)
                with act.Fori(0, 2) as i:
                    for k in (0, 1):
                        turn(k, i * 4, i * 2 + 2 + k)
                turn(4, 0, 6)
                turn(5, 0, 7, True)
                for c in range(NC_D if l == 0 else 0):
                    act.wait_ge(panel_used, p0 + 14)
                    act.wait_ge(acc_done, AC["ffa1"] + c + 1)
                    act.activation(xh[:, c, :], x[:, c, :], ACT.Copy,
                                   scale=gn[:, GCOL["ffa1"] + c:GCOL["ffa1"] + c + 1]).then_inc(xh_act, 1)
                    if c == 1:
                        upper(p0 + 16, 0, 8)
            root(norm, D)
            act.wait_ge(rc_ready, norm + 1)
            for j in range(NTT):
                n = P if j < 4 else TS
                act.wait_ge(yt_ready, j + 1 if j < 4 else 9)
                act.activation(xin[0:n, j, 0:512], ps[0:n, 2 * j % 8, :], ACT.Copy, scale=rc[0:n, j:j + 1]).then_inc(y_act, 1)

        @block.vector
        def _(dve):
            v = {"chain": 0, "norm": 0, "dyn": 0}

            def link(ins):
                v["chain"] += 1
                ins.then_inc(chain, 1)
                dve.wait_ge(chain, v["chain"] + v["dyn"])

            def inverse():
                v["norm"] += 1
                dve.wait_ge(sd_ready, v["norm"])
                dve.reciprocal(rc[:, 0:NTT], sd[:, 0:NTT]).then_inc(rc_ready, 1)

            def spread(out):
                dve.wait_ge(rb_ready, v["norm"])
                link(dve.tensor_copy(out[:, :], flat(4, T)))

            def rms(out=r):
                inverse()
                spread(out)

            def square_sum(xf, name, k, dyn, cl, cdyn):
                dve.tensor_tensor(sq[:, :], xf, xf, ALU.mult).then_inc(chain, 1)
                dve.wait_ge(chain, cl + 1 + cdyn)
                dve.wait_ge(acc_done, AC[name] + k + dyn)
                dve.tensor_tensor(acc[:, 0:T], acc[:, 0:T], sq[:, :], ALU.add).then_inc(acc_done, 1)

            def lower_split(xf, c, name):
                hc = xh[:, bass.ds(c, 1), :].rearrange("p a t -> p (a t)")
                lc = xl[:, bass.ds(c, 1), :].rearrange("p a t -> p (a t)")
                dve.scalar_tensor_tensor(out=lc, in0=xf, scalar=gn[:, bass.ds(c + GCOL[name], 1)], in1=hc.bitcast(F32),
                                         op0=ALU.mult, op1=ALU.subtract).then_inc(xg_ready, 1)

            def after_x(xf, c, name, dyn, k, cdyn, cl):
                hc = xh[:, bass.ds(c, 1), :].rearrange("p a t -> p (a t)")
                dve.tensor_scalar(hc, xf, gn[:, bass.ds(c + GCOL[name], 1)], None, ALU.mult).then_inc(chain, 1)
                dve.wait_ge(chain, cl + 1 + cdyn)
                lower_split(xf, c, name)
                square_sum(xf, name, k, dyn, cl + 1, cdyn)

            def clear_acc():
                link(dve.memset(acc[:, 0:T], 0.0))

            def chunks(t0, name, tiles_ready, update):
                clear_acc()
                links = 2
                c0 = v["chain"]
                with dve.Fori(0, NC_D // 2) as i:
                    for k in (0, 1):
                        c = i * 2 + k
                        tiles_ready(i, k)
                        xf = x[:, bass.ds(c, 1), :].rearrange("p a t -> p (a t)")
                        update(xf, t0 + k)
                        dve.wait_ge(tile_taken, t0 + k + 1 + i * 2)
                        after_x(xf, c, name, i * 2, k, i * (2 * links), c0 + k * links)
                v["chain"] += 8 * links

            def ffn_in(name, ubase):
                p0, t0 = P0[name], T0[name]
                c0 = v["chain"]
                with dve.Fori(0, NC_F // 2) as i:
                    for k in (0, 1):
                        pa, ta, j, cl = p0 + 2 * k, t0 + 2 * k, i * 2 + k, c0 + 2 * k
                        dve.wait_ge(panel_used, pa + 1 + i * 4)
                        dve.tensor_tensor(half(tA[:, :]), slot(ta), half(r[:, :]), ALU.mult).then_inc(tile_taken, 1)
                        dve.wait_ge(silu_done, ubase + k + 1 + i * 2)
                        dve.tensor_tensor(sA[:, :], sA[:, :], r[:, :], ALU.mult).then_inc(chain, 1)
                        dve.wait_ge(panel_used, pa + 2 + i * 4)
                        dve.wait_ge(chain, cl + 1 + i * 4)
                        dve.tensor_tensor(half(ub[:, :]), slot(ta + 1), half(sA[:, :]), ALU.mult).then_inc(tile_taken, 1)
                        dve.wait_ge(tile_taken, ta + 2 + i * 4)
                        hj = uh[:, bass.ds(j, 1), :].rearrange("p a t -> p (a t)")
                        lj = ul[:, bass.ds(j, 1), :].rearrange("p a t -> p (a t)")
                        dve.tensor_copy(hj, ub[:, :]).then_inc(chain, 1)
                        dve.wait_ge(chain, cl + 2 + i * 4)
                        dve.tensor_tensor(lj, ub[:, :], hj.bitcast(F32), ALU.subtract).then_inc(u_ready, 1)
                v["chain"] += NC_F * 2

            def ffn_out(name, nxt):
                def ready(i, k):
                    dve.wait_ge(panel_used, P0[name] + 4 * (k + 1) + i * 8)

                def update(xf, t):
                    dve.scalar_tensor_tensor(out=half(xf), in0=slot(t), scalar=0.5, in1=half(xf),
                                             op0=ALU.mult, op1=ALU.add).then_inc(tile_taken, 1)
                chunks(T0[name], nxt, ready, update)

            def added(name, nxt):
                def ready(i, k):
                    dve.wait_ge(panel_used, P0[name] + k + 1 + i * 2)

                def update(xf, t):
                    dve.tensor_tensor(half(xf), slot(t), half(xf), ALU.add).then_inc(tile_taken, 1)
                chunks(T0[name], nxt, ready, update)

            def ple(l, nxt):
                p0, t0 = P0[f"ple{l}"], T0[f"ple{l}"]
                links = 2
                clear_acc()

                def gate(c, p, t, dyn):
                    dve.wait_ge(panel_used, p + 1 + dyn)
                    gc = sg[:, bass.ds(c, 1), :].rearrange("p a t -> p (a t)")
                    dve.tensor_tensor(half(gc), slot(t), half(r[:, :]), ALU.mult).then_inc(tile_taken, 1)

                def proj(c, k, kdyn, p, t, dyn, cl, cdyn):
                    dve.wait_ge(panel_used, p + 1 + dyn)
                    dve.wait_ge(sg_ready, 8 * l + k + 1 + kdyn)
                    gc = sg[:, bass.ds(c, 1), :].rearrange("p a t -> p (a t)")
                    xf = x[:, bass.ds(c, 1), :].rearrange("p a t -> p (a t)")
                    dve.tensor_tensor(half(ub[:, :]), slot(t), half(gc), ALU.mult).then_inc(chain, 1)
                    dve.wait_ge(chain, cl + 1 + cdyn)
                    dve.tensor_tensor(xf, ub[:, :], xf, ALU.add).then_inc(tile_taken, 1)
                    dve.wait_ge(tile_taken, t + 1 + dyn)
                    if l == 1:
                        yc = yT[:, bass.ds(c, 1), :].rearrange("p a t -> p (a t)")
                        dve.tensor_scalar(yc, xf, gn[:, bass.ds(c + GCOL[nxt], 1)], None, ALU.mult).then_inc(y_ready, 1)
                    square_sum(xf, nxt, k, kdyn, cl + 1, cdyn)

                def lowers(chunks_):
                    for c in chunks_ if l == 0 else ():
                        dve.wait_ge(xh_act, c + 1)
                        lower_split(x[:, c, :], c, nxt)
                gate(0, p0, t0, 0)
                gate(1, p0 + 1, t0 + 1, 0)
                for c in (0, 1):
                    dve.wait_ge(pt_ready, 2 * l + c + 1)
                    b = 2 * ((t0 + 2 + c) % 2)
                    link(dve.tensor_copy(pth[:, c, :], flat(b, T)))
                    dve.tensor_tensor(ptl[:, c, :], flat(b, T), pth[:, c, :].bitcast(F32),
                                      ALU.subtract).then_inc(tile_taken, 1)
                c0 = v["chain"]
                proj(0, 0, 0, p0 + 2, t0 + 4, 0, c0, 0)
                with dve.Fori(0, 3) as i:
                    for k in (0, 1):
                        gate(i * 2 + 2 + k, p0 + 3 + 2 * k, t0 + 5 + 2 * k, i * 4)
                        proj(i * 2 + 1 + k, 1 + k, i * 2, p0 + 4 + 2 * k, t0 + 6 + 2 * k, i * 4,
                             c0 + (1 + k) * links, i * (2 * links))
                lowers(range(0, 3))
                proj(7, 7, 0, p0 + 15, t0 + 17, 0, c0 + 7 * links, 0)
                lowers(range(3, NC_D))
                v["chain"] += 8 * links

            dve.memset(eps[:, :], EPS).then_inc(zeroed, 1)
            dve.memset(acc[:, :], 0.0).then_inc(zeroed, 1)
            dve.wait_ge(zeroed, 2)
            dve.wait_ge(gn_ready, 16)
            for c in range(NC_D):
                dve.wait_ge(x_taken, c + 1)
                g = gn[:, c:c + 1]
                dve.tensor_scalar(xh[:, c, :], x[:, c, :], g, None, ALU.mult).then_inc(tile_taken, 1)
                dve.wait_ge(tile_taken, c + 1)
                dve.scalar_tensor_tensor(out=xl[:, c, :], in0=x[:, c, :], scalar=g, in1=xh[:, c, :].bitcast(F32),
                                         op0=ALU.mult, op1=ALU.subtract).then_inc(xg_ready, 1)
                dve.wait_ge(x_sq, c + 1)
                if c:
                    dve.wait_ge(acc_done, c)
                dve.tensor_tensor(acc[:, 0:T], acc[:, 0:T], (tA, sA)[c % 2][:, :], ALU.add).then_inc(acc_done, 1)
            dve.wait_ge(consts_ready, 32)
            link(dve.tensor_copy(cb[:, :], cbf[:, :]))
            for l in (0, 1):
                rms()
                ffn_in(f"ffa{l}_in", 44 * l)
                ffn_out(f"ffa{l}_out", f"mix{l}")
                mixer_dves[l](dve, v, link, rms, inverse, spread, added)
                rms()
                ffn_in(f"ffb{l}_in", 44 * l + 22)
                ffn_out(f"ffb{l}_out", f"ple{l}")
                rms()
                ple(l, "ffa1" if l == 0 else "final")
            dve.wait_ge(sd_ready, v["norm"] + 1)
            dve.reciprocal(rc[:, 0:NTT], sd[:, 0:NTT]).then_inc(rc_ready, 1)
            dve.wait_ge(rc_ready, v["norm"] + 1)
            for j in range(NTT):
                n = P if j < 4 else TS
                dve.wait_ge(yt_ready, j + 5 if j < 4 else 10)
                dve.tensor_scalar(xin[0:n, j, 512:1024], ps[0:n, (2 * j + 1) % 8, :], rc[0:n, j:j + 1], None,
                                  ALU.mult).then_inc(y_dve, 1)

        @block.tensor
        def _(pe):
            mm = nc.tensor.matmul
            v = {"norm": 0, "acc": 0}

            def products(p, dyn, n_chunks, mh, ml, out, first=True, last=True, waits=None, at=None, place=None):
                hi, lo = place or (whi[:, p % SPLIT, :, :], wlo[:, p % SPLIT, :, :])
                pe.wait_ge(whi_ready, p - 7 + dyn)
                pe.wait_ge(wlo_ready, p - 7 + dyn)
                for n in range(n_chunks):
                    if at and n in at:
                        at[n]()
                    if waits:
                        waits(n)
                    h0, l0 = half(mh(n)), half(ml(n))
                    for q in (0, 1):
                        mm(out[:, q, :], hi[:, n, :], h0[:, q, :], start=first and n == 0, stop=False)
                    for q in (0, 1):
                        mm(out[:, q, :], hi[:, n, :], l0[:, q, :], start=False, stop=False)
                    end = last and n == n_chunks - 1
                    for q in (0, 1):
                        ins = mm(out[:, q, :], lo[:, n, :], h0[:, q, :], start=False, stop=end)
                ins.then_inc(panel_used, 1)

            def sums(n_acc):
                v["acc"] += n_acc
                pe.wait_ge(acc_done, v["acc"])
                for j in range(NTT):
                    ins = mm(ps[:, 5, 100 + j:101 + j], acc[:, j * P:(j + 1) * P], ones[:, 0:1], start=True, stop=True)
                ins.then_inc(ss_ready, 1)

            def broadcast():
                n = v["norm"]; v["norm"] += 1
                pe.wait_ge(rc_ready, n + 1)
                for j in range(NTT):
                    w = P if j < 4 else TS
                    ins = mm(flat(4, T)[:, j * P:j * P + w], rc[:, j:j + 1].to_broadcast([P, P]), ident[:, 0:w],
                             start=True, stop=True)
                ins.then_inc(rb_ready, 1)

            def tiles(name, n_chunks, per_tile, mh, ml, iters, per, xg0=None, at0=None):
                def tile(k, dyn, waits=None, at=None):
                    if waits is not turned:
                        pe.wait_ge(tile_taken, T0[name] + k - 1 + dyn)
                    products(P0[name] + k, dyn, n_chunks, mh, ml, slot(T0[name] + k), waits=waits, at=at)
                if xg0 is not None:
                    tile(0, 0, turned if xg0 == 0 else lambda n: pe.wait_ge(xg_ready, xg0 + n + 1))
                    sums(8)
                    tile(1, 0, at={4: broadcast})
                    for k in range(2, per):
                        tile(k, 0)
                elif at0:
                    for k in range(per):
                        tile(k, 0, at=at0 if k == 0 else None)
                with pe.Fori(0 if xg0 is None and at0 is None else 1, iters) as i:
                    for k in range(per):
                        tile(k, i * per)

            def ffn_out(name, ubase):
                with pe.Fori(0, NC_D // 2) as i:
                    for k in (0, 1):
                        pe.wait_ge(tile_taken, T0[name] + k - 1 + i * 2)
                        for q, (a, b) in enumerate(FF_PARTS):
                            products(P0[name] + 4 * k + q, i * 8, b - a, lambda n: uh[:, a + n, :],
                                     lambda n: ul[:, a + n, :], slot(T0[name] + k), q == 0, q == 3,
                                     (lambda n: pe.wait_ge(u_ready, ubase + a + n + 1)) if k == 0 else None)

            xgh, xgl = (lambda n: xh[:, n, :]), (lambda n: xl[:, n, :])
            pe.wait_ge(id_ready, 16)

            def turn(c):
                pe.wait_ge(in_ready[c // 4], 16 * NTT)
                if c >= 2:
                    pe.wait_ge(x_taken, c - 1)
                for j in range(NTT):
                    n = P if j < 4 else TS
                    ins = nc.tensor.transpose(flat(4 + 2 * (c % 2), T)[:, j * P:j * P + n],
                                              xin[0:n, j, c * P:(c + 1) * P], ident[0:n, 0:n])
                    if c == 0 and j == 0:
                        ins.then_inc(panel_used, NC_D)
                ins.then_inc(x_turned, 1)

            def turned(n):
                if n + 2 < NC_D:
                    turn(n + 2)
                pe.wait_ge(xg_ready, n + 1)
            turn(0)
            turn(1)
            for l in (0, 1):
                tiles(f"ffa{l}_in", 8, 1, xgh, xgl, 11, 4, XG[f"ffa{l}"])
                ffn_out(f"ffa{l}_out", 44 * l)
                mixer_pes[l](pe, v, products, sums, broadcast, tiles, xgh, xgl)
                tiles(f"ffb{l}_in", 8, 1, xgh, xgl, 11, 4, XG[f"ffb{l}"])
                ffn_out(f"ffb{l}_out", 44 * l + 22)
                p0, t0 = P0[f"ple{l}"], T0[f"ple{l}"]

                def gate(c, p, t, dyn, waits=None, at=None):
                    pe.wait_ge(tile_taken, t - 1 + dyn)
                    products(p, dyn, 8, xgh, xgl, slot(t), waits=waits, at=at, place=ple_split(l, c, False))

                def proj(c, p, t, dyn):
                    pe.wait_ge(tile_taken, t - 1 + dyn)
                    products(p, dyn, 2, lambda n: pth[:, n, :], lambda n: ptl[:, n, :], slot(t),
                             place=ple_split(l, c, True))
                gate(0, p0, t0, 0, waits=lambda n: pe.wait_ge(xg_ready, XG[f"ple{l}"] + n + 1))
                sums(8)
                gate(1, p0 + 1, t0 + 1, 0, at={4: broadcast})
                pe.wait_ge(p_ready, 16 * NTT * (l + 1))
                for c in (0, 1):
                    t = t0 + 2 + c
                    pe.wait_ge(tile_taken, t - 1)
                    for j in range(NTT):
                        n = P if j < 4 else TS
                        ins = nc.tensor.transpose(flat(2 * (t % 2), T)[:, j * P:j * P + n],
                                                  pn[0:n, j, c * P:(c + 1) * P], ident[0:n, 0:n])
                    ins.then_inc(pt_ready, 1)
                pe.wait_ge(tile_taken, t0 + 4)
                proj(0, p0 + 2, t0 + 4, 0)
                with pe.Fori(0, 3) as i:
                    for k in (0, 1):
                        gate(2 + k, p0 + 3 + 2 * k, t0 + 5 + 2 * k, i * 4)
                        proj(1 + k, p0 + 4 + 2 * k, t0 + 6 + 2 * k, i * 4)
                proj(7, p0 + 15, t0 + 17, 0)
            pe.wait_ge(tile_taken, T0["ple1"] + 18)
            for q, j in [(0, j) for j in range(4)] + [(1, j) for j in range(4)] + [(0, 4), (1, 4)]:
                n, b = P if j < 4 else TS, (2 * j + q) % 8
                if j == 0:
                    pe.wait_ge(y_ready, 4 * q + 4)
                    if q:
                        sums(8)
                if b == 5:
                    pe.wait_ge(sd_ready, v["norm"] + 1)
                if j == 4:
                    pe.wait_ge((y_act, y_dve)[q], 1)
                for c in range(4):
                    ins = nc.tensor.transpose(ps[0:n, b, c * P:(c + 1) * P], yT[:, 4 * q + c, j * P:j * P + n], ident)
                ins.then_inc(yt_ready, 1)


_INS = ['x_prompt', 'x_sample', 'cache_ckv', 'cache_krope', 'state_C', 'state_n', 'state_m', 'page_table',
        'p_prompt', 'p_sample', 'w_ffa_in', 'w_ffa_out', 'w_ffb_in', 'w_ffb_out', 'w_ple_gate', 'w_ple_proj',
        'w_mla_in', 'w_uq', 'w_uk', 'w_uv', 'w_mla_out', 'w_mlstm_in', 'b_igate', 'b_fgate', 'w_mlstm_out']
_OUTS = [("y_prompt", (1, 512, 1024)), ("y_sample", (8, 8, 1024)), ("ckv_prompt", (1, 1, 512, 256)),
         ("kr_prompt", (1, 1, 512, 32)), ("ckv_sample", (1, 8, 8, 256)), ("kr_sample", (1, 8, 8, 32)),
         ("C_prompt", (1, 1, 4, 128, 256)), ("n_prompt", (1, 1, 4, 128)), ("m_prompt", (1, 1, 4)),
         ("C_sample", (1, 8, 4, 128, 256)), ("n_sample", (1, 8, 4, 128)), ("m_sample", (1, 8, 4))]
_PAST = 2048


def constants():
    cf = np.zeros((P, NCF), np.float32)
    cf[:, C_ID:C_ID + P] = np.eye(P)
    cf[:, C_ONE:C_ONE + 8] = 1.0
    half = ROPE // 2
    inv = (np.float32(10000.0) ** (-np.arange(half, dtype=np.float32) / np.float32(half))).astype(np.float32)
    pos = np.concatenate([np.arange(TP), np.tile(_PAST + np.arange(TB), NB)]).astype(np.float32)
    ang = inv[:, None] * pos[None, :]
    cos, sin = np.cos(ang.astype(np.float64)), np.sin(ang.astype(np.float64))
    cf[64:80, C_ROPE:C_ROPE + T] = cos
    cf[80:96, C_ROPE:C_ROPE + T] = cos
    cf[96:112, C_ROPE:C_ROPE + T] = -sin
    cf[112:128, C_ROPE:C_ROPE + T] = sin
    s = np.arange(TS)
    cf[0:TS, C_BLK:C_BLK + NB] = (s[:, None] // TB == np.arange(NB)[None, :])
    for h in range(LH):
        cf[h, C_SEL + h * P:C_SEL + (h + 1) * P] = 1.0
    k = np.arange(P)
    cf[:, C_TRI:C_TRI + P] = np.where(k[:, None] <= k[None, :], 0.0, -NEG)
    ok = (s[:, None] // TB == s[None, :] // TB) & (s[:, None] <= s[None, :])
    cf[0:TS, C_STRI:C_STRI + TS] = np.where(ok, 0.0, -NEG)
    cb = np.zeros((P, NCB), np.float32)
    cb[:, B_ID:B_ID + P] = np.eye(P)
    cb[:, B_CAUSAL:B_CAUSAL + P] = np.where(k[None, :] <= k[:, None], 0.0, NEG)
    t = np.arange(P) // NH
    for b in range(NB):
        ok = (s[None, :] // TB == b) & (s[None, :] % TB <= t[:, None])
        cb[:, B_SAMPLE + b * TS:B_SAMPLE + (b + 1) * TS] = np.where(ok, 0.0, NEG)
    return cf, cb


def layout(inputs):
    a = {n: np.ascontiguousarray(inputs[n]) for n in _INS}
    g = np.asarray
    rows = [g(inputs["g_ffa"])[0], g(inputs["g_mix"])[0], g(inputs["g_ffb"])[0], g(inputs["g_ple"])[0],
            g(inputs["g_ffa"])[1], g(inputs["g_mix"])[1], g(inputs["g_ffb"])[1], g(inputs["g_ple"])[1],
            g(inputs["g_final"]), g(inputs["g_mlstm_head"])[0], g(inputs["g_q_lat"])[0], g(inputs["g_kv_lat"])[0]]
    a["gains"] = np.ascontiguousarray(np.concatenate([r.reshape(-1, P) for r in rows]).T)
    a["cf"], a["cb"] = constants()
    return a


def kernel(**inputs):
    import concourse.bacc as _bacc
    from concourse.bass_utils import run_bass_kernel_spmd as _run

    nc = _bacc.Bacc("TRN2", target_bir_lowering=False, num_devices=1)
    arrays, ins, outs = {}, {}, {}
    for name, a in layout(inputs).items():
        arrays[f"in_{name}"] = a
        ins[name] = nc.dram_tensor(f"in_{name}", a.shape, mybir.dt.from_np(a.dtype), kind="ExternalInput").ap()
    for name, shape in _OUTS:
        outs[name] = nc.dram_tensor(f"out_{name}", shape, F32, kind="ExternalOutput").ap()
    hybrid_step(nc, ins, outs)
    got = _run(nc, [arrays], core_ids=[0]).results[0]
    return tuple(got[f"out_{n}"] for n, _ in _OUTS)
```

```python
from contextlib import ExitStack

import numpy as np

import concourse.bass as bass
from concourse import mybir

ACT = mybir.ActivationFunctionType
ALU = mybir.AluOpType
AX = mybir.AxisListType
F32 = mybir.dt.float32
F32R = mybir.dt.float32r
BF16 = mybir.dt.bfloat16

P = 128
D = 1024
NC_D = D // P
FF = 2816
NC_F = FF // P
TP, TS = 512, 64
T = TP + TS
H = T // 2
NB, TB = 8, 8
NTT = 5
EPS = 1e-6
NH, NOPE, ROPE, VD = 16, 64, 32, 64
QR, KR = 384, 256
PAGE, NPG = 128, 16
SCALE = (NOPE + ROPE) ** -0.5
LH, DK, DV = 4, 128, 256
CAP = 15.0
PD = 256
UNIT = 112
RAW, SPLIT = 4, 2
NEG = -1e30
FF_PARTS = [(0, 6), (6, 12), (12, 17), (17, 22)]

GAINS = ["ffa0", "mix0", "ffb0", "ple0", "ffa1", "mix1", "ffb1", "ple1", "final", "head"]
GCOL = {n: i * NC_D for i, n in enumerate(GAINS)}
GCOL["q"], GCOL["kv"] = 80, 83
NG = 85
C_ID, C_ONE, C_ROPE, C_BLK, C_SEL, C_TRI, C_STRI = 0, 128, 136, 712, 720, 1232, 1360
NCF = 1424
B_ID, B_CAUSAL, B_SAMPLE = 0, 128, 256
NCB = 768

STAGES = [("embed", 8, 8)]
for _l in (0, 1):
    STAGES += [(f"ffa{_l}_in", 44, 44), (f"ffa{_l}_out", 32, 8)]
    STAGES += [("mla_in", 6, 6), ("mla_heads", 16, 0), ("mla_out", 8, 8)] if _l == 0 else \
        [("mlstm_gates", 1, 1), ("mlstm_in", 24, 24), ("mlstm_out", 8, 8)]
    STAGES += [(f"ffb{_l}_in", 44, 44), (f"ffb{_l}_out", 32, 8), (f"ple{_l}", 16, 18)]
P0, T0 = {}, {}
_p = _t = 0
for _n, _a, _b in STAGES:
    P0[_n], T0[_n] = _p, _t
    _p, _t = _p + _a, _t + _b
NPANEL = _p


class Region:

    def __init__(self, nc, start, end):
        self.nc, self.start, self.at, self.end = nc, start, start, end

    def put(self, name, shape, dt=F32):
        size = int(np.prod(shape[1:])) * (2 if dt == BF16 else 4)
        t = self.nc.alloc_sbuf_tensor_at(name, shape, dt, offset=self.at)
        self.at += (size + 31) // 32 * 32
        assert self.at <= self.end, (name, self.at, self.end)
        return t


def hybrid_step(nc, ins, outs):
    I = ins
    with ExitStack() as ctx:
        def sem(name):
            return ctx.enter_context(nc.semaphore(name))

        base = (nc.sbuf_base + 31) // 32 * 32
        whole = Region(nc, base, nc.sbuf_top)
        x = whole.put("x", [P, NC_D, T])
        raw = whole.put("raw", [P, RAW, 8, P])
        whi = whole.put("whi", [P, SPLIT, 8, P], F32R)
        wlo = whole.put("wlo", [P, SPLIT, 8, P], F32R)
        acc = whole.put("acc", [P, NTT * P])
        r = whole.put("r", [P, T])
        gn = whole.put("gn", [P, NG])
        cf = whole.put("cf", [P, NCF])
        cb = whole.put("cb", [P, NCB], BF16)
        sd = whole.put("sd", [P, 8])
        rc = whole.put("rc", [P, 8])
        eps = whole.put("eps", [P, 1])
        ptab = nc.alloc_sbuf_tensor_at("ptab", [P, NB * NPG], mybir.dt.int32, offset=whole.at)
        whole.at += 4 * NB * NPG
        m0 = whole.put("m0", [P, NB])
        ident, ones, rope = cf[:, C_ID:C_ID + P], cf[:, C_ONE:C_ONE + 8], cf[:, C_ROPE:C_ROPE + T]
        idb = cb[:, B_ID:B_ID + P]
        X0 = whole.at
        xh = whole.put("xh", [P, NC_D, T], F32R)
        xl = whole.put("xl", [P, NC_D, T], F32R)
        X1 = whole.at
        uh = whole.put("uh", [P, NC_F, T], F32R)
        ul = whole.put("ul", [P, NC_F, T], F32R)
        TMP = whole.at
        tmp = Region(nc, TMP, whole.end)
        tA = tmp.put("tA", [P, T])
        sA = tmp.put("sA", [P, T])
        ub = tmp.put("ub", [P, T])
        sq = tmp.put("sq", [P, T])
        cbf = Region(nc, TMP + 4 * 2 * T, whole.end).put("cbf", [P, NCB])
        pg = Region(nc, X1, TMP)
        sg = pg.put("sg", [P, NC_D, T])
        pn = pg.put("pn", [P, NTT, PD])
        pth = pg.put("pth", [P, 2, T], F32R)
        ptl = pg.put("ptl", [P, 2, T], F32R)
        jhi = pg.put("jhi", [P, SPLIT, 2, P], F32R)
        jlo = pg.put("jlo", [P, SPLIT, 2, P], F32R)
        xin = pg.put("xin", [P, NTT, D])
        yT = pg.put("yT", [P, NC_D, T])
        ps = nc.psum_tensor("ps", [P, 8, 512], F32)
        ps = ctx.enter_context(ps)
        flat = lambda b, n: ps[:, b:b + (n + 511) // 512, :].rearrange("p b n -> p (b n)")[:, 0:n]

        def ple_split(l, c, proj):
            s = c % SPLIT if proj else (P0[f"ple{l}"] + c) % SPLIT
            return (jhi[:, s, :, :], jlo[:, s, :, :]) if proj else (whi[:, s, :, :], wlo[:, s, :, :])

        def half(t):
            return t.rearrange("p (h n) -> p h n", h=2)

        def slot(t):
            return ps[:, 2 * (t % 2):2 * (t % 2) + 2, 0:H]

        raw_ready = [sem(f"raw_ready{s}") for s in range(RAW)]
        whi_ready, wlo_ready = sem("whi_ready"), sem("wlo_ready")
        panel_used = sem("panel_used")
        tile_taken = sem("tile_taken")
        silu_done, u_ready = sem("silu_done"), sem("u_ready")
        xg_ready, acc_done = sem("xg_ready"), sem("acc_done")
        ss_ready, sd_ready, rc_ready = sem("ss_ready"), sem("sd_ready"), sem("rc_ready")
        in_ready, consts_ready, zeroed = [sem("in_ready0"), sem("in_ready1")], sem("consts_ready"), sem("zeroed")
        chain = sem("dve_chain")
        p_ready, pt_ready, sg_ready = sem("p_ready"), sem("pt_ready"), sem("sg_ready")
        y_ready, yt_ready, y_act, y_dve, stored = sem("y_ready"), sem("yt_ready"), sem("y_act"), sem("y_dve"), sem("stored")
        xh_act, gn_ready = sem("xh_act"), sem("gn_ready")
        id_ready, x_turned, x_taken, x_sq = sem("id_ready"), sem("x_turned"), sem("x_taken"), sem("x_sq")

        NORMS = ["ffa0", "mix0", "ffb0", "ple0", "ffa1", "mix1", "ffb1", "ple1", "final"]
        XG = {n: 8 * i for i, n in enumerate(NORMS)}
        AC = {n: 8 * i + (5 if i > 1 else 0) for i, n in enumerate(NORMS)}
        AC["q"] = 16
        mu = Region(nc, X1, TMP)
        oTh = mu.put("oTh", [P, NC_D, T], F32R)
        oTl = mu.put("oTl", [P, NC_D, T], F32R)
        ckv = mu.put("ckv", [P, 2, T])
        krT = mu.put("krT", [P, T])
        QA = mu.put("QA", [P, 3, NB * TB * NH])
        wuv = mu.put("wuv", [P, 2, NH * VD])
        mu1 = Region(nc, mu.at, TMP)
        zc = mu1.put("zc", [P, 6, T])
        cqh = mu1.put("cqh", [P, 3, T], F32R)
        cql = mu1.put("cql", [P, 3, T], F32R)
        Q = mu1.put("Q", [P, 2, T])
        mu2 = Region(nc, X0, X1)
        KEYS = NPG * PAGE + TS
        S = mu2.put("S", [P, 2, KEYS + P - TS])
        KT = mu2.put("KT", [P, 2, 3, 512])
        QAb = mu2.put("QAb", [P, 2, 3, P])
        mx = mu2.put("mx", [P, 2, 8])
        mxx = Region(nc, X0, X1)
        PP = mxx.put("PP", [P, 2, 1280])
        PT = mxx.put("PT", [P, 2, 1280])
        Vp = mxx.put("Vp", [P, 4, P])
        Kp = mxx.put("Kp", [P, 2, TP])
        WT = mxx.put("WT", [P, 2, KR])
        st = mxx.put("st", [P, 2, 12])
        qtmp = mxx.put("qtmp", [P, T])
        pages = Region(nc, mu.at, TMP).put("pages", [P, 2 * NPG, KR + ROPE])
        mt = Region(nc, TMP, whole.end)
        ckt = mt.put("ckt", [P, NTT, KR + ROPE])
        PTs = mt.put("PTs", [P, 2, 512])
        krS = mt.put("krS", [P, TS])
        rl, gql = sA, ub
        QT = [0, P, 3 * P, 6 * P]
        KO = [0, 4 * P, 7 * P, 9 * P]

        cq_ready, ckv_ready, kr_ready = sem("cq_ready"), sem("ckv_ready"), sem("kr_ready")
        ct_ready, ct_taken, wuv_ready = sem("ct_ready"), sem("ct_taken"), sem("wuv_ready")
        kv_ready, k_taken, v_taken, wt_taken = sem("kv_ready"), sem("k_taken"), sem("v_taken"), sem("wt_taken")
        qn_taken, qr_taken = sem("qn_taken"), sem("qr_taken")
        sc_ready, nm_ready, ex_ready, pp_ready = sem("sc_ready"), sem("nm_ready"), sem("ex_ready"), sem("pp_ready")
        qa_ready, qa_taken = sem("qa_ready"), sem("qa_taken")
        tr_ready, tr_act, tr_dve = sem("tr_ready"), sem("tr_act"), sem("tr_dve")
        pv_ready, ov_hi, ov_lo = sem("pv_ready"), sem("ov_hi"), sem("ov_lo")
        pg = [sem(f"page_ready{n}") for n in range(8)]
        kt_ready, kt_act, kt_dve = sem("kt_ready"), sem("kt_act"), sem("kt_dve")
        ss_sc, mx_dve, s_act, qab_ready = sem("sample_scores"), sem("mx_dve"), sem("s_act"), sem("qab_ready")
        sample_negmax, sample_exp, sp_ready = sem("sample_negmax"), sem("sample_exp"), sem("sample_p")
        sample_inv, sp_pool = sem("sample_inv"), sem("sample_p_pool")
        pts_ready, pts_taken, sample_pv = sem("pts_ready"), sem("pts_taken"), sem("sample_pv")
        sample_o_act, sample_o_dve = sem("sample_o_act"), sem("sample_o_dve")
        zq_ready, cqh_act = sem("zq_ready"), sem("cqh_act")
        sample_v_ready, sample_v_hi, sample_v_lo = sem("sample_v_ready"), sem("sample_v_hi"), sem("sample_v_lo")
        PM, PH, PO = P0["mla_in"], P0["mla_heads"], P0["mla_out"]

        def mla_loads(sp, load):
            w = I["w_mla_in"][0].rearrange("(c p) n -> p c n", p=P)
            sp.dma_start(ptab[0:1, :], I["page_table"].rearrange("(a b) n -> a (b n)", a=1)).then_inc(wuv_ready, 16)
            for m in range(5):
                load(PM + m, 0, lambda d: [(d, w[:, :, m * P:(m + 1) * P], UNIT)])
            last = w[:, :, QR + KR - 64:QR + KR + ROPE]
            load(PM + 5, 0, lambda d: [(d[:, :, 0:96], last, 48),
                                       (d[:, :, 96:112], w[:, :, QR + KR + 16:QR + KR + 32], 32),
                                       (d[:, :, 112:128], w[:, :, QR + KR:QR + KR + 16], 32)])
            uq = I["w_uq"][0].rearrange("(c p) h d -> p c (h d)", p=P)
            uk = I["w_uk"][0].rearrange("(c p) h d -> p c (h d)", p=P)

            def head(k, i, first=False):
                h = i * 4 + k
                e = NOPE + ROPE

                def parts(d):
                    out = [(d[:, 0:3, 0:e], uq[:, :, bass.ds(h * e, e)], 32),
                           (d[:, 0:3, 96:112], uq[:, :, bass.ds(h * e + 80, 16)], 16 if k % 2 == 0 else 32),
                           (d[:, 0:3, 112:128], uq[:, :, bass.ds(h * e + 64, 16)], 16 if k % 2 == 0 else 48)]
                    if k % 2 == 0:
                        out.append((d[:, 3:5, :], uk[:, :, bass.ds(h * NOPE, P)], 48))
                    return out
                if not first and k % 2 == 0:
                    sp.wait_ge(panel_used, PH + k - 2 + i * 4)
                load(PH + k, i * 4, parts, free=first or k % 2 == 1)
            for k in range(4):
                head(k, 0, True)
            sp.wait_ge(panel_used, PM + 6)
            sp.wait_ge(u_ready, 22)
            sp.dma_start(wuv[:, :, :], I["w_uv"][0].rearrange("(c p) h d -> p c (h d)", p=P)).then_inc(wuv_ready, 16)

            def page_group(b, g, s):
                sp.wait_ge(wuv_ready, 32)
                for k in range(4):
                    page = sp.value_load(ptab[0:1, bass.ds(b * NPG + 4 * g + k, 1)], min_val=0,
                                         max_val=I["cache_ckv"].shape[1] - 1)
                    q = s * NPG + 4 * g + k
                    sp.dma_start(pages[:, q, 0:KR], I["cache_ckv"][0][bass.ds(page, 1), :, :].rearrange("a k r -> (a k) r")
                                 ).then_inc(pg[s * 4 + g], 16)
                    sp.dma_start(pages[:, q, KR:KR + ROPE],
                                 I["cache_krope"][0][bass.ds(page, 1), :, :].rearrange("a k r -> (a k) r")
                                 ).then_inc(pg[s * 4 + g], 16)
            sp.wait_ge(kr_ready, 1)
            for g in range(3):
                page_group(0, g, 0)
            with sp.Fori(1, 4) as i:
                for k in range(4):
                    head(k, i)
            sp.wait_ge(ct_taken, 2 * NTT)
            for j in range(NTT):
                n = P if j < 4 else TS
                a = outs["ckv_prompt"][0, 0, j * P:(j + 1) * P, :] if j < 4 else outs["ckv_sample"][0].rearrange("b t r -> (b t) r")
                b = outs["kr_prompt"][0, 0, j * P:(j + 1) * P, :] if j < 4 else outs["kr_sample"][0].rearrange("b t r -> (b t) r")
                sp.dma_start(a, ckt[0:n, j, 0:KR]).then_inc(stored, 16)
                sp.dma_start(b, ckt[0:n, j, KR:KR + ROPE]).then_inc(stored, 16)
            wo = I["w_mla_out"][0].rearrange("(c p) n -> p c n", p=P)
            for k in range(4):
                if k % 2 == 0:
                    sp.wait_ge(panel_used, PO + k - 2)
                load(PO + k, 0, lambda d: [(d, wo[:, :, k * P:(k + 1) * P], UNIT)])

            sp.wait_ge(pv_ready, NH)
            sp.wait_ge(qa_taken, 2 * NH // 2)
            for b in range(2):
                for g in range(3 if b == 0 else 0, 4):
                    page_group(b, g, b)
            with sp.Fori(0, 3) as i:
                for s in range(2):
                    for g in range(4):
                        sp.wait_ge(sample_pv, 5 * s + g + 1 + i * 10)
                        page_group(i * 2 + s + 2, g, s)
            for k in range(4, 8):
                load(PO + k, 0, lambda d: [(d, wo[:, :, k * P:(k + 1) * P], UNIT)])

        def mla_lowers(pool, lower, stage):
            for k in range(6):
                lower(PM + k, 0, 8)
            stage("mla_heads", [3] * 4, 4)

            def scale(b, db):
                pool.wait_ge(sample_inv, b + 1 + db)
                pool.tensor_tensor(S[:, b % 2, 512:KEYS], S[:, b % 2, 512:KEYS],
                                   mx[:, b % 2, 7:8].to_broadcast([P, KEYS - 512]), ALU.mult).then_inc(sp_pool, 1)
            lower(PO, 0, 8)
            with pool.Fori(0, NB // 2) as i:
                scale(0, i * 2)
                scale(1, i * 2)
            for k in range(1, 8):
                lower(PO + k, 0, 8)

        def mla_acts(act, upper, root, square, norm):
            for k in range(6):
                upper(PM + 1 + k, 0, 8 if k < 5 else 3)
                if k == 0:
                    root(norm, D); norm += 1
                if k == 4:
                    root(norm, QR, rl); norm += 1
                    for c in range(3):
                        act.wait_ge(zq_ready, c + 1)
                        act.activation(cqh[:, c, :], zc[:, c, :], ACT.Copy).then_inc(cqh_act, 1)
            root(norm, KR, rl); norm += 1

            def softmax_exp(h, dyn, s, banks):
                for n in range(4):
                    act.wait_ge(nm_ready, 4 * h + max(n + 1, 2) + dyn * 4)
                    act.activation(PP[:, s, QT[n]:QT[n] + (n + 1) * P], banks[n], ACT.Exp, bias=st[:, s, n:n + 1],
                                   accum_out=st[:, s, 4 + n:5 + n]).then_inc(ex_ready, 1)

            with act.Fori(0, 4) as i:
                for j in (0, 1):
                    h = 2 * j
                    d4, d2 = i * 4, i * 2
                    upper(PH + 1 + h, i * 4, 3)
                    act.wait_ge(panel_used, PH + h + 1 + d4)
                    act.activation(Q[0:64, 0, :].rearrange("p (h n) -> p h n", h=2), ps[0:64, 0:2, 0:H], ACT.Copy).then_inc(qn_taken, 1)
                    act.wait_ge(kv_ready, 3 * j + 1 + i * 6)
                    act.activation(Kp[0:64, 0, :], ps[0:64, 2, :], ACT.Copy).then_inc(k_taken, 1)
                    act.activation(Kp[0:64, 1, :], ps[64:128, 2, :], ACT.Copy).then_inc(k_taken, 1)
                    upper(PH + 2 + h, i * 4, 3 if j == 0 else 8)
                    act.wait_ge(panel_used, PH + h + 2 + d4)
                    act.activation(Q[0:64, 1, :].rearrange("p (h n) -> p h n", h=2), ps[0:64, 0:2, 0:H], ACT.Copy).then_inc(qn_taken, 1)
                    for hh in (0, 1):
                        softmax_exp(h + hh, d4, hh, score_banks(hh))
                    for hh in (0, 1):
                        act.wait_ge(tr_ready, h + hh + 1 + d4)
                        act.activation(PT[:, hh, 0:512], ps[:, pt_banks[hh][0], :], ACT.Copy).then_inc(tr_act, 1)
                    for hh in (0, 1):
                        act.wait_ge(pv_ready, h + hh + 1 + d4)
                        rows = slice(64 * hh, 64 * hh + 64)
                        act.activation(oTh[rows, bass.ds(i * 2 + j, 1), 0:TP].rearrange("p a t -> p (a t)"),
                                       ps[rows, pv_bank[hh], :], ACT.Copy).then_inc(ov_hi, 1)

            def kt_copy(n, dn):
                act.wait_ge(kt_ready, n + 1 + dn)
                act.activation(KT[:, n % 2, 0, :], ps[:, 0, :], ACT.Copy)
                act.activation(KT[0:ROPE, n % 2, 2, :], ps[0:ROPE, 2, :], ACT.Copy).then_inc(kt_act, 1)

            def step(b, db, first, last):
                if not last:
                    for g in range(5):
                        if g < 3:
                            kt_copy(4 * b + g + 1, db * 4)
                        if g == 4 and b < NB - 1:
                            kt_copy(4 * b + 4, db * 4)
                        act.wait_ge(mx_dve, 5 * b + g + 1 + db * 5)
                        n = 512 if g < 4 else TS
                        act.activation(S[:, b % 2, g * 512:g * 512 + n], ps[:, 3 + (5 * b + g) % 2, 0:n], ACT.Copy
                                       ).then_inc(s_act, 1)
                if not first:
                    act.wait_ge(sample_pv, 5 * b + db * 5)
                    act.activation(QA[:, 0, bass.ds((b - 1 + db) * P, P)], ps[:, 6, 0:P], ACT.Copy).then_inc(sample_o_act, 1)
                if not last:
                    act.wait_ge(sample_negmax, b + 1 + db)
                    act.wait_ge(s_act, 5 * b + 5 + db * 5)
                    act.activation(S[:, b % 2, 0:KEYS], S[:, b % 2, 0:KEYS], ACT.Exp, bias=mx[:, b % 2, 5:6],
                                   accum_out=mx[:, b % 2, 6:7]).then_inc(sample_exp, 1)
            kt_copy(0, 0)
            step(0, 0, True, False)
            with act.Fori(0, 3) as i:
                step(1, i * 2, False, False)
                step(2, i * 2, False, False)
            step(7, 0, False, False)
            step(8, 0, False, True)
            for q in (0, 1):
                act.wait_ge(sample_v_ready, q + 1)
                for s in (0, 1):
                    rows = slice(64 * s, 64 * s + 64)
                    src = ps[rows, q, :].rearrange("p (j s t) -> p j s t", s=2, t=TS)[:, :, s, :]
                    act.activation(oTh[rows, 4 * q:4 * q + 4, TP:T], src, ACT.Copy).then_inc(sample_v_hi, 1)
            square("mla_out", 8)
            return norm

        def mla_dves(dve, v, link, rms, added):
            rms()
            cols = lambda c: gn[:, c:c + 1]
            link(dve.memset(krT[:, :], 0.0))
            link(dve.memset(acc[:, 0:T], 0.0))
            t0 = T0["mla_in"]
            a0 = AC["q"]
            link(dve.tensor_scalar(gql[:, 0:3], gn[:, GCOL["q"]:GCOL["q"] + 3], SCALE, None, ALU.mult))
            for k in range(6):
                dve.wait_ge(panel_used, PM + k + 1)
                dve.tensor_tensor(half(zc[:, k, :]), slot(t0 + k), half(r[:, :]), ALU.mult).then_inc(tile_taken, 1)
                dve.wait_ge(tile_taken, t0 + k + 1)
                if k == 3:
                    rms(rl)
                    link(dve.memset(acc[:, 0:T], 0.0))
                if k < 5:
                    link(dve.tensor_tensor(sq[:, :], zc[:, k, :], zc[:, k, :], ALU.mult))
                    dve.tensor_tensor(acc[:, 0:T], acc[:, 0:T], sq[:, :], ALU.add).then_inc(acc_done, 1)
                    dve.wait_ge(acc_done, a0 + k + 1)
                if k == 3:
                    for c in range(3):
                        dve.scalar_tensor_tensor(out=zc[:, c, :], in0=zc[:, c, :], scalar=gql[:, c:c + 1], in1=rl[:, :],
                                                 op0=ALU.mult, op1=ALU.mult).then_inc(zq_ready, 1)
                if k == 4:
                    for c in range(3):
                        dve.wait_ge(cqh_act, c + 1)
                        dve.tensor_tensor(cql[:, c, :], zc[:, c, :], cqh[:, c, :].bitcast(F32), ALU.subtract).then_inc(cq_ready, 1)
            link(dve.tensor_tensor(sq[64:96, :], zc[96:128, 5, :], rope[96:128, :], ALU.mult))
            link(dve.tensor_tensor(krT[64:96, :], zc[64:96, 5, :], rope[64:96, :], ALU.mult))
            link(dve.tensor_tensor(krT[64:96, :], krT[64:96, :], sq[64:96, :], ALU.add))
            rms(rl)
            for c in range(2):
                dve.scalar_tensor_tensor(out=ckv[:, c, :], in0=zc[:, 3 + c, :], scalar=cols(GCOL["kv"] + c),
                                         in1=rl[:, :], op0=ALU.mult, op1=ALU.mult).then_inc(ckv_ready, 1)
            for s in (0, 1):
                link(dve.tensor_copy(Kp[64:96, s, :], krT[64:96, 0:TP]))
            dve.tensor_copy(krS[0:ROPE, :], krT[64:96, TP:T]).then_inc(kr_ready, 1)
            for j in range(NTT):
                n = P if j < 4 else TS
                dve.wait_ge(ct_ready, j + 1)
                b = 2 + j % 2
                dve.tensor_copy(ckt[0:n, j, 0:KR], ps[0:n, b, 0:KR]).then_inc(ct_taken, 1)
                dve.tensor_copy(ckt[0:n, j, KR:KR + ROPE], ps[0:n, b, KR + 64:KR + 96]).then_inc(ct_taken, 1)
            dve.wait_ge(ct_taken, 2 * NTT)
            dve.memset(st[:, 0, 0:1], 0.0).then_inc(ov_lo, 1)

            def rope_query(h, hh, dh):
                dve.wait_ge(panel_used, PH + h + 1 + dh)
                link(dve.tensor_tensor(half(qtmp[64:96, :]), ps[96:128, 0:2, 0:H], half(rope[96:128, :]), ALU.mult))
                link(dve.tensor_tensor(half(Q[64:96, hh, :]), ps[64:96, 0:2, 0:H], half(rope[64:96, :]), ALU.mult))
                dve.tensor_tensor(Q[64:96, hh, :], Q[64:96, hh, :], qtmp[64:96, :], ALU.add).then_inc(qr_taken, 1)
                dve.wait_ge(qr_taken, h + 1 + dh)
                dst = QA[0:ROPE, 2, :].rearrange("p (t h) -> p t h", h=NH)[:, :, bass.ds(h + dh, 1)]
                link(dve.tensor_copy(dst, Q[64:96, hh, TP:T].rearrange("p (t a) -> p t a", a=1)))

            LP = 2 * 3 + 2
            c0 = v["chain"]
            with dve.Fori(0, 4) as i:
                v["dyn"] = i * (2 * LP)
                for j in (0, 1):
                    h, d4 = 2 * j, i * 4
                    assert v["chain"] == c0 + j * LP
                    rope_query(h, 0, d4)
                    dve.wait_ge(kv_ready, 3 * j + 2 + i * 6)
                    dve.tensor_copy(WT[0:64, 0, :], ps[0:64, 4, 0:KR]).then_inc(wt_taken, 1)
                    dve.tensor_copy(WT[0:64, 1, :], ps[64:128, 4, 0:KR]).then_inc(wt_taken, 1)
                    rope_query(h + 1, 1, d4)
                    for hh in (0, 1):
                        banks = score_banks(hh)
                        for n in range(4):
                            dve.wait_ge(sc_ready, 4 * (h + hh) + max(n + 1, 2) + d4 * 4)
                            dve.tensor_reduce(out=st[:, hh, n:n + 1], in_=banks[n], axis=AX.X, op=ALU.max,
                                              negate=True).then_inc(nm_ready, 1)
                    for hh in (0, 1):
                        dve.wait_ge(ex_ready, 4 * (h + hh) + 4 + d4 * 4)
                        link(dve.reciprocal(st[:, hh, 8:12], st[:, hh, 4:8]))
                        for n in range(4):
                            o = PP[:, hh, QT[n]:QT[n] + (n + 1) * P]
                            dve.tensor_scalar(o, o, st[:, hh, 8 + n:9 + n], None, ALU.mult).then_inc(pp_ready, 1)
                        if hh:
                            continue
                        dve.wait_ge(kv_ready, 3 * j + 3 + i * 6)
                        dve.tensor_copy(Vp[:, :, :].rearrange("p a d -> p (a d)"), ps[:, 1, :]).then_inc(v_taken, 1)
                        dve.wait_ge(qa_ready, j + 1 + i * 2)
                        for s in (0, 1):
                            dst = QA[:, 0:2, :].rearrange("p c (t h) -> p c t h", h=NH)[:, :, :, bass.ds(h + s + d4, 1)]
                            src = ps[:, 4, 256 + 128 * s:384 + 128 * s].rearrange("p (c t a) -> p c t a", c=2, a=1)
                            dve.tensor_copy(dst, src).then_inc(qa_taken, 1)
                    for hh in (0, 1):
                        dve.wait_ge(tr_ready, h + hh + 1 + d4)
                        b = pt_banks[hh]
                        dve.tensor_copy(PT[:, hh, KO[1]:KO[2]], ps[:, b[1], 0:384]).then_inc(tr_dve, 1)
                        dve.tensor_copy(PT[:, hh, KO[2]:1280], ps[:, b[2], 0:384]).then_inc(tr_dve, 1)
                    for hh in (0, 1):
                        dve.wait_ge(ov_hi, h + hh + 1 + d4)
                        rows = slice(64 * hh, 64 * hh + 64)
                        jj = i * 2 + j
                        dve.tensor_tensor(oTl[rows, bass.ds(jj, 1), 0:TP].rearrange("p a t -> p (a t)"),
                                          ps[rows, pv_bank[hh], :],
                                          oTh[rows, bass.ds(jj, 1), 0:TP].rearrange("p a t -> p (a t)").bitcast(F32),
                                          ALU.subtract).then_inc(ov_lo, 1)
            assert v["chain"] == c0 + 2 * LP
            v["chain"] = c0 + 8 * LP
            v["dyn"] = 0

            def kt_copy(n, dn):
                dve.wait_ge(kt_ready, n + 1 + dn)
                dve.tensor_copy(KT[:, n % 2, 1, :], ps[:, 1, :]).then_inc(kt_dve, 1)

            def pts_copy(n, dn, g):
                dve.wait_ge(pts_ready, n + 1 + dn)
                if g < 4:
                    dve.tensor_copy(PTs[:, n % 2, :], ps[:, 5, :]).then_inc(pts_taken, 1)
                else:
                    dve.tensor_copy(PTs[0:TS, n % 2, 0:P], ps[0:TS, 5, 0:P]).then_inc(pts_taken, 1)

            def ahead(b, db):
                link(dve.tensor_copy(QAb[:, b % 2, 0:2, :], QA[:, 0:2, bass.ds((b + db) * P, P)]))
                dve.tensor_copy(QAb[0:ROPE, b % 2, 2, :], QA[0:ROPE, 2, bass.ds((b + db) * P, P)]).then_inc(qab_ready, 1)

            def step(b, db, first, last):
                if not last:
                    kt_copy(4 * b + 1, db * 4)
                for g in range(5):
                    if not last and 0 < g < 3:
                        kt_copy(4 * b + g + 1, db * 4)
                    if not last and g == 4 and b < NB - 1:
                        kt_copy(4 * b + 4, db * 4)
                    if not first and g:
                        pts_copy(5 * (b - 1) + g, db * 5, g)
                    if not last:
                        dve.wait_ge(ss_sc, 5 * b + g + 1 + db * 5)
                        n = 512 if g < 4 else TS
                        dve.reduce_max(mx[:, b % 2, g:g + 1], ps[:, 3 + (5 * b + g) % 2, 0:n], AX.X).then_inc(mx_dve, 1)
                    if not first and g == 0:
                        pts_copy(5 * (b - 1) + g, db * 5, g)
                if not first:
                    dve.wait_ge(sample_pv, 5 * b + db * 5)
                    dve.tensor_copy(QA[:, 1, bass.ds((b - 1 + db) * P, P)], ps[:, 7, 0:P]).then_inc(sample_o_dve, 1)
                if not last:
                    dve.wait_ge(mx_dve, 5 * b + 5 + db * 5)
                    dve.tensor_reduce(out=mx[:, b % 2, 5:6], in_=mx[:, b % 2, 0:5], axis=AX.X, op=ALU.max,
                                      negate=True).then_inc(sample_negmax, 1)
                    if b < NB - 1:
                        ahead(b + 1, db)
                    dve.wait_ge(sample_exp, b + 1 + db)
                    dve.reciprocal(mx[:, b % 2, 7:8], mx[:, b % 2, 6:7]).then_inc(sample_inv, 1)
                    dve.wait_ge(sample_inv, b + 1 + db)
                    dve.tensor_scalar(S[:, b % 2, 0:512], S[:, b % 2, 0:512], mx[:, b % 2, 7:8], None, ALU.mult).then_inc(sp_ready, 1)
            ahead(0, 0)
            kt_copy(0, 0)
            link(dve.memset(S[:, :, KEYS:KEYS + P - TS], 0.0))
            step(0, 0, True, False)
            c0 = v["chain"]
            with dve.Fori(0, 3) as i:
                v["dyn"] = i * 2
                step(1, i * 2, False, False)
                step(2, i * 2, False, False)
            assert v["chain"] == c0 + 2
            v["chain"], v["dyn"] = c0 + 6, 0
            step(7, 0, False, False)
            step(8, 0, False, True)
            for q in (0, 1):
                for s in (0, 1):
                    rows = slice(64 * s, 64 * s + 64)
                    dve.wait_ge(sample_v_hi, 2 * q + s + 1)
                    src = ps[rows, q, :].rearrange("p (j s t) -> p j s t", s=2, t=TS)[:, :, s, :]
                    dve.tensor_tensor(oTl[rows, 4 * q:4 * q + 4, TP:T], src,
                                      oTh[rows, 4 * q:4 * q + 4, TP:T].bitcast(F32), ALU.subtract).then_inc(sample_v_lo, 1)
            added("mla_out", "ffb0")

        pt_banks, pv_bank = [(7, 5, 6), (0, 2, 3)], [6, 7]

        def score_banks(hh):
            a, b, c = (5, 6, 7) if hh == 0 else (2, 3, 0)
            return [ps[:, c, 0:P], ps[:, c, P:3 * P], ps[:, b, 0:3 * P], ps[:, a, :]]

        def mla_pes(pe, v, products, sums, tiles, xgh, xgl):
            mm, tr = nc.tensor.matmul, nc.tensor.transpose
            hooks = {5: {6: lambda: sums(2)}}
            for k in range(6):
                pe.wait_ge(tile_taken, T0["mla_in"] + k - 1)
                products(PM + k, 0, 8, xgh, xgl, slot(T0["mla_in"] + k),
                         waits=(lambda n: pe.wait_ge(xg_ready, XG["mix0"] + n + 1)) if k == 0 else None, at=hooks.get(k))
                if k in (0, 3):
                    sums(8 if k == 0 else 3)
            pe.wait_ge(ckv_ready, 2)
            pe.wait_ge(tile_taken, T0["mla_in"] + 6)
            for j in range(NTT):
                n = P if j < 4 else TS
                b = 2 + j % 2
                if j >= 2:
                    pe.wait_ge(ct_taken, 2 * j - 2)
                for c in range(3):
                    src = ckv[:, c, j * P:j * P + n] if c < 2 else krT[:, j * P:j * P + n]
                    ins = tr(ps[0:n, b, c * P:(c + 1) * P], src, ident)
                ins.then_inc(ct_ready, 1)
            pe.wait_ge(cq_ready, 3)
            pe.wait_ge(wuv_ready, 32)
            pe.wait_ge(ov_lo, 1)
            with pe.Fori(0, 4) as i:
                for j in (0, 1):
                    h, d4, d2 = 2 * j, i * 4, i * 2

                    def query(hh):
                        products(PH + h + hh, d4, 3, lambda n: cqh[:, n, :], lambda n: cql[:, n, :], ps[:, 0:2, 0:H])
                    query(0)
                    rw = raw[:, (PH + h + 0) % RAW, :, :]
                    for c in range(2):
                        ins = mm(ps[:, 2, :], rw[:, 3 + c, :], ckv[:, c, 0:TP], start=c == 0, stop=c == 1)
                    ins.then_inc(kv_ready, 1)
                    for c in range(2):
                        ins = tr(ps[:, 4, c * P:(c + 1) * P], rw[:, 3 + c, :], ident)
                    ins.then_inc(kv_ready, 1)
                    pe.wait_ge(qn_taken, h + 1 + d4)
                    pe.wait_ge(qr_taken, h + 1 + d4)
                    query(1)

                    def scores(hh):
                        banks = score_banks(hh)
                        pe.wait_ge(qn_taken, h + hh + 1 + d4)
                        pe.wait_ge(qr_taken, h + hh + 1 + d4)
                        pe.wait_ge(k_taken, 2 * j + 2 + i * 4)
                        for n in range(4):
                            mm(banks[n], Q[0:96, hh, n * P:(n + 1) * P], Kp[0:96, hh, 0:(n + 1) * P], start=True, stop=False)
                            mm(banks[n][:, n * P:(n + 1) * P], idb, cb[:, B_CAUSAL:B_CAUSAL + P], start=False,
                               stop=True).then_inc(sc_ready, 1)
                    pe.wait_ge(ov_lo, h + 1 + d4)
                    scores(0)
                    scores(1)
                    for kt in range(4):
                        for c in range(2):
                            ins = mm(ps[:, 1, kt * P:(kt + 1) * P], ckv[:, c, kt * P:(kt + 1) * P],
                                     wuv[:, c, bass.ds((d2 + j) * P, P)], start=c == 0, stop=c == 1)
                    ins.then_inc(kv_ready, 1)
                    pe.wait_ge(wt_taken, 2 * j + 2 + i * 4)
                    pe.wait_ge(qn_taken, h + 2 + d4)
                    for s in (0, 1):
                        for c in (0, 1):
                            ins = mm(ps[:, 4, 256 + 128 * s + 64 * c:320 + 128 * s + 64 * c],
                                     WT[0:64, s, c * P:(c + 1) * P], Q[0:64, s, TP:T], start=True, stop=True)
                    ins.then_inc(qa_ready, 1)
                    for hh in (0, 1):
                        pe.wait_ge(pp_ready, 4 * (h + hh) + 4 + d4 * 4)
                        bank = pt_banks[hh]
                        where = [ps[:, bank[0], :], ps[:, bank[1], :], ps[:, bank[2], :], ps[:, bank[2], 256:512]]
                        for kt in range(4):
                            for n in range(kt, 4):
                                ins = tr(where[kt][:, (n - kt) * P:(n - kt + 1) * P],
                                         PP[:, hh, QT[n] + kt * P:QT[n] + (kt + 1) * P], ident)
                        ins.then_inc(tr_ready, 1)
                        if hh == 0:
                            continue
                        pe.wait_ge(v_taken, j + 1 + d2)
                        pe.wait_ge(qa_taken, 2 * j + 2 + i * 4)
                        for s in (0, 1):
                            pe.wait_ge(tr_act, h + s + 1 + d4)
                            pe.wait_ge(tr_dve, 2 * (h + s) + 2 + d4 * 2)
                            for kt in range(4):
                                ins = mm(ps[:, pv_bank[s], kt * P:512], Vp[:, kt, :], PT[:, s, KO[kt]:KO[kt] + (4 - kt) * P],
                                         start=kt == 0, stop=kt == 3)
                            ins.then_inc(pv_ready, 1)

            pe.wait_ge(ov_lo, NH + 1)

            def pages_t(b, db, g):
                n = 4 * b + g
                s = b % 2
                pe.wait_ge(pg[s * 4 + g], 128 * (b // 2 + 1) + (db // 2 if isinstance(db, int) else db) * 64)
                if n:
                    pe.wait_ge(kt_act, n + db * 4)
                    pe.wait_ge(kt_dve, n + db * 4)
                for k in range(4):
                    for c in range(3):
                        w = P if c < 2 else ROPE
                        ins = tr(ps[0:w, c, k * P:(k + 1) * P], pages[:, s * NPG + 4 * g + k, c * P:c * P + w], ident)
                ins.then_inc(kt_ready, 1)

            def scores_s(b, db, g):
                m = 5 * b + g
                bank = ps[:, 3 + m % 2, :]
                s = b % 2
                if g == 0:
                    pe.wait_ge(qab_ready, b + 1 + db)
                if m >= 2:
                    pe.wait_ge(s_act, m - 1 + db * 5)
                    pe.wait_ge(mx_dve, m - 1 + db * 5)
                if g < 4:
                    pe.wait_ge(kt_act, 4 * b + g + 1 + db * 4)
                    pe.wait_ge(kt_dve, 4 * b + g + 1 + db * 4)
                    for c in range(3):
                        w = P if c < 2 else ROPE
                        ins = mm(bank, QAb[0:w, s, c, :], KT[0:w, g % 2, c, :], start=c == 0, stop=c == 2)
                else:
                    mm(bank[:, 0:TS], QAb[:, s, 0, :], ckv[:, 0, TP:T], start=True, stop=False)
                    mm(bank[:, 0:TS], QAb[:, s, 1, :], ckv[:, 1, TP:T], start=False, stop=False)
                    mm(bank[:, 0:TS], QAb[0:ROPE, s, 2, :], krS[0:ROPE, :], start=False, stop=False)
                    ins = mm(bank[:, 0:TS], idb, cb[:, bass.ds(B_SAMPLE + (b + db) * TS, TS)], start=False, stop=True)
                ins.then_inc(ss_sc, 1)

            def probs_t(b, db, g):
                n, s = 5 * (b - 1) + g, (b - 1) % 2
                if g == 0:
                    pe.wait_ge(sp_ready, b + db)
                if g == 1:
                    pe.wait_ge(sp_pool, b + db)
                if n:
                    pe.wait_ge(pts_taken, n + db * 5)
                if g < 4:
                    for k in range(4):
                        ins = tr(ps[:, 5, k * P:(k + 1) * P], S[:, s, g * 512 + k * P:g * 512 + (k + 1) * P], ident)
                else:
                    ins = tr(ps[:, 5, 0:P], S[:, s, 2048:2048 + P], ident)
                ins.then_inc(pts_ready, 1)

            def out_s(b, db, g):
                n, s = 5 * (b - 1) + g, (b - 1) % 2
                pe.wait_ge(pts_taken, n + 1 + db * 5)
                if g == 0 and b > 1:
                    pe.wait_ge(sample_o_act, b - 1 + db)
                    pe.wait_ge(sample_o_dve, b - 1 + db)
                if g < 4:
                    for k in range(4):
                        for c in (0, 1):
                            ins = mm(ps[:, 6 + c, 0:P], pages[:, s * NPG + 4 * g + k, c * P:(c + 1) * P],
                                     PTs[:, n % 2, k * P:(k + 1) * P], start=g == 0 and k == 0, stop=False)
                else:
                    for c in (0, 1):
                        ins = mm(ps[:, 6 + c, 0:P], ckt[0:TS, 4, c * P:(c + 1) * P], PTs[0:TS, n % 2, 0:P],
                                 start=False, stop=True)
                ins.then_inc(sample_pv, 1)

            def step(b, db, first, last):
                if not last:
                    pages_t(b, db, 1)
                    scores_s(b, db, 0)
                if not first:
                    probs_t(b, db, 0)
                for g in range(5):
                    if not last and g < 2:
                        pages_t(b, db, g + 2)
                    if not last and g == 3 and b < NB - 1:
                        pages_t(b + 1, db, 0)
                    if last and g < 4:
                        probs_t(b, db, g + 1)
                    if not first:
                        out_s(b, db, g)
                        if g < 4 and not last:
                            probs_t(b, db, g + 1)
                    if not last and g < 4:
                        scores_s(b, db, g + 1)
            pages_t(0, 0, 0)
            step(0, 0, True, False)
            with pe.Fori(0, 3) as i:
                step(1, i * 2, False, False)
                step(2, i * 2, False, False)
            step(7, 0, False, False)
            step(8, 0, False, True)
            pe.wait_ge(sample_o_act, NB)
            pe.wait_ge(sample_o_dve, NB)
            lat = QA[:, 0:2, :].rearrange("p c (t h) -> p c t h", h=NH)
            for q in (0, 1):
                for h in range(8 * q, 8 * q + 8):
                    for c in (0, 1):
                        ins = mm(ps[:, q, (h % 8) * TS:(h % 8 + 1) * TS], wuv[:, c, (h // 2) * P:(h // 2 + 1) * P],
                                 lat[:, c, :, h], start=c == 0, stop=c == 1)
                ins.then_inc(sample_v_ready, 1)
            pe.wait_ge(sample_v_lo, 4)
            tiles("mla_out", 8, 1, lambda n: oTh[:, n, :], lambda n: oTl[:, n, :], 2, 4)

        lu = Region(nc, X1, TMP)
        gTh = lu.put("gTh", [P, NC_D, T], F32R)
        gTl = lu.put("gTl", [P, NC_D, T], F32R)
        qT = lu.put("qT", [P, LH, T])
        kT = lu.put("kT", [P, LH, T])
        so = lu.put("so", [P, NC_D, T])
        Cb = lu.put("Cb", [P, NB, DV + 1])
        cols = lu.put("cols", [P, 64])
        nT = lu.put("nT", [P, NB * LH])
        nP = lu.put("nP", [P, LH])
        bg = lu.put("bg", [P, 2])
        den = lu.put("den", [P, 16])
        V0 = lu.at
        vT = lu.put("vT", [P, NC_D, T])
        lv = Region(nc, V0, TMP)
        Dm = lv.put("Dm", [P, 1280 + TS])
        SD = lv.put("SD", [P, 1280 + P])
        qd = lv.put("qd", [P, TS])
        qn = lv.put("qn", [P, P])
        kw = lv.put("kw", [P, 4, DK])
        RX = lv.put("RX", [P, 2, T])
        late = Region(nc, V0, TMP)
        nrow = late.put("nrow", [P, P])
        nst = late.put("nst", [NB * LH, DK])
        sqn = Region(nc, V0, TMP).put("sqn", [P, 2, NTT * P])
        lx = Region(nc, X0, X1)
        Vt = lx.put("Vt", [P, NTT, LH, DV + 1])
        kt = lx.put("kt", [P, NTT, LH, DK])
        kwb = lx.put("kwb", [P, NB, DK])
        wC = lx.put("wC", [P, NTT * LH])
        Wm = lx.put("Wm", [P, LH, NB])
        eC = lx.put("eC", [P, NTT * LH])
        lt = Region(nc, TMP, whole.end)
        RB = lt.put("RB", [P, T])
        lt2 = Region(nc, lt.at, whole.end)
        RA, RC, RD = (lt.put(n, [P, T]) for n in ("RA", "RC", "RD"))
        RE = lt.put("RE", [P, 2 * TS + NB])
        Mb = lt2.put("Mb", [P, T + TS + NB])
        Md = lt2.put("Md", [P, T])
        Co = lt2.put("Co", [P, DV + 1])
        nst0 = Region(nc, X1, TMP).put("nst0", [NB * LH, DK])
        SO = [0, 4 * P, 7 * P, 9 * P, 10 * P]
        GP, IP, LO = P0["mlstm_gates"], P0["mlstm_in"], P0["mlstm_out"]
        GT, IT = T0["mlstm_gates"], T0["mlstm_in"]
        st_ready, g_dve, g_act = sem("state_ready"), sem("g_dve"), sem("g_act")
        o_sig, m_ready, kv_turned, kv_copied = sem("o_sig"), sem("m_ready"), sem("kv_turned"), sem("kv_copied")
        norms_turned, colw_in, colw_exp = sem("norms_turned"), sem("colw_in"), sem("colw_exp")
        mb_copied, mb_masked = sem("mb_copied"), sem("mb_masked")
        decays_ready, dmat_ready = sem("decays_ready"), sem("dmat_ready")
        qk_ready, weighted_ready = sem("qk_ready"), sem("weighted_ready")
        qn_scaled, num_ready = sem("qn_scaled"), sem("num_ready")
        hsq_ready, hss_ready = sem("hsq_ready"), sem("hss_ready")
        hvar_ready, hrstd_ready = sem("hvar_ready"), sem("hrstd_ready")
        rowscale_ready, rows_spread = sem("rowscale_ready"), sem("rows_spread")
        rowscale_copied, hout_ready = sem("rowscale_copied"), sem("hout_ready")
        gated_ready, gated_hi, gated_lo = sem("gated_ready"), sem("gated_hi"), sem("gated_lo")
        kw_ready, kwb_ready = sem("kw_ready"), sem("kwb_ready")
        cprompt_ready, cprompt_copied, cprompt_stored = sem("cprompt_ready"), sem("cprompt_copied"), sem("cprompt_stored")
        csample_in, csample_prod = sem("csample_in"), sem("csample_prod")
        csample_new, csample_stored = sem("csample_new"), sem("csample_stored")
        norms_back, norms_copied = sem("norms_back"), sem("norms_copied")

        def mlstm_loads(sp, load):
            w = I["w_mlstm_in"][0].rearrange("(c p) n -> p c n", p=P)
            G = 2 * LH * DK + 2 * LH * DV
            load(GP, 0, lambda d: [(d[:, :, 0:8], w[:, :, G:G + 8], 16), (d[:, :, 8:32], w[:, :, 0:24], 16),
                                   (d[:, :, 32:36], w[:, :, G + 4:G + 8], 32), (d[:, :, 36:128], w[:, :, 0:92], 48)])
            with sp.Fori(0, 6) as i:
                for k in range(4):
                    load(IP + k, i * 4, lambda d: [(d, w[:, :, bass.ds((i * 4 + k) * P, P)], UNIT)])
            wo = I["w_mlstm_out"][0].rearrange("(c p) n -> p c n", p=P)
            for k in range(4):
                load(LO + k, 0, lambda d: [(d, wo[:, :, k * P:(k + 1) * P], UNIT)])
            sC = I["state_C"][0].rearrange("b h k v -> k b h v")
            oC = outs["C_sample"][0].rearrange("b h k v -> k b h v")
            with nc.allow_non_contiguous_dma(reason="four stabilisers a row"):
                sp.wait_ge(m_ready, 1)
                sp.dma_start(outs["m_prompt"][0].rearrange("b h -> h b"), RD[0:LH, TP - 1:TP]).then_inc(stored, 16)
                sp.dma_start(outs["m_sample"][0].rearrange("b h -> h b"),
                             RD[0:LH, TP:T].rearrange("h (b t) -> h b t", t=TB)[:, :, TB - 1]).then_inc(stored, 16)
            sp.wait_ge(st_ready, 64)
            for h in range(LH):
                if h:
                    sp.wait_ge(csample_new, NB * h)
                    sp.dma_start(oC[:, :, h - 1, :], Cb[:, :, 0:DV]).then_inc(csample_stored, 16)
                    sp.wait_ge(csample_stored, 16 * h)
                sp.dma_start(Cb[:, :, 0:DV], sC[:, :, h, :]).then_inc(csample_in, 16)
                sp.wait_ge(cprompt_copied, 2 * h + 2)
                sp.dma_start(outs["C_prompt"][0, 0, h], Co[:, 0:DV]).then_inc(cprompt_stored, 16)
            sp.wait_ge(csample_new, NB * LH)
            sp.dma_start(oC[:, :, LH - 1, :], Cb[:, :, 0:DV]).then_inc(csample_stored, 16)
            sp.wait_ge(norms_copied, 2)
            sp.dma_start(outs["n_prompt"][0, 0], nrow[0:LH, :]).then_inc(stored, 16)
            sp.dma_start(outs["n_sample"][0].rearrange("b h k -> (b h) k"), nst[:, :]).then_inc(stored, 16)
            sp.wait_ge(csample_stored, 16 * LH)
            sp.wait_ge(cprompt_stored, 16 * LH)
            for k in range(4, 8):
                load(LO + k, 0, lambda d: [(d, wo[:, :, k * P:(k + 1) * P], UNIT)])

        def mlstm_lowers(pool, lower, stage):
            lower(GP, 0, 8)
            stage("mlstm_in", [8] * 4, 6)
            lower(LO, 0, 8)
            pool.memset(den[:, 15:16], -0.5).then_inc(hrstd_ready, 1)
            for h in range(LH):
                pool.wait_ge(hvar_ready, h + 1)
                pool.wait_ge(hrstd_ready, h + 1)
                pool.tensor_tensor(den[:, 10:15], den[:, 5:10], den[:, 15:16].to_broadcast([P, 5]), ALU.pow).then_inc(hrstd_ready, 1)
                for c in (0, 1):
                    pool.wait_ge(gated_hi, 2 * h + c + 1)
                    pool.tensor_tensor(gTl[:, 2 * h + c, :], RX[:, c, :], gTh[:, 2 * h + c, :].bitcast(F32),
                                       ALU.subtract).then_inc(gated_lo, 1)
            for k in range(1, 8):
                lower(LO + k, 0, 8)

        def mlstm_acts(act, upper, root, square, norm):
            upper(GP + 1, 0, 8)
            root(norm, D); norm += 1
            with nc.allow_non_contiguous_dma(reason="biases and stabilisers, a word each"):
                act.dma_start(bg[0:LH, 0:1], I["b_igate"].rearrange("a h -> h a")).then_inc(st_ready, 16)
                act.dma_start(bg[0:LH, 1:2], I["b_fgate"].rearrange("a h -> h a")).then_inc(st_ready, 16)
                act.dma_start(m0[0:LH, :], I["state_m"][0].rearrange("b h -> h b")).then_inc(st_ready, 16)
            act.wait_ge(panel_used, GP)
            act.dma_start(nst0[:, :], I["state_n"][0].rearrange("b h k -> (b h) k")).then_inc(st_ready, 16)
            upper(IP + 1, 0, 8)
            act.wait_ge(g_dve, 1)
            act.activation(RA[0:LH, :], RA[0:LH, :], ACT.Tanh, bias=bg[0:LH, 0:1], scale=1.0 / CAP)
            act.activation(RB[0:LH, :], RB[0:LH, :], ACT.Tanh, bias=bg[0:LH, 1:2], scale=1.0 / CAP).then_inc(g_act, 1)
            act.wait_ge(g_act, 1)
            act.activation(RC[0:LH, :], RB[0:LH, :], ACT.Exp, scale=-CAP).then_inc(g_act, 1)
            upper(IP + 2, 0, 8)
            act.wait_ge(g_dve, 2)
            act.activation(RB[0:LH, :], RD[0:LH, :], ACT.Ln).then_inc(g_act, 1)
            for k in range(2, 16):
                upper(IP + 1 + k, 0, 8)
            for c in range(NC_D):
                upper(IP + 17 + c, 0, 8)
                act.wait_ge(tile_taken, IT + 17 + c)
                act.activation(so[:, c, :], so[:, c, :], ACT.Sigmoid).then_inc(o_sig, 1)
            act.wait_ge(colw_in, 1)
            act.activation(wC[:, :], wC[:, :], ACT.Exp).then_inc(colw_exp, 1)
            act.activation(eC[:, :], cols[:, 20:40], ACT.Exp, scale=-1.0).then_inc(colw_exp, 1)
            def upper_part(h):
                for c in (0, 1):
                    act.wait_ge(gated_ready, 2 * h + c + 1)
                    act.activation(gTh[:, 2 * h + c, :], RX[:, c, :], ACT.Copy).then_inc(gated_hi, 1)
            for h in range(LH):
                act.wait_ge(mb_copied, h + 1)
                act.activation(Mb[:, T:T + TS + NB], Mb[:, T:T + TS + NB], ACT.Exp).then_inc(decays_ready, 1)
                act.wait_ge(mb_masked, h + 1)
                if h:
                    act.wait_ge(hss_ready, h)
                for s in range(NTT):
                    n = P if s < 4 else TS
                    ins = act.activation(Dm[0:n, SO[s]:SO[s] + n], Md[0:n, s * P:s * P + n], ACT.Exp,
                                         bias=cols[0:n, 4 * s + h:4 * s + h + 1], scale=-1.0)
                    if s < 3:
                        ins = act.activation(Dm[:, SO[s] + P:SO[s + 1]], Mb[:, (s + 1) * P:TP], ACT.Exp,
                                             bias=cols[:, 4 * s + h:4 * s + h + 1], scale=-1.0)
                    ins.then_inc(dmat_ready, 1)
                if h:
                    upper_part(h - 1)
                for s in range(4):
                    ins = act.activation(kw[:, s, :], kt[:, s, h, :], ACT.Copy, scale=wC[:, 4 * s + h:4 * s + h + 1])
                ins.then_inc(kw_ready, 1)
                for c in (0, 1):
                    act.wait_ge(num_ready, 3 * h + c + 1)
                    act.wait_ge(weighted_ready, 5 * h + 5)
                    act.activation(sqn[:, c, 0:TP], ps[:, 6 + c, :], ACT.Square).then_inc(hsq_ready, 1)
                act.wait_ge(num_ready, 3 * h + 3)
                act.activation(sqn[:, :, T:NTT * P], ident.rearrange("p (c t) -> p c t", c=2), ACT.Copy, scale=0.0)
                act.activation(sqn[:, :, TP:T], ps[:, 5, P:2 * P].rearrange("p (c t) -> p c t", c=2), ACT.Square).then_inc(hsq_ready, 1)
            upper_part(LH - 1)
            square("mlstm_out", 8)
            return norm

        def mlstm_dves(dve, v, link, rms, added):
            rms()
            dve.wait_ge(st_ready, 64)
            link(dve.tensor_scalar(bg[0:LH, :], bg[0:LH, :], 1.0 / CAP, None, ALU.mult))
            link(dve.memset(cols[:, :], 0.0))
            dve.wait_ge(panel_used, GP + 1)
            tg = 2 * (GT % 2)
            link(dve.tensor_tensor(half(RA[0:LH, :]), ps[0:LH, tg:tg + 2, 0:H], half(r[0:LH, :]), ALU.mult))
            dve.tensor_tensor(half(RB[0:LH, :]), ps[32:32 + LH, tg:tg + 2, 0:H], half(r[32:32 + LH, :]), ALU.mult).then_inc(tile_taken, 1)
            dve.wait_ge(tile_taken, GT + 1)
            dve.memset(den[:, 0:1], 0.0).then_inc(g_dve, 1)

            rows = lambda t: t[0:LH, 0:TP]
            segs = lambda t: t[0:LH, TP:T].rearrange("h (b t) -> h b t", t=TB)

            def scan(n, src, dst, op):
                d = 1 << n
                link(dve.tensor_tensor(rows(dst)[:, d:], rows(src)[:, d:], rows(src)[:, 0:TP - d], op))
                link(dve.tensor_copy(rows(dst)[:, 0:d], rows(src)[:, 0:d]))
                if n < 3:
                    link(dve.tensor_tensor(segs(dst)[:, :, d:], segs(src)[:, :, d:], segs(src)[:, :, 0:TB - d], op))
                    link(dve.tensor_copy(segs(dst)[:, :, 0:d], segs(src)[:, :, 0:d]))

            def evacuate(t):
                dst = (qT[:, t, :] if t < 4 else kT[:, t - 4, :] if t < 8 else vT[:, t - 8, :] if t < 16
                       else so[:, t - 16, :])
                dve.wait_ge(panel_used, IP + t + 1)
                if t < 4:
                    dve.scalar_tensor_tensor(out=half(dst), in0=slot(IT + t), scalar=DK ** -0.5, in1=half(r[:, :]),
                                             op0=ALU.mult, op1=ALU.mult).then_inc(tile_taken, 1)
                else:
                    dve.tensor_tensor(half(dst), slot(IT + t), half(r[:, :]), ALU.mult).then_inc(tile_taken, 1)

            L = slice(0, LH)
            for t in range(24):
                evacuate(t)
                if t == 0:
                    dve.wait_ge(g_act, 2)
                    dve.tensor_scalar(RD[L, :], RC[L, :], 1.0, None, ALU.add).then_inc(g_dve, 1)
                    dve.wait_ge(g_dve, 2)
                if t == 1:
                    dve.wait_ge(g_act, 3)
                    link(dve.tensor_scalar(RD[L, :], RD[L, :], 1.0, None, ALU.subtract))
                    link(dve.reciprocal(RD[L, :], RD[L, :]))
                if t == 2:
                    link(dve.tensor_tensor(RC[L, :], RC[L, :], RD[L, :], ALU.mult))
                    link(dve.scalar_tensor_tensor(out=RB[L, :], in0=RB[L, :], scalar=-1.0, in1=RC[L, :],
                                                  op0=ALU.mult, op1=ALU.mult))
                if 3 <= t < 12:
                    n = t - 3
                    scan(n, (RB, RC)[n % 2], (RC, RB)[n % 2], ALU.add)
                    if n == 2:
                        link(dve.tensor_copy(RB[L, TP:T], RC[L, TP:T]))
                if t == 12:
                    link(dve.scalar_tensor_tensor(out=RA[L, :], in0=RA[L, :], scalar=CAP, in1=RC[L, :],
                                                  op0=ALU.mult, op1=ALU.subtract))
                    scan(0, RA, RB, ALU.max)
                if 13 <= t < 21:
                    n = t - 12
                    scan(n, (RB, RD)[(n - 1) % 2], (RD, RB)[(n - 1) % 2], ALU.max)
                if t == 21:
                    link(dve.tensor_scalar(rows(RB), rows(RB), 0.0, None, ALU.max))
                    mb = m0[0:LH, :].rearrange("h (b a) -> h b a", a=1).to_broadcast([LH, NB, TB])
                    link(dve.tensor_tensor(segs(RB), segs(RB), mb, ALU.max))
                    dve.tensor_tensor(RD[L, :], RC[L, :], RB[L, :], ALU.add).then_inc(m_ready, 1)
                    end = segs(RB)[:, :, TB - 1:TB]
                    link(dve.tensor_copy(RE[L, 0:TS].rearrange("h (b t) -> h b t", t=TB), end.to_broadcast([LH, NB, TB])))
                    link(dve.tensor_tensor(RE[L, TS:2 * TS].rearrange("h (b t) -> h b t", t=TB), mb, segs(RB), ALU.subtract))
                    link(dve.tensor_tensor(RE[L, 2 * TS:2 * TS + NB].rearrange("h (b a) -> h b a", a=1),
                                           m0[0:LH, :].rearrange("h (b a) -> h b a", a=1), end, ALU.subtract))
                    dve.memset(den[:, 1:2], 0.0).then_inc(g_dve, 1)
            dve.wait_ge(norms_turned, 1)
            link(dve.tensor_copy(cols[:, 0:16], ps[:, 4, 0:16]))
            link(dve.tensor_copy(cols[0:TS, 16:20], ps[0:TS, 4, 16:20]))
            link(dve.tensor_copy(cols[:, 20:36], ps[:, 4, 20:36]))
            link(dve.tensor_copy(cols[0:TS, 36:44], ps[0:TS, 4, 36:44]))
            link(dve.tensor_copy(cols[:, 44:48], ps[:, 4, 44:48]))
            link(dve.tensor_copy(nT[:, :], ps[:, 4, 64:96]))
            mt_ = cols[:, 44:48].rearrange("p (a h) -> p a h", a=1).to_broadcast([P, 4, LH])
            link(dve.memset(wC[:, 16:20], 0.0))
            link(dve.tensor_tensor(wC[:, 0:16].rearrange("p (s h) -> p s h", h=LH),
                                   cols[:, 0:16].rearrange("p (s h) -> p s h", h=LH), mt_, ALU.subtract))
            dve.tensor_tensor(wC[0:TS, 16:20], cols[0:TS, 16:20], cols[0:TS, 40:44], ALU.subtract).then_inc(colw_in, 1)
            link(dve.memset(Vt[:, :, :, DV:DV + 1], 1.0))
            for j in range(NTT):
                n = P if j < 4 else TS
                for q in range(3):
                    dve.wait_ge(kv_turned, 3 * j + q + 1)
                    src = ps[0:n, 5 + q, :]
                    if q == 0:
                        dve.tensor_copy(kt[0:n, j, :, :].rearrange("p h d -> p (h d)"), src).then_inc(kv_copied, 1)
                    else:
                        dve.tensor_copy(Vt[0:n, j, 2 * q - 2:2 * q, 0:DV], src.rearrange("p (h d) -> p h d", h=2)).then_inc(kv_copied, 1)
            dve.wait_ge(kv_copied, 3 * NTT)
            dve.wait_ge(colw_exp, 2)
            wm = wC[0:TS, 16:20].rearrange("p (h a) -> p h a", a=1).to_broadcast([TS, LH, NB])
            bm = cf[0:TS, C_BLK:C_BLK + NB].rearrange("p (a b) -> p a b", a=1).to_broadcast([TS, LH, NB])
            link(dve.tensor_tensor(Wm[0:TS, :, :], wm, bm, ALU.mult))
            link(dve.memset(SD[:, 1280:1280 + P], 0.0))
            link(dve.memset(qn[:, :], 0.0))
            tri = cf[:, C_TRI:C_TRI + P].rearrange("p (a t) -> p a t", a=1).to_broadcast([P, 4, P])
            nTh = lambda h: nT[:, :].rearrange("p (b h) -> p b h", h=LH)[:, :, h:h + 1]

            def stabilisers(h):
                dve.wait_ge(rows_spread, 2 * h if h else 1)
                if h:
                    dve.wait_ge(dmat_ready, NTT * h)
                dve.tensor_copy(Mb[:, :], flat(0, T + TS + NB)).then_inc(mb_copied, 1)
                dve.wait_ge(mb_copied, h + 1)
                link(dve.tensor_tensor(Md[:, 0:TP].rearrange("p (s t) -> p s t", s=4),
                                       Mb[:, 0:TP].rearrange("p (s t) -> p s t", s=4), tri, ALU.add))
                dve.tensor_tensor(Md[0:TS, TP:T], Mb[0:TS, TP:T], cf[0:TS, C_STRI:C_STRI + TS], ALU.add).then_inc(mb_masked, 1)

            def weigh(h):
                for s, (bank, o, there) in enumerate([(2, 0, 1), (3, 0, 3), (4, 0, 5), (4, 256, 5), (3, 384, 3)]):
                    dve.wait_ge(qk_ready, NTT * h + there)
                    dve.wait_ge(dmat_ready, NTT * h + s + 1)
                    w, n = (SO[s + 1] - SO[s], P) if s < 4 else (TS, TS)
                    dve.tensor_tensor(SD[0:n, SO[s]:SO[s] + w], ps[0:n, bank, o:o + w], Dm[0:n, SO[s]:SO[s] + w],
                                      ALU.mult).then_inc(weighted_ready, 1)

            stabilisers(0)
            weigh(0)
            for h in range(LH):
                dve.wait_ge(decays_ready, h + 1)
                link(dve.tensor_tensor(qd[:, :], qT[:, h, TP:T], Mb[:, T:T + TS], ALU.mult))
                dve.tensor_tensor(qn[:, 0:TS].rearrange("p (b t) -> p b t", t=TB),
                                  qd[:, :].rearrange("p (b t) -> p b t", t=TB), nTh(h).to_broadcast([P, NB, TB]),
                                  ALU.mult).then_inc(qn_scaled, 1)
                ks = kt[0:TS, 4, h, :].rearrange("p (a d) -> p a d", a=1).to_broadcast([TS, NB, DK])
                ws = Wm[0:TS, h, :].rearrange("p (b a) -> p b a", a=1).to_broadcast([TS, NB, DK])
                dve.tensor_tensor(kwb[0:TS, :, :], ks, ws, ALU.mult).then_inc(kwb_ready, 1)
                dve.wait_ge(csample_in, 16 * (h + 1))
                link(dve.tensor_copy(Cb[:, :, DV:DV + 1], nTh(h)))
                for b in range(NB):
                    if b == 4:
                        if h:
                            dve.wait_ge(cprompt_stored, 16 * h)
                        dve.wait_ge(cprompt_ready, h + 1)
                        dve.tensor_copy(Co[:, :], ps[:, 2, 0:DV + 1]).then_inc(cprompt_copied, 1)
                        dve.wait_ge(cprompt_copied, 2 * h + 1)
                        dve.tensor_copy(nP[:, h:h + 1], Co[:, DV:DV + 1]).then_inc(cprompt_copied, 1)
                    dve.wait_ge(csample_prod, NB * h + b + 1)
                    dve.scalar_tensor_tensor(out=Cb[:, b, :], in0=Cb[:, b, :], scalar=Mb[:, T + TS + b:T + TS + b + 1],
                                             in1=ps[:, 3 + b % 2, 0:DV + 1], op0=ALU.mult, op1=ALU.add).then_inc(csample_new, 1)
                dve.wait_ge(csample_new, NB * (h + 1))
                link(dve.tensor_copy(nTh(h), Cb[:, :, DV:DV + 1]))
                if h < LH - 1:
                    stabilisers(h + 1)
                else:
                    dve.memset(bg[:, 0:1], 0.0).then_inc(norms_back, 1)
                dve.wait_ge(hss_ready, h + 1)
                link(dve.tensor_copy(den[:, 0:10], ps[:, 1, 300:310]))
                link(dve.scalar_tensor_tensor(out=den[:, 0:5], in0=den[:, 0:5], scalar=-1.0, in1=den[:, 0:5],
                                              op0=ALU.mult, op1=ALU.max))
                eh = eC[:, :].rearrange("p (s h) -> p s h", h=LH)[:, :, h:h + 1]
                link(dve.tensor_tensor(den[:, 0:5].rearrange("p (s a) -> p s a", a=1),
                                       den[:, 0:5].rearrange("p (s a) -> p s a", a=1), eh, ALU.max))
                link(dve.reciprocal(den[:, 0:5], den[:, 0:5]))
                link(dve.tensor_tensor(den[:, 5:10], den[:, 5:10], den[:, 0:5], ALU.mult))
                link(dve.tensor_tensor(den[:, 5:10], den[:, 5:10], den[:, 0:5], ALU.mult))
                dve.tensor_scalar(den[:, 5:10], den[:, 5:10], 1.0 / DV, EPS, ALU.mult, ALU.add).then_inc(hvar_ready, 1)
                dve.wait_ge(hrstd_ready, h + 2)
                dve.tensor_tensor(den[:, 0:5], den[:, 0:5], den[:, 10:15], ALU.mult).then_inc(rowscale_ready, 1)
                if h < LH - 1:
                    weigh(h + 1)
                else:
                    dve.wait_ge(norms_back, 2)
                    dve.tensor_copy(nrow[0:LH, :], ps[0:LH, 2, 0:P]).then_inc(norms_copied, 1)
                    dve.tensor_copy(nst[:, :], ps[0:NB * LH, 2, P:2 * P]).then_inc(norms_copied, 1)
                dve.wait_ge(rows_spread, 2 * h + 3 if h < LH - 1 else 2 * LH)
                dve.tensor_copy(r[:, :], flat(0, T)).then_inc(rowscale_copied, 1)
                dve.wait_ge(rowscale_copied, h + 1)
                if h == 0:
                    dve.wait_ge(o_sig, 8)
                else:
                    dve.wait_ge(gated_lo, 2 * h)
                dve.wait_ge(hsq_ready, 3 * h + 3)
                for part in ("prompt", "sample"):
                    for c in (0, 1):
                        gcol = gn[:, GCOL["head"] + 2 * h + c:GCOL["head"] + 2 * h + c + 1]
                        src, t = (ps[:, 6 + c, :], slice(0, TP)) if part == "prompt" else \
                            (ps[:, 5, P + c * TS:P + (c + 1) * TS], slice(TP, T))
                        dve.scalar_tensor_tensor(out=RX[:, c, t], in0=src, scalar=gcol, in1=r[:, t],
                                                 op0=ALU.mult, op1=ALU.mult).then_inc(hout_ready, 1)
                dve.wait_ge(hout_ready, 4 * h + 4)
                for c in (0, 1):
                    dve.tensor_tensor(RX[:, c, :], RX[:, c, :], so[:, 2 * h + c, :], ALU.mult).then_inc(gated_ready, 1)
            dve.wait_ge(cprompt_stored, 16 * LH)
            dve.wait_ge(csample_stored, 16 * LH)
            dve.wait_ge(stored, 16 * (2 * NTT + 4))
            added("mlstm_out", "ffb1")

        def mlstm_pes(pe, v, products, sums, tiles, xgh, xgl):
            mm, tr = nc.tensor.matmul, nc.tensor.transpose
            pe.wait_ge(tile_taken, GT - 1)
            products(GP, 0, 8, xgh, xgl, slot(GT), waits=lambda n: pe.wait_ge(xg_ready, XG["mix1"] + n + 1))
            sums(8)
            tiles("mlstm_in", 8, 1, xgh, xgl, 6, 4)
            pe.wait_ge(g_dve, 3)
            pe.wait_ge(m_ready, 1)
            pe.wait_ge(tile_taken, IT + 24)
            for o, src in ((0, RA), (20, RD)):
                for j in range(NTT):
                    n = P if j < 4 else TS
                    tr(ps[0:n, 4, o + 4 * j:o + 4 * j + 4], src[0:LH, j * P:j * P + n], ident[0:LH, 0:LH])
            tr(ps[0:TS, 4, 40:44], RE[0:LH, 0:TS], ident[0:LH, 0:LH])
            for h in range(LH):
                mm(ps[:, 4, 44 + h:45 + h], cf[0:LH, C_SEL + h * P:C_SEL + (h + 1) * P], RB[0:LH, TP - 1:TP],
                   start=True, stop=True)
            pe.wait_ge(st_ready, 64)
            tr(ps[:, 4, 64:96], nst0[:, :], ident[0:NB * LH, 0:NB * LH]).then_inc(norms_turned, 1)
            for j in range(NTT):
                n = P if j < 4 else TS
                for q in range(3):
                    if j:
                        pe.wait_ge(kv_copied, 3 * (j - 1) + q + 1)
                    for e in range(4):
                        src = kT[:, e, :] if q == 0 else vT[:, 4 * (q - 1) + e, :]
                        ins = tr(ps[0:n, 5 + q, e * P:(e + 1) * P], src[:, j * P:j * P + n], ident)
                    ins.then_inc(kv_turned, 1)
            pe.wait_ge(kv_copied, 3 * NTT)
            def stabilisers(h):
                sel = cf[0:LH, C_SEL + h * P:C_SEL + (h + 1) * P]
                mm(ps[:, 0, :], sel, RB[0:LH, 0:TP], start=True, stop=True)
                mm(ps[:, 1, 0:TS], sel, RB[0:LH, TP:T], start=True, stop=True)
                mm(ps[:, 1, TS:2 * TS + NB], sel, RE[0:LH, TS:2 * TS + NB], start=True, stop=True).then_inc(rows_spread, 1)

            def scores(h, tiles_):
                for s in tiles_:
                    if s == 4:
                        mm(ps[0:TS, 3, 384:384 + TS], kT[:, h, TP:T], qT[:, h, TP:T], start=True, stop=True).then_inc(qk_ready, 1)
                        continue
                    bank, o = [(2, 0), (3, 0), (4, 0), (4, 256)][s]
                    mm(ps[:, bank, o:o + TP - s * P], kT[:, h, s * P:(s + 1) * P], qT[:, h, s * P:TP],
                       start=True, stop=True).then_inc(qk_ready, 1)

            def states(h, b):
                if b >= 2:
                    pe.wait_ge(csample_new, NB * h + b - 1)
                mm(ps[:, 3 + b % 2, 0:DV + 1], kwb[0:TS, b, :], Vt[0:TS, 4, h, :], start=True, stop=True).then_inc(csample_prod, 1)

            def squares(j):
                for c in (0, 1):
                    ins = mm(ps[:, 1, 305 + j:306 + j], sqn[:, c, j * P:(j + 1) * P], ones[:, 0:1], start=c == 0, stop=c == 1)
                return ins

            stabilisers(0)
            scores(0, (0, 1, 4, 2, 3))
            for h in range(LH):
                pe.wait_ge(weighted_ready, NTT * (h + 1))
                for c in (0, 1):
                    if h:
                        pe.wait_ge(hout_ready, 4 * h - 3 + c)
                    for s in range(4):
                        ins = mm(ps[:, 6 + c, s * P:TP], Vt[:, s, h, c * P:(c + 1) * P], SD[:, SO[s]:SO[s + 1]],
                                 start=s == 0, stop=s == 3)
                    ins.then_inc(num_ready, 1)
                pe.wait_ge(qn_scaled, h + 1)
                pe.wait_ge(csample_in, 16 * (h + 1))
                if h:
                    pe.wait_ge(hout_ready, 4 * h)
                for c in (0, 1):
                    o = P + c * TS
                    mm(ps[:, 5, o:o + TS], Vt[0:TS, 4, h, c * P:(c + 1) * P], SD[0:TS, 1280:1280 + TS], start=True, stop=False)
                    for b in range(NB):
                        ins = mm(ps[:, 5, o + b * TB:o + (b + 1) * TB], Cb[:, b, c * P:(c + 1) * P],
                                 qd[:, b * TB:(b + 1) * TB], start=False, stop=b == NB - 1)
                ins.then_inc(num_ready, 1)
                pe.wait_ge(kwb_ready, h + 1)
                states(h, 0)
                states(h, 1)
                pe.wait_ge(mb_copied, h + 1)
                for j in range(NTT):
                    for s in range(j + 1 if j < 4 else 0):
                        mm(ps[:, 1, 300 + j:301 + j], SD[:, SO[s] + (j - s) * P:SO[s] + (j - s + 1) * P], ones[:, 0:1],
                           start=s == 0, stop=s == j)
                mm(ps[:, 1, 304:305], SD[0:TS, 1280:1280 + P], ones[0:TS, 0:1], start=True, stop=False)
                mm(ps[:, 1, 304:305], qn[:, :], ones[:, 0:1], start=False, stop=True)
                states(h, 2)
                states(h, 3)
                pe.wait_ge(kw_ready, h + 1)
                for s in range(4):
                    ins = mm(ps[:, 2, 0:DV + 1], kw[:, s, :], Vt[:, s, h, :], start=s == 0, stop=s == 3)
                ins.then_inc(cprompt_ready, 1)
                for b in range(4, NB):
                    states(h, b)
                if h < LH - 1:
                    stabilisers(h + 1)
                    pe.wait_ge(csample_new, NB * (h + 1))
                    pe.wait_ge(cprompt_copied, 2 * h + 2)
                    scores(h + 1, (0,))
                    pe.wait_ge(mb_copied, h + 2)
                pe.wait_ge(hsq_ready, 3 * (h + 1))
                for j in range(NTT):
                    ins = squares(j)
                ins.then_inc(hss_ready, 1)
                if h < LH - 1:
                    scores(h + 1, (1, 4, 2, 3))
                else:
                    pe.wait_ge(norms_back, 1)
                    pe.wait_ge(cprompt_copied, 2 * LH)
                    tr(ps[0:LH, 2, 0:P], nP[:, :], ident)
                    tr(ps[0:NB * LH, 2, P:2 * P], nT[:, :], ident).then_inc(norms_back, 1)
                pe.wait_ge(rowscale_ready, h + 1)
                for j in range(NTT):
                    w = P if j < 4 else TS
                    ins = mm(flat(0, T)[:, j * P:j * P + w], den[:, j:j + 1].to_broadcast([P, P]), ident[:, 0:w],
                             start=True, stop=True)
                ins.then_inc(rows_spread, 1)
            pe.wait_ge(norms_copied, 2)
            pe.wait_ge(rowscale_copied, LH)
            tiles("mlstm_out", 8, 1, lambda n: gTh[:, n, :], lambda n: gTl[:, n, :], 2, 4,
                  waits0=lambda n: pe.wait_ge(gated_lo, n + 1))

        mixer_loads, mixer_lowers = [mla_loads, mlstm_loads], [mla_lowers, mlstm_lowers]
        mixer_acts, mixer_dves, mixer_pes = [mla_acts, mlstm_acts], [mla_dves, mlstm_dves], [mla_pes, mlstm_pes]

        xr = [I["x_prompt"][0, j * P:(j + 1) * P, :] for j in range(4)] + [I["x_sample"].rearrange("b t d -> (b t) d")]

        block = ctx.enter_context(nc.Block())
        @block.sync
        def _(sp):
            def load(p, dyn, parts, free=True):
                s = p % RAW
                if free:
                    sp.wait_ge(wlo_ready, p - RAW - 7 + dyn)
                for dst, src, inc in parts(raw[:, s, :, :]):
                    sp.dma_start(dst, src).then_inc(raw_ready[s], inc)

            def ffn_in(name, w):
                v = w.rearrange("(c p) n -> p c n", p=P)
                p0 = P0[name]

                def pair(i, k, dyn, free=True):
                    for half_ in (0, 1):
                        col = half_ * FF + (i * 2 + k) * P
                        load(p0 + 2 * k + half_, dyn, lambda d: [(d, v[:, :, bass.ds(col, P)], UNIT)], free)
                if p0 == 8:
                    pair(0, 0, 0, False)
                    pair(0, 1, 0, False)
                with sp.Fori(1 if p0 == 8 else 0, NC_F // 2) as i:
                    for k in (0, 1):
                        pair(i, k, i * 4)

            def ffn_out(name, w):
                v = w.rearrange("(c p) n -> p c n", p=P)
                with sp.Fori(0, NC_D // 2) as i:
                    for k in (0, 1):
                        for q, (a, b) in enumerate(FF_PARTS):
                            load(P0[name] + 4 * k + q, i * 8,
                                 lambda d: [(d[:, 0:b - a, :], v[:, a:b, bass.ds((i * 2 + k) * P, P)], UNIT)])

            def ple(l):
                p0 = P0[f"ple{l}"]
                g = I["w_ple_gate"][l].rearrange("(c p) n -> p c n", p=P)
                w = I["w_ple_proj"][l].rearrange("(c p) n -> p c n", p=P)

                def gate(p, c, dyn):
                    load(p, dyn, lambda d: [(d, g[:, :, bass.ds(c * P, P)], UNIT)])

                def proj(p, c, dyn):
                    load(p, dyn, lambda d: [(d[:, 0:2, :], w[:, :, bass.ds(c * P, P)], UNIT)])
                gate(p0, 0, 0)
                gate(p0 + 1, 1, 0)
                proj(p0 + 2, 0, 0)
                with sp.Fori(0, 3) as i:
                    for k in (0, 1):
                        gate(p0 + 3 + 2 * k, i * 2 + 2 + k, i * 4)
                        proj(p0 + 4 + 2 * k, i * 2 + 1 + k, i * 4)
                proj(p0 + 15, 7, 0)

            sp.dma_start(gn[:, :], I["gains"]).then_inc(gn_ready, 16)
            for j in range(NTT):
                sp.dma_start(xin[0:(P if j < 4 else TS), j, 512:1024], xr[j][:, 512:1024]).then_inc(in_ready[1], 16)
            for l in (0, 1):
                ffn_in(f"ffa{l}_in", I["w_ffa_in"][l])
                ffn_out(f"ffa{l}_out", I["w_ffa_out"][l])
                mixer_loads[l](sp, load)
                ffn_in(f"ffb{l}_in", I["w_ffb_in"][l])
                ffn_out(f"ffb{l}_out", I["w_ffb_out"][l])
                ple(l)
            for j in range(NTT):
                dst = outs["y_prompt"][0, j * P:(j + 1) * P, :] if j < 4 else \
                    outs["y_sample"].rearrange("b t d -> (b t) d")
                for q, y_row in enumerate((y_act, y_dve)):
                    sp.wait_ge(y_row, j + 1)
                    sp.dma_start(dst[:, q * 512:(q + 1) * 512],
                                 xin[0:(P if j < 4 else TS), j, q * 512:(q + 1) * 512]).then_inc(stored, 16)
            sp.wait_ge(stored, 16 * (2 * NTT + 4 + 2 * NTT))

        @block.gpsimd
        def _(pool):
            def lower(p, dyn, n, place=None):
                hi, lo = place or (whi[:, p % SPLIT, :, :], wlo[:, p % SPLIT, :, :])
                pool.wait_ge(whi_ready, p - 7 + dyn)
                pool.tensor_tensor(lo[:, 0:n, :], raw[:, p % RAW, 0:n, :], hi[:, 0:n, :].bitcast(F32),
                                   ALU.subtract).then_inc(wlo_ready, 1)

            def stage(name, counts, iters):
                with pool.Fori(0, iters) as i:
                    for k, n in enumerate(counts):
                        lower(P0[name] + k, i * len(counts), n)

            sizes = [b - a for a, b in FF_PARTS]
            for l in (0, 1):
                stage(f"ffa{l}_in", [8] * 4, 11)
                stage(f"ffa{l}_out", sizes * 2, 4)
                mixer_lowers[l](pool, lower, stage)
                stage(f"ffb{l}_in", [8] * 4, 11)
                stage(f"ffb{l}_out", sizes * 2, 4)
                p0 = P0[f"ple{l}"]
                lower(p0, 0, 8)
                lower(p0 + 1, 0, 8)
                lower(p0 + 2, 0, 2, ple_split(l, 0, True))
                with pool.Fori(0, 3) as i:
                    for k in (0, 1):
                        lower(p0 + 3 + 2 * k, i * 4, 8, ple_split(l, 2 + k, False))
                        lower(p0 + 4 + 2 * k, i * 4, 2, ple_split(l, 1 + k, True))
                lower(p0 + 15, 0, 2, ple_split(l, 7, True))

        @block.scalar
        def _(act):
            act.dma_start(cf[:, 0:C_ROPE], I["cf"][:, 0:C_ROPE]).then_inc(id_ready, 16)
            for j in range(NTT):
                act.dma_start(xin[0:(P if j < 4 else TS), j, 0:512], xr[j][:, 0:512]).then_inc(in_ready[0], 16)
            act.dma_start(cf[:, C_ROPE:], I["cf"][:, C_ROPE:]).then_inc(consts_ready, 16)
            act.dma_start(cbf[:, :], I["cb"]).then_inc(consts_ready, 16)

            def upper(p, dyn, n, place=None, back=1):
                hi = place[0] if place else whi[:, p % SPLIT, :, :]
                act.wait_ge(raw_ready[p % RAW], UNIT * (p // RAW - 1) + dyn * (UNIT // RAW))
                act.wait_ge(panel_used, p - back + dyn)
                act.activation(hi[:, 0:n, :], raw[:, p % RAW, 0:n, :], ACT.Copy).then_inc(whi_ready, 1)

            def root(n, width, out=r):
                act.wait_ge(ss_ready, n + 1)
                act.activation(out[:, :], flat(4, T), ACT.Sqrt, bias=eps[:, 0:1], scale=1.0 / width).then_inc(sd_ready, 1)

            def ffn_in(name, norm):
                p0, t0 = P0[name], T0[name]

                def pair(k, dyn, first):
                    if not (first and p0 == 8):
                        upper(p0 + 2 * k + 1, dyn, 8)
                    if first:
                        root(norm, D)
                    upper(p0 + 2 * k + 2, dyn, 8)
                    act.wait_ge(tile_taken, t0 + 2 * k + 1 + dyn)
                    act.activation(sA[:, :], tA[:, :], ACT.Silu).then_inc(silu_done, 1)
                pair(0, 0, True)
                pair(1, 0, False)
                with act.Fori(1, NC_F // 2) as i:
                    for k in (0, 1):
                        pair(k, i * 4, False)

            def ffn_out(name):
                sizes = [b - a for a, b in FF_PARTS]
                nxt = (sizes * 2)[1:] + [8]
                with act.Fori(0, NC_D // 2) as i:
                    for k in range(8):
                        upper(P0[name] + 1 + k, i * 8, nxt[k])

            def square(name, n):
                with act.Fori(0, 2) as i:
                    for k in range(4):
                        upper(P0[name] + 1 + k, i * 4, n if k < 3 else 8)

            act.wait_ge(zeroed, 2)
            for c in range(NC_D):
                act.wait_ge(x_turned, c + 1)
                act.activation(x[:, c, :], flat(4 + 2 * (c % 2), T), ACT.Copy).then_inc(x_taken, 1)
                act.wait_ge(x_taken, c + 1)
                if c >= 2:
                    act.wait_ge(acc_done, c - 1)
                act.activation((tA, sA)[c % 2][:, :], x[:, c, :], ACT.Square).then_inc(x_sq, 1)
                if c in (1, 6):
                    upper(8 + c // 6, 0, 8)
            norm = 0
            for l in (0, 1):
                ffn_in(f"ffa{l}_in", norm); norm += 1
                ffn_out(f"ffa{l}_out")
                norm = mixer_acts[l](act, upper, root, square, norm)
                ffn_in(f"ffb{l}_in", norm); norm += 1
                ffn_out(f"ffb{l}_out")
                p0, t0 = P0[f"ple{l}"], T0[f"ple{l}"]
                act.wait_ge(panel_used, p0)
                pr = [I["p_prompt"][l, 0, j * P:(j + 1) * P, :] for j in range(4)] + \
                    [I["p_sample"][l].rearrange("b t d -> (b t) d")]
                for j in range(NTT):
                    act.dma_start(pn[0:(P if j < 4 else TS), j, :], pr[j]).then_inc(p_ready, 16)

                def sigmoid(c, t, dyn):
                    act.wait_ge(tile_taken, t + 1 + dyn)
                    gc = sg[:, bass.ds(c, 1), :]
                    act.activation(gc, gc, ACT.Sigmoid).then_inc(sg_ready, 1)
                upper(p0 + 1, 0, 8)
                root(norm, D); norm += 1
                sigmoid(0, t0, 0)
                upper(p0 + 2, 0, 2, ple_split(l, 0, True))
                upper(p0 + 3, 0, 8, ple_split(l, 2, False), back=2)
                sigmoid(1, t0 + 1, 0)

                def turn(k, dyn, c, last=False):
                    upper(p0 + 4 + 2 * k, dyn, 2, ple_split(l, 1 + k, True), back=3)
                    if last:
                        upper(p0 + 15, 0, 2, ple_split(l, 7, True), back=2)
                    else:
                        upper(p0 + 5 + 2 * k, dyn, 8, ple_split(l, 3 + k, False), back=3)
                    sigmoid(c, t0 + 5 + 2 * k, dyn)
                with act.Fori(0, 2) as i:
                    for k in (0, 1):
                        turn(k, i * 4, i * 2 + 2 + k)
                turn(4, 0, 6)
                turn(5, 0, 7, True)
                for c in range(NC_D if l == 0 else 0):
                    act.wait_ge(panel_used, p0 + 14)
                    act.wait_ge(acc_done, AC["ffa1"] + c + 1)
                    act.activation(xh[:, c, :], x[:, c, :], ACT.Copy,
                                   scale=gn[:, GCOL["ffa1"] + c:GCOL["ffa1"] + c + 1]).then_inc(xh_act, 1)
                    if c == 1:
                        upper(p0 + 16, 0, 8)
            act.wait_ge(ss_ready, norm + 1)
            act.activation(sd[:, 0:NTT], ps[:, 5, 100:100 + NTT], ACT.Sqrt, bias=eps[:, 0:1],
                           scale=1.0 / D).then_inc(sd_ready, 1)
            act.wait_ge(rc_ready, 1)
            for j in range(NTT):
                n = P if j < 4 else TS
                act.wait_ge(yt_ready, j + 1 if j < 4 else 9)
                act.activation(xin[0:n, j, 0:512], ps[0:n, 2 * j % 8, :], ACT.Copy, scale=rc[0:n, j:j + 1]).then_inc(y_act, 1)

        @block.vector
        def _(dve):
            v = {"chain": 0, "norm": 0, "dyn": 0}

            def link(ins):
                v["chain"] += 1
                ins.then_inc(chain, 1)
                dve.wait_ge(chain, v["chain"] + v["dyn"])

            def rms(out=r):
                v["norm"] += 1
                dve.wait_ge(sd_ready, v["norm"])
                link(dve.reciprocal(out[:, :], out[:, :]))

            def square_sum(xf, name, k, dyn, cl, cdyn):
                dve.tensor_tensor(sq[:, :], xf, xf, ALU.mult).then_inc(chain, 1)
                dve.wait_ge(chain, cl + 1 + cdyn)
                dve.wait_ge(acc_done, AC[name] + k + dyn)
                dve.tensor_tensor(acc[:, 0:T], acc[:, 0:T], sq[:, :], ALU.add).then_inc(acc_done, 1)

            def lower_split(xf, c, name):
                hc = xh[:, bass.ds(c, 1), :].rearrange("p a t -> p (a t)")
                lc = xl[:, bass.ds(c, 1), :].rearrange("p a t -> p (a t)")
                dve.scalar_tensor_tensor(out=lc, in0=xf, scalar=gn[:, bass.ds(c + GCOL[name], 1)], in1=hc.bitcast(F32),
                                         op0=ALU.mult, op1=ALU.subtract).then_inc(xg_ready, 1)

            def after_x(xf, c, name, dyn, k, cdyn, cl):
                hc = xh[:, bass.ds(c, 1), :].rearrange("p a t -> p (a t)")
                dve.tensor_scalar(hc, xf, gn[:, bass.ds(c + GCOL[name], 1)], None, ALU.mult).then_inc(chain, 1)
                dve.wait_ge(chain, cl + 1 + cdyn)
                lower_split(xf, c, name)
                square_sum(xf, name, k, dyn, cl + 1, cdyn)

            def clear_acc():
                link(dve.memset(acc[:, 0:T], 0.0))

            def chunks(t0, name, tiles_ready, update):
                clear_acc()
                links = 2
                c0 = v["chain"]
                with dve.Fori(0, NC_D // 2) as i:
                    for k in (0, 1):
                        c = i * 2 + k
                        tiles_ready(i, k)
                        xf = x[:, bass.ds(c, 1), :].rearrange("p a t -> p (a t)")
                        update(xf, t0 + k)
                        dve.wait_ge(tile_taken, t0 + k + 1 + i * 2)
                        after_x(xf, c, name, i * 2, k, i * (2 * links), c0 + k * links)
                v["chain"] += 8 * links

            def ffn_in(name, ubase):
                p0, t0 = P0[name], T0[name]
                c0 = v["chain"]
                with dve.Fori(0, NC_F // 2) as i:
                    for k in (0, 1):
                        pa, ta, j, cl = p0 + 2 * k, t0 + 2 * k, i * 2 + k, c0 + 2 * k
                        dve.wait_ge(panel_used, pa + 1 + i * 4)
                        dve.tensor_tensor(half(tA[:, :]), slot(ta), half(r[:, :]), ALU.mult).then_inc(tile_taken, 1)
                        dve.wait_ge(silu_done, ubase + k + 1 + i * 2)
                        dve.tensor_tensor(sA[:, :], sA[:, :], r[:, :], ALU.mult).then_inc(chain, 1)
                        dve.wait_ge(panel_used, pa + 2 + i * 4)
                        dve.wait_ge(chain, cl + 1 + i * 4)
                        dve.tensor_tensor(half(ub[:, :]), slot(ta + 1), half(sA[:, :]), ALU.mult).then_inc(tile_taken, 1)
                        dve.wait_ge(tile_taken, ta + 2 + i * 4)
                        hj = uh[:, bass.ds(j, 1), :].rearrange("p a t -> p (a t)")
                        lj = ul[:, bass.ds(j, 1), :].rearrange("p a t -> p (a t)")
                        dve.tensor_copy(hj, ub[:, :]).then_inc(chain, 1)
                        dve.wait_ge(chain, cl + 2 + i * 4)
                        dve.tensor_tensor(lj, ub[:, :], hj.bitcast(F32), ALU.subtract).then_inc(u_ready, 1)
                v["chain"] += NC_F * 2

            def ffn_out(name, nxt):
                def ready(i, k):
                    dve.wait_ge(panel_used, P0[name] + 4 * (k + 1) + i * 8)

                def update(xf, t):
                    dve.scalar_tensor_tensor(out=half(xf), in0=slot(t), scalar=0.5, in1=half(xf),
                                             op0=ALU.mult, op1=ALU.add).then_inc(tile_taken, 1)
                chunks(T0[name], nxt, ready, update)

            def added(name, nxt):
                def ready(i, k):
                    dve.wait_ge(panel_used, P0[name] + k + 1 + i * 2)

                def update(xf, t):
                    dve.tensor_tensor(half(xf), slot(t), half(xf), ALU.add).then_inc(tile_taken, 1)
                chunks(T0[name], nxt, ready, update)

            def ple(l, nxt):
                p0, t0 = P0[f"ple{l}"], T0[f"ple{l}"]
                links = 2
                clear_acc()

                def gate(c, p, t, dyn):
                    dve.wait_ge(panel_used, p + 1 + dyn)
                    gc = sg[:, bass.ds(c, 1), :].rearrange("p a t -> p (a t)")
                    dve.tensor_tensor(half(gc), slot(t), half(r[:, :]), ALU.mult).then_inc(tile_taken, 1)

                def proj(c, k, kdyn, p, t, dyn, cl, cdyn):
                    dve.wait_ge(panel_used, p + 1 + dyn)
                    dve.wait_ge(sg_ready, 8 * l + k + 1 + kdyn)
                    gc = sg[:, bass.ds(c, 1), :].rearrange("p a t -> p (a t)")
                    xf = x[:, bass.ds(c, 1), :].rearrange("p a t -> p (a t)")
                    dve.tensor_tensor(half(ub[:, :]), slot(t), half(gc), ALU.mult).then_inc(chain, 1)
                    dve.wait_ge(chain, cl + 1 + cdyn)
                    dve.tensor_tensor(xf, ub[:, :], xf, ALU.add).then_inc(tile_taken, 1)
                    dve.wait_ge(tile_taken, t + 1 + dyn)
                    if l == 1:
                        yc = yT[:, bass.ds(c, 1), :].rearrange("p a t -> p (a t)")
                        dve.tensor_scalar(yc, xf, gn[:, bass.ds(c + GCOL[nxt], 1)], None, ALU.mult).then_inc(y_ready, 1)
                    square_sum(xf, nxt, k, kdyn, cl + 1, cdyn)

                def lowers(chunks_):
                    for c in chunks_ if l == 0 else ():
                        dve.wait_ge(xh_act, c + 1)
                        lower_split(x[:, c, :], c, nxt)
                gate(0, p0, t0, 0)
                gate(1, p0 + 1, t0 + 1, 0)
                for c in (0, 1):
                    dve.wait_ge(pt_ready, 2 * l + c + 1)
                    b = 2 * ((t0 + 2 + c) % 2)
                    link(dve.tensor_copy(pth[:, c, :], flat(b, T)))
                    dve.tensor_tensor(ptl[:, c, :], flat(b, T), pth[:, c, :].bitcast(F32),
                                      ALU.subtract).then_inc(tile_taken, 1)
                c0 = v["chain"]
                proj(0, 0, 0, p0 + 2, t0 + 4, 0, c0, 0)
                with dve.Fori(0, 3) as i:
                    for k in (0, 1):
                        gate(i * 2 + 2 + k, p0 + 3 + 2 * k, t0 + 5 + 2 * k, i * 4)
                        proj(i * 2 + 1 + k, 1 + k, i * 2, p0 + 4 + 2 * k, t0 + 6 + 2 * k, i * 4,
                             c0 + (1 + k) * links, i * (2 * links))
                lowers(range(0, 3))
                proj(7, 7, 0, p0 + 15, t0 + 17, 0, c0 + 7 * links, 0)
                lowers(range(3, NC_D))
                v["chain"] += 8 * links

            dve.memset(eps[:, :], EPS).then_inc(zeroed, 1)
            dve.memset(acc[:, :], 0.0).then_inc(zeroed, 1)
            dve.wait_ge(zeroed, 2)
            dve.wait_ge(gn_ready, 16)
            for c in range(NC_D):
                dve.wait_ge(x_taken, c + 1)
                g = gn[:, c:c + 1]
                dve.tensor_scalar(xh[:, c, :], x[:, c, :], g, None, ALU.mult).then_inc(tile_taken, 1)
                dve.wait_ge(tile_taken, c + 1)
                dve.scalar_tensor_tensor(out=xl[:, c, :], in0=x[:, c, :], scalar=g, in1=xh[:, c, :].bitcast(F32),
                                         op0=ALU.mult, op1=ALU.subtract).then_inc(xg_ready, 1)
                dve.wait_ge(x_sq, c + 1)
                if c:
                    dve.wait_ge(acc_done, c)
                dve.tensor_tensor(acc[:, 0:T], acc[:, 0:T], (tA, sA)[c % 2][:, :], ALU.add).then_inc(acc_done, 1)
            dve.wait_ge(consts_ready, 32)
            link(dve.tensor_copy(cb[:, :], cbf[:, :]))
            for l in (0, 1):
                rms()
                ffn_in(f"ffa{l}_in", 44 * l)
                ffn_out(f"ffa{l}_out", f"mix{l}")
                mixer_dves[l](dve, v, link, rms, added)
                rms()
                ffn_in(f"ffb{l}_in", 44 * l + 22)
                ffn_out(f"ffb{l}_out", f"ple{l}")
                rms()
                ple(l, "ffa1" if l == 0 else "final")
            dve.wait_ge(sd_ready, v["norm"] + 1)
            dve.reciprocal(rc[:, 0:NTT], sd[:, 0:NTT]).then_inc(rc_ready, 1)
            dve.wait_ge(rc_ready, 1)
            for j in range(NTT):
                n = P if j < 4 else TS
                dve.wait_ge(yt_ready, j + 5 if j < 4 else 10)
                dve.tensor_scalar(xin[0:n, j, 512:1024], ps[0:n, (2 * j + 1) % 8, :], rc[0:n, j:j + 1], None,
                                  ALU.mult).then_inc(y_dve, 1)

        @block.tensor
        def _(pe):
            mm = nc.tensor.matmul
            v = {"norm": 0, "acc": 0}

            def products(p, dyn, n_chunks, mh, ml, out, first=True, last=True, waits=None, at=None, place=None):
                hi, lo = place or (whi[:, p % SPLIT, :, :], wlo[:, p % SPLIT, :, :])
                pe.wait_ge(whi_ready, p - 7 + dyn)
                pe.wait_ge(wlo_ready, p - 7 + dyn)
                for n in range(n_chunks):
                    if at and n in at:
                        at[n]()
                    if waits:
                        waits(n)
                    h0, l0 = half(mh(n)), half(ml(n))
                    for q in (0, 1):
                        mm(out[:, q, :], hi[:, n, :], h0[:, q, :], start=first and n == 0, stop=False)
                    for q in (0, 1):
                        mm(out[:, q, :], hi[:, n, :], l0[:, q, :], start=False, stop=False)
                    end = last and n == n_chunks - 1
                    for q in (0, 1):
                        ins = mm(out[:, q, :], lo[:, n, :], h0[:, q, :], start=False, stop=end)
                ins.then_inc(panel_used, 1)

            def sums(n_acc):
                v["norm"] += 1
                v["acc"] += n_acc
                pe.wait_ge(acc_done, v["acc"])
                every = ones[:, 0:1].to_broadcast([P, P])
                mm(ps[:, 4, :], every, acc[:, 0:512], start=True, stop=True)
                mm(ps[:, 5, 0:T - 512], every, acc[:, 512:T], start=True, stop=True).then_inc(ss_ready, 1)

            def sums_by_tokens():
                v["norm"] += 1
                pe.wait_ge(acc_done, v["acc"] + 8)
                for j in range(NTT):
                    ins = mm(ps[:, 5, 100 + j:101 + j], acc[:, j * P:(j + 1) * P], ones[:, 0:1], start=True, stop=True)
                ins.then_inc(ss_ready, 1)

            def tiles(name, n_chunks, per_tile, mh, ml, iters, per, xg0=None, waits0=None):
                def tile(k, dyn, waits=None):
                    if waits is not turned:
                        pe.wait_ge(tile_taken, T0[name] + k - 1 + dyn)
                    products(P0[name] + k, dyn, n_chunks, mh, ml, slot(T0[name] + k), waits=waits)
                if xg0 is not None:
                    tile(0, 0, turned if xg0 == 0 else lambda n: pe.wait_ge(xg_ready, xg0 + n + 1))
                    sums(8)
                    tile(1, 0)
                    for k in range(2, per):
                        tile(k, 0)
                elif waits0:
                    tile(0, 0, waits0)
                    for k in range(1, per):
                        tile(k, 0)
                with pe.Fori(0 if xg0 is None and not waits0 else 1, iters) as i:
                    for k in range(per):
                        tile(k, i * per)

            def ffn_out(name, ubase):
                with pe.Fori(0, NC_D // 2) as i:
                    for k in (0, 1):
                        pe.wait_ge(tile_taken, T0[name] + k - 1 + i * 2)
                        for q, (a, b) in enumerate(FF_PARTS):
                            products(P0[name] + 4 * k + q, i * 8, b - a, lambda n: uh[:, a + n, :],
                                     lambda n: ul[:, a + n, :], slot(T0[name] + k), q == 0, q == 3,
                                     (lambda n: pe.wait_ge(u_ready, ubase + a + n + 1)) if k == 0 else None)

            xgh, xgl = (lambda n: xh[:, n, :]), (lambda n: xl[:, n, :])
            pe.wait_ge(id_ready, 16)

            def turn(c):
                pe.wait_ge(in_ready[c // 4], 16 * NTT)
                if c >= 2:
                    pe.wait_ge(x_taken, c - 1)
                for j in range(NTT):
                    n = P if j < 4 else TS
                    ins = nc.tensor.transpose(flat(4 + 2 * (c % 2), T)[:, j * P:j * P + n],
                                              xin[0:n, j, c * P:(c + 1) * P], ident[0:n, 0:n])
                    if c == 0 and j == 0:
                        ins.then_inc(panel_used, NC_D)
                ins.then_inc(x_turned, 1)

            def turned(n):
                if n + 4 < NC_D:
                    turn(n + 4)
                pe.wait_ge(xg_ready, n + 1)
            for c in range(4):
                turn(c)
            for l in (0, 1):
                tiles(f"ffa{l}_in", 8, 1, xgh, xgl, 11, 4, XG[f"ffa{l}"])
                ffn_out(f"ffa{l}_out", 44 * l)
                mixer_pes[l](pe, v, products, sums, tiles, xgh, xgl)
                tiles(f"ffb{l}_in", 8, 1, xgh, xgl, 11, 4, XG[f"ffb{l}"])
                ffn_out(f"ffb{l}_out", 44 * l + 22)
                p0, t0 = P0[f"ple{l}"], T0[f"ple{l}"]

                def gate(c, p, t, dyn, waits=None):
                    pe.wait_ge(tile_taken, t - 1 + dyn)
                    products(p, dyn, 8, xgh, xgl, slot(t), waits=waits, place=ple_split(l, c, False))

                def proj(c, p, t, dyn):
                    pe.wait_ge(tile_taken, t - 1 + dyn)
                    products(p, dyn, 2, lambda n: pth[:, n, :], lambda n: ptl[:, n, :], slot(t),
                             place=ple_split(l, c, True))
                gate(0, p0, t0, 0, waits=lambda n: pe.wait_ge(xg_ready, XG[f"ple{l}"] + n + 1))
                sums(8)
                gate(1, p0 + 1, t0 + 1, 0)
                pe.wait_ge(p_ready, 16 * NTT * (l + 1))
                for c in (0, 1):
                    t = t0 + 2 + c
                    pe.wait_ge(tile_taken, t - 1)
                    for j in range(NTT):
                        n = P if j < 4 else TS
                        ins = nc.tensor.transpose(flat(2 * (t % 2), T)[:, j * P:j * P + n],
                                                  pn[0:n, j, c * P:(c + 1) * P], ident[0:n, 0:n])
                    ins.then_inc(pt_ready, 1)
                pe.wait_ge(tile_taken, t0 + 4)
                proj(0, p0 + 2, t0 + 4, 0)
                with pe.Fori(0, 3) as i:
                    for k in (0, 1):
                        gate(2 + k, p0 + 3 + 2 * k, t0 + 5 + 2 * k, i * 4)
                        proj(1 + k, p0 + 4 + 2 * k, t0 + 6 + 2 * k, i * 4)
                proj(7, p0 + 15, t0 + 17, 0)
            pe.wait_ge(tile_taken, T0["ple1"] + 18)
            for q, j in [(0, j) for j in range(4)] + [(1, j) for j in range(4)] + [(0, 4), (1, 4)]:
                n, b = P if j < 4 else TS, (2 * j + q) % 8
                if j == 0:
                    pe.wait_ge(y_ready, 4 * q + 4)
                    if q:
                        sums_by_tokens()
                if b == 5:
                    pe.wait_ge(sd_ready, v["norm"])
                if j == 4:
                    pe.wait_ge((y_act, y_dve)[q], 1)
                for c in range(4):
                    ins = nc.tensor.transpose(ps[0:n, b, c * P:(c + 1) * P], yT[:, 4 * q + c, j * P:j * P + n], ident)
                ins.then_inc(yt_ready, 1)


_INS = ['x_prompt', 'x_sample', 'cache_ckv', 'cache_krope', 'state_C', 'state_n', 'state_m', 'page_table',
        'p_prompt', 'p_sample', 'w_ffa_in', 'w_ffa_out', 'w_ffb_in', 'w_ffb_out', 'w_ple_gate', 'w_ple_proj',
        'w_mla_in', 'w_uq', 'w_uk', 'w_uv', 'w_mla_out', 'w_mlstm_in', 'b_igate', 'b_fgate', 'w_mlstm_out']
_OUTS = [("y_prompt", (1, 512, 1024)), ("y_sample", (8, 8, 1024)), ("ckv_prompt", (1, 1, 512, 256)),
         ("kr_prompt", (1, 1, 512, 32)), ("ckv_sample", (1, 8, 8, 256)), ("kr_sample", (1, 8, 8, 32)),
         ("C_prompt", (1, 1, 4, 128, 256)), ("n_prompt", (1, 1, 4, 128)), ("m_prompt", (1, 1, 4)),
         ("C_sample", (1, 8, 4, 128, 256)), ("n_sample", (1, 8, 4, 128)), ("m_sample", (1, 8, 4))]
_PAST = 2048


def constants():
    cf = np.zeros((P, NCF), np.float32)
    cf[:, C_ID:C_ID + P] = np.eye(P)
    cf[:, C_ONE:C_ONE + 8] = 1.0
    half = ROPE // 2
    inv = (np.float32(10000.0) ** (-np.arange(half, dtype=np.float32) / np.float32(half))).astype(np.float32)
    pos = np.concatenate([np.arange(TP), np.tile(_PAST + np.arange(TB), NB)]).astype(np.float32)
    ang = inv[:, None] * pos[None, :]
    cos, sin = np.cos(ang.astype(np.float64)), np.sin(ang.astype(np.float64))
    cf[64:80, C_ROPE:C_ROPE + T] = cos
    cf[80:96, C_ROPE:C_ROPE + T] = cos
    cf[96:112, C_ROPE:C_ROPE + T] = -sin
    cf[112:128, C_ROPE:C_ROPE + T] = sin
    s = np.arange(TS)
    cf[0:TS, C_BLK:C_BLK + NB] = (s[:, None] // TB == np.arange(NB)[None, :])
    for h in range(LH):
        cf[h, C_SEL + h * P:C_SEL + (h + 1) * P] = 1.0
    k = np.arange(P)
    cf[:, C_TRI:C_TRI + P] = np.where(k[:, None] <= k[None, :], 0.0, -NEG)
    ok = (s[:, None] // TB == s[None, :] // TB) & (s[:, None] <= s[None, :])
    cf[0:TS, C_STRI:C_STRI + TS] = np.where(ok, 0.0, -NEG)
    cb = np.zeros((P, NCB), np.float32)
    cb[:, B_ID:B_ID + P] = np.eye(P)
    cb[:, B_CAUSAL:B_CAUSAL + P] = np.where(k[None, :] <= k[:, None], 0.0, NEG)
    t = np.arange(P) // NH
    for b in range(NB):
        ok = (s[None, :] // TB == b) & (s[None, :] % TB <= t[:, None])
        cb[:, B_SAMPLE + b * TS:B_SAMPLE + (b + 1) * TS] = np.where(ok, 0.0, NEG)
    return cf, cb


def layout(inputs):
    a = {n: np.ascontiguousarray(inputs[n]) for n in _INS}
    g = np.asarray
    rows = [g(inputs["g_ffa"])[0], g(inputs["g_mix"])[0], g(inputs["g_ffb"])[0], g(inputs["g_ple"])[0],
            g(inputs["g_ffa"])[1], g(inputs["g_mix"])[1], g(inputs["g_ffb"])[1], g(inputs["g_ple"])[1],
            g(inputs["g_final"]), g(inputs["g_mlstm_head"])[0], g(inputs["g_q_lat"])[0], g(inputs["g_kv_lat"])[0]]
    a["gains"] = np.ascontiguousarray(np.concatenate([r.reshape(-1, P) for r in rows]).T)
    a["cf"], a["cb"] = constants()
    return a


def kernel(**inputs):
    import concourse.bacc as _bacc
    from concourse.bass_utils import run_bass_kernel_spmd as _run

    nc = _bacc.Bacc("TRN2", target_bir_lowering=False, num_devices=1)
    arrays, ins, outs = {}, {}, {}
    for name, a in layout(inputs).items():
        arrays[f"in_{name}"] = a
        ins[name] = nc.dram_tensor(f"in_{name}", a.shape, mybir.dt.from_np(a.dtype), kind="ExternalInput").ap()
    for name, shape in _OUTS:
        outs[name] = nc.dram_tensor(f"out_{name}", shape, F32, kind="ExternalOutput").ap()
    hybrid_step(nc, ins, outs)
    got = _run(nc, [arrays], core_ids=[0]).results[0]
    return tuple(got[f"out_{n}"] for n, _ in _OUTS)
```
